# Optimizing a Trainium2 kernel written in Bass

```python
import math
import jax, jax.numpy as jnp
from jax import lax
import numpy as np

D_MODEL = 1024
BATCH = 1
SEQ = 1024
DEPTH = 1

CHUNK = 64
N_MEM = 256
EPS = 1e-6

DSA_HEADS = 16
DSA_HEAD_DIM = 64
DSA_KV_RANK = 256
IDX_HEADS = 8
IDX_HEAD_DIM = 64
TOPK_MAX = 256
Q_BLOCK = 128

SWA_HEADS = 16
SWA_KV_HEADS = 2
SWA_HEAD_DIM = 64
SWA_WINDOW = 128
SWA_CHUNKS = SWA_WINDOW // CHUNK

SSM_D_INNER = 1024
SSM_HEAD_DIM = 64
SSM_HEADS = SSM_D_INNER // SSM_HEAD_DIM
SSM_GROUPS = 2
SSM_STATE = 128
SSM_CONV = 4
SSM_CONV_DIM = SSM_D_INNER + 2 * SSM_GROUPS * SSM_STATE

XA_HEADS = 4
XA_HEAD_DIM = D_MODEL // XA_HEADS

D_FF = ((-(-8 * D_MODEL // 3) + 255) // 256) * 256

N_BRANCH = 3
IN_SPLITS = (
    DSA_HEADS * DSA_HEAD_DIM,
    DSA_KV_RANK,
    IDX_HEADS * IDX_HEAD_DIM,
    IDX_HEAD_DIM,
    IDX_HEADS,
    SWA_HEADS * SWA_HEAD_DIM,
    SWA_KV_HEADS * SWA_HEAD_DIM,
    SWA_KV_HEADS * SWA_HEAD_DIM,
    SSM_D_INNER,
    SSM_CONV_DIM,
    SSM_HEADS,
    N_BRANCH * D_MODEL,
)
N_IN = sum(IN_SPLITS)

kernel_name = 'hybrid_dsa_swa_ssd_stream_block'

def _rms(x, w):
    xf = x.astype(jnp.float32)
    y = xf * lax.rsqrt(jnp.mean(xf * xf, axis=-1, keepdims=True) + EPS)
    return (y * w.astype(jnp.float32)).astype(x.dtype)

def _layer_norm(x, w, b):
    xf = x.astype(jnp.float32)
    mu = jnp.mean(xf, axis=-1, keepdims=True)
    var = jnp.mean(jnp.square(xf - mu), axis=-1, keepdims=True)
    y = (xf - mu) * lax.rsqrt(var + EPS)
    return (y * w.astype(jnp.float32) + b.astype(jnp.float32)).astype(x.dtype)

def _split_cols(a, sizes):
    out, o = [], 0
    for sz in sizes:
        out.append(a[..., o:o + sz])
        o += sz
    return out

def dsa_mixer(q, c_kv, iq, ik, iw, kv_norm, w_ukv, q_norm, k_norm, ik_w, ik_b):
    b, s = q.shape[:2]
    q = _rms(q.reshape(b, s, DSA_HEADS, DSA_HEAD_DIM), q_norm)
    kv = _rms(c_kv, kv_norm) @ w_ukv
    k = _rms(kv[..., :DSA_HEAD_DIM], k_norm)
    v = kv[..., DSA_HEAD_DIM:]
    iq = iq.reshape(b, s, IDX_HEADS, IDX_HEAD_DIM)
    ik = _layer_norm(ik, ik_w, ik_b)
    iw = iw.astype(jnp.float32) * (IDX_HEADS ** -0.5 * IDX_HEAD_DIM ** -0.5)
    top_k = min(TOPK_MAX, s // 4)
    n_blk = s // Q_BLOCK
    key_chunk = jnp.arange(s) // CHUNK

    def to_blocks(a):
        return jnp.moveaxis(a.reshape((b, n_blk, Q_BLOCK) + a.shape[2:]), 1, 0)

    def block(args):
        qb, iqb, iwb, q_chunk = args
        rel = jax.nn.relu(jnp.einsum('bqhd,bsd->bqhs', iqb, ik).astype(jnp.float32))
        score = jnp.einsum('bqhs,bqh->bqs', rel, iwb)
        admissible = key_chunk[None, :] <= q_chunk[:, None]
        score = jnp.where(admissible[None], score, -jnp.inf)
        _, idx = lax.top_k(score, top_k)
        valid = key_chunk[idx] <= q_chunk[None, :, None]
        kg = jax.vmap(lambda kk, ii: kk[ii])(k, idx)
        vg = jax.vmap(lambda vv, ii: vv[ii])(v, idx)
        logits = jnp.einsum('bqhd,bqkd->bqhk', qb, kg).astype(jnp.float32) * DSA_HEAD_DIM ** -0.5
        logits = jnp.where(valid[:, :, None, :], logits, -jnp.inf)
        p = jax.nn.softmax(logits, axis=-1).astype(vg.dtype)
        return jnp.einsum('bqhk,bqkd->bqhd', p, vg)

    q_chunks = (jnp.arange(s) // CHUNK).reshape(n_blk, Q_BLOCK)
    out = lax.map(block, (to_blocks(q), to_blocks(iq), to_blocks(iw), q_chunks))
    return jnp.moveaxis(out, 0, 1).reshape(b, s, DSA_HEADS * DSA_HEAD_DIM)

def swa_mixer(q, k, v, q_norm, k_norm, sinks):
    b, s = q.shape[:2]
    n_c = s // CHUNK
    grp = SWA_HEADS // SWA_KV_HEADS
    q = _rms(q.reshape(b, n_c, CHUNK, SWA_KV_HEADS, grp, SWA_HEAD_DIM), q_norm)
    k = _rms(k.reshape(b, n_c, CHUNK, SWA_KV_HEADS, SWA_HEAD_DIM), k_norm)
    v = v.reshape(b, n_c, CHUNK, SWA_KV_HEADS, SWA_HEAD_DIM)

    def band(a):
        parts = [jnp.pad(a, ((0, 0), (j, 0), (0, 0), (0, 0), (0, 0)))[:, :n_c]
                 for j in range(SWA_CHUNKS - 1, -1, -1)]
        return jnp.concatenate(parts, axis=2)

    kw, vw = band(k), band(v)
    lag = jnp.repeat(jnp.arange(SWA_CHUNKS - 1, -1, -1), CHUNK)
    valid = jnp.arange(n_c)[:, None] >= lag[None, :]
    logits = jnp.einsum('bclkgd,bcwkd->bckglw', q, kw).astype(jnp.float32) * SWA_HEAD_DIM ** -0.5
    logits = jnp.where(valid[None, :, None, None, None, :], logits, -jnp.inf)
    sink = jnp.broadcast_to(sinks.astype(jnp.float32).reshape(1, 1, SWA_KV_HEADS, grp, 1, 1),
                            logits.shape[:-1] + (1,))
    p = jax.nn.softmax(jnp.concatenate([logits, sink], axis=-1), axis=-1)[..., :-1].astype(vw.dtype)
    out = jnp.einsum('bckglw,bcwkd->bclkgd', p, vw)
    return out.reshape(b, s, SWA_HEADS * SWA_HEAD_DIM)

def _causal_dwconv(u, w, bias):
    c = u.shape[-1]
    y = lax.conv_general_dilated(u, w[:, None, :].astype(u.dtype), window_strides=(1,),
                                 padding=[(SSM_CONV - 1, 0)],
                                 dimension_numbers=('NWC', 'WIO', 'NWC'),
                                 feature_group_count=c)
    return y + bias.astype(u.dtype)

def _ssd(x, a_dt, bm, cm):
    b, s, h, p = x.shape
    n_c = s // CHUNK
    r = h // SSM_GROUPS
    x = x.reshape(b, n_c, CHUNK, SSM_GROUPS, r, p)
    bm = bm.reshape(b, n_c, CHUNK, SSM_GROUPS, SSM_STATE)
    cm = cm.reshape(b, n_c, CHUNK, SSM_GROUPS, SSM_STATE)
    a = a_dt.reshape(b, n_c, CHUNK, SSM_GROUPS, r).transpose(0, 3, 4, 1, 2)
    a_cum = jnp.cumsum(a, axis=-1)
    tril = jnp.tril(jnp.ones((CHUNK, CHUNK), dtype=bool))
    decay_in = jnp.exp(jnp.where(tril, a_cum[..., :, None] - a_cum[..., None, :], -jnp.inf))
    cb = jnp.einsum('bclgn,bcsgn->bgcls', cm, bm)
    y_diag = jnp.einsum('bgrcls,bcsgrp->bclgrp', cb[:, :, None] * decay_in, x)

    def to_clgr(t):
        return t.transpose(0, 3, 4, 1, 2)

    decay_to_end = to_clgr(jnp.exp(a_cum[..., -1:] - a_cum))
    chunk_states = jnp.einsum('bclgn,bclgrp->bcgrpn', bm, x * decay_to_end[..., None])
    chunk_decay = jnp.exp(a_cum[..., -1])

    def step(state, inp):
        st, dec = inp
        return state * dec[..., None, None] + st, state

    init = jnp.zeros(chunk_states.shape[:1] + chunk_states.shape[2:], x.dtype)
    _, prev = lax.scan(step, init, (jnp.moveaxis(chunk_states, 1, 0), jnp.moveaxis(chunk_decay, -1, 0)))
    y_off = jnp.einsum('bclgn,cbgrpn->bclgrp', cm, prev) * to_clgr(jnp.exp(a_cum))[..., None]
    return (y_diag + y_off).reshape(b, s, h, p)

def mamba2_mixer(z, xbc, dt, conv_w, conv_b, dt_bias, a_log, d_skip, norm_w):
    b, s = z.shape[:2]
    f32 = jnp.float32
    xbc = jax.nn.silu(_causal_dwconv(xbc, conv_w, conv_b))
    gn = SSM_GROUPS * SSM_STATE
    xs = xbc[..., :SSM_D_INNER].reshape(b, s, SSM_HEADS, SSM_HEAD_DIM).astype(f32)
    bm = xbc[..., SSM_D_INNER:SSM_D_INNER + gn].reshape(b, s, SSM_GROUPS, SSM_STATE).astype(f32)
    cm = xbc[..., SSM_D_INNER + gn:].reshape(b, s, SSM_GROUPS, SSM_STATE).astype(f32)
    dt = jax.nn.softplus(dt.astype(f32) + dt_bias.astype(f32))
    a = -jnp.exp(a_log.astype(f32))
    y = _ssd(xs * dt[..., None], dt * a, bm, cm) + xs * d_skip.astype(f32)[:, None]
    y = y.reshape(b, s, SSM_D_INNER) * jax.nn.silu(z.astype(f32))
    y = _rms(y.reshape(b, s, SSM_GROUPS, SSM_D_INNER // SSM_GROUPS),
             norm_w.reshape(SSM_GROUPS, SSM_D_INNER // SSM_GROUPS))
    return y.reshape(b, s, SSM_D_INNER).astype(z.dtype)

def memory_cross_attention(u, m, wq, wkv, q_norm, k_norm, wo):
    b, s = u.shape[:2]
    q = _rms((u @ wq).reshape(b, s, XA_HEADS, XA_HEAD_DIM), q_norm)
    kv = (m @ wkv).reshape(b, m.shape[1], 2, XA_HEADS, XA_HEAD_DIM)
    k = _rms(kv[:, :, 0], k_norm)
    v = kv[:, :, 1]
    logits = jnp.einsum('bshd,bmhd->bhsm', q, k).astype(jnp.float32) * XA_HEAD_DIM ** -0.5
    p = jax.nn.softmax(logits, axis=-1).astype(v.dtype)
    o = jnp.einsum('bhsm,bmhd->bshd', p, v).reshape(b, s, XA_HEADS * XA_HEAD_DIM)
    return o @ wo

def swiglu_ffn(u, w_gate_up, w_down):
    gu = u @ w_gate_up
    return (jax.nn.silu(gu[..., :D_FF]) * gu[..., D_FF:]) @ w_down

def setup_inputs(seed: int = 0) -> dict:
    key = jax.random.key(seed)
    ks = iter(jax.random.split(key, 64))
    L = DEPTH

    def nrm(shape, scale):
        return jax.random.normal(next(ks), shape, jnp.float32) * scale

    def gain(shape):
        return 1.0 + nrm(shape, 0.01)

    x = nrm((BATCH, SEQ, D_MODEL), 1.0)
    mem = nrm((BATCH, N_MEM, D_MODEL), 1.0)
    norm_mix = gain((L, D_MODEL))
    w_in = nrm((L, D_MODEL, N_IN), D_MODEL ** -0.5)
    dsa_kv_norm = gain((L, DSA_KV_RANK))
    dsa_w_ukv = nrm((L, DSA_KV_RANK, 2 * DSA_HEAD_DIM), DSA_KV_RANK ** -0.5)
    dsa_q_norm = gain((L, DSA_HEAD_DIM))
    dsa_k_norm = gain((L, DSA_HEAD_DIM))
    idx_k_ln_w = gain((L, IDX_HEAD_DIM))
    idx_k_ln_b = nrm((L, IDX_HEAD_DIM), 0.01)
    swa_q_norm = gain((L, SWA_HEAD_DIM))
    swa_k_norm = gain((L, SWA_HEAD_DIM))
    swa_sinks = nrm((L, SWA_HEADS), 0.5)
    ssm_conv_w = nrm((L, SSM_CONV, SSM_CONV_DIM), SSM_CONV ** -0.5)
    ssm_conv_b = nrm((L, SSM_CONV_DIM), 0.01)
    dt0 = jnp.exp(jax.random.uniform(next(ks), (L, SSM_HEADS), jnp.float32,
                                     minval=math.log(1e-3), maxval=math.log(1e-1)))
    ssm_dt_bias = dt0 + jnp.log(-jnp.expm1(-dt0))
    ssm_a_log = jnp.log(jax.random.uniform(next(ks), (L, SSM_HEADS), jnp.float32, minval=1.0, maxval=16.0))
    ssm_d = gain((L, SSM_HEADS))
    ssm_norm = gain((L, SSM_D_INNER))
    w_br_dsa = nrm((L, DSA_HEADS * DSA_HEAD_DIM, D_MODEL), (DSA_HEADS * DSA_HEAD_DIM) ** -0.5)
    w_br_swa = nrm((L, SWA_HEADS * SWA_HEAD_DIM, D_MODEL), (SWA_HEADS * SWA_HEAD_DIM) ** -0.5)
    w_br_ssm = nrm((L, SSM_D_INNER, D_MODEL), SSM_D_INNER ** -0.5)
    w_out = nrm((L, D_MODEL, D_MODEL), D_MODEL ** -0.5)
    norm_xa = gain((L, D_MODEL))
    norm_mem = gain((L, D_MODEL))
    xa_wq = nrm((L, D_MODEL, XA_HEADS * XA_HEAD_DIM), D_MODEL ** -0.5)
    xa_wkv = nrm((L, D_MODEL, 2 * XA_HEADS * XA_HEAD_DIM), D_MODEL ** -0.5)
    xa_q_norm = gain((L, XA_HEAD_DIM))
    xa_k_norm = gain((L, XA_HEAD_DIM))
    xa_wo = nrm((L, XA_HEADS * XA_HEAD_DIM, D_MODEL), (XA_HEADS * XA_HEAD_DIM) ** -0.5)
    norm_ffn = gain((L, D_MODEL))
    ffn_w_gate_up = nrm((L, D_MODEL, 2 * D_FF), D_MODEL ** -0.5)
    ffn_w_down = nrm((L, D_FF, D_MODEL), D_FF ** -0.5)
    return {
        'x': x, 'mem': mem,
        'norm_mix': norm_mix, 'w_in': w_in,
        'dsa_kv_norm': dsa_kv_norm, 'dsa_w_ukv': dsa_w_ukv, 'dsa_q_norm': dsa_q_norm, 'dsa_k_norm': dsa_k_norm,
        'idx_k_ln_w': idx_k_ln_w, 'idx_k_ln_b': idx_k_ln_b,
        'swa_q_norm': swa_q_norm, 'swa_k_norm': swa_k_norm, 'swa_sinks': swa_sinks,
        'ssm_conv_w': ssm_conv_w, 'ssm_conv_b': ssm_conv_b, 'ssm_dt_bias': ssm_dt_bias,
        'ssm_a_log': ssm_a_log, 'ssm_d': ssm_d, 'ssm_norm': ssm_norm,
        'w_br_dsa': w_br_dsa, 'w_br_swa': w_br_swa, 'w_br_ssm': w_br_ssm, 'w_out': w_out,
        'norm_xa': norm_xa, 'norm_mem': norm_mem, 'xa_wq': xa_wq, 'xa_wkv': xa_wkv,
        'xa_q_norm': xa_q_norm, 'xa_k_norm': xa_k_norm, 'xa_wo': xa_wo,
        'norm_ffn': norm_ffn, 'ffn_w_gate_up': ffn_w_gate_up, 'ffn_w_down': ffn_w_down,
    }

def reference(x, mem, norm_mix, w_in,
              dsa_kv_norm, dsa_w_ukv, dsa_q_norm, dsa_k_norm, idx_k_ln_w, idx_k_ln_b,
              swa_q_norm, swa_k_norm, swa_sinks,
              ssm_conv_w, ssm_conv_b, ssm_dt_bias, ssm_a_log, ssm_d, ssm_norm,
              w_br_dsa, w_br_swa, w_br_ssm, w_out,
              norm_xa, norm_mem, xa_wq, xa_wkv, xa_q_norm, xa_k_norm, xa_wo,
              norm_ffn, ffn_w_gate_up, ffn_w_down):
    b, s, d = x.shape
    for i in range(DEPTH):
        u = _rms(x, norm_mix[i])
        (dq, dckv, iq, ik, iw, sq, sk, sv, zz, xbc, dt, gates) = _split_cols(u @ w_in[i], IN_SPLITS)
        y_dsa = dsa_mixer(dq, dckv, iq, ik, iw, dsa_kv_norm[i], dsa_w_ukv[i], dsa_q_norm[i],
                          dsa_k_norm[i], idx_k_ln_w[i], idx_k_ln_b[i]) @ w_br_dsa[i]
        y_swa = swa_mixer(sq, sk, sv, swa_q_norm[i], swa_k_norm[i], swa_sinks[i]) @ w_br_swa[i]
        y_ssm = mamba2_mixer(zz, xbc, dt, ssm_conv_w[i], ssm_conv_b[i], ssm_dt_bias[i],
                             ssm_a_log[i], ssm_d[i], ssm_norm[i]) @ w_br_ssm[i]
        g = jax.nn.sigmoid(gates.astype(jnp.float32)).astype(x.dtype).reshape(b, s, N_BRANCH, d)
        merged = g[:, :, 0] * y_dsa + g[:, :, 1] * y_swa + g[:, :, 2] * y_ssm
        x = x + merged @ w_out[i]
        x = x + memory_cross_attention(_rms(x, norm_xa[i]), _rms(mem, norm_mem[i]), xa_wq[i], xa_wkv[i],
                                       xa_q_norm[i], xa_k_norm[i], xa_wo[i])
        x = x + swiglu_ffn(_rms(x, norm_ffn[i]), ffn_w_gate_up[i], ffn_w_down[i])
    return x


_drawn_inputs = setup_inputs


def setup_inputs(seed=0):
    import zlib

    import numpy as np

    out = dict(_drawn_inputs(seed))
    spreads = {}
    factors = {'norm_mix': 5.784,
     'dsa_kv_norm': 8.0,
     'dsa_q_norm': 8.0,
     'dsa_k_norm': 8.0,
     'idx_k_ln_w': 8.0,
     'idx_k_ln_b': 8.0,
     'swa_q_norm': 8.0,
     'swa_k_norm': 8.0,
     'swa_sinks': 8.0,
     'ssm_conv_b': 7.488,
     'ssm_d': 8.0,
     'ssm_norm': 8.0,
     'norm_xa': 8.0,
     'norm_mem': 8.0,
     'xa_q_norm': 8.0,
     'xa_k_norm': 8.0,
     'norm_ffn': 8.0}
    for name, (base, spread) in spreads.items():
        noise = np.random.default_rng([zlib.crc32(name.encode()), seed]).standard_normal(out[name].shape)
        drawn = base * np.exp(spread * noise) if base else spread * noise
        out[name] = __import__('jax').numpy.asarray(drawn.astype(out[name].dtype))
    for name, factor in factors.items():
        out[name] = (out[name] * factor).astype(out[name].dtype)
    return out
```

```python
from contextlib import ExitStack

import concourse.bass as bass
from concourse import mybir

F32 = mybir.dt.float32
F32R = mybir.dt.float32r
ALU = mybir.AluOpType
ACT = mybir.ActivationFunctionType
AXX = mybir.AxisListType.X

P = 128
D = 1024
S = 1024
KT = D // P
NT = S // P
CHUNK = 64
EPS = 1e-6
HD = 64
HEADS = 16
PAIRS = HEADS // 2
KV_RANK = 256
IDX_HEADS = 8
TOPK = 256
GROUPS = 2
STATE = 128
XC = (D + 2 * GROUPS * STATE) // P
CONV = 4
N_MEM = 256
MT = N_MEM // P
XH = 4
XD = D // XH
DFF = 2816
FT = DFF // P
FC = 4
FCH = -(-FT // FC)
PARAMS = 9 + 1 + 12 + 4 + 1
NEG = -1e30
TAKEN = -3e38
BARRED = -1e38
AT_SCALE = HD ** -0.5
XA_SCALE = XD ** -0.5
IDX_SCALE = IDX_HEADS ** -0.5 * HD ** -0.5

C_Q, C_CKV, C_IQ, C_IK = 0, 1024, 1280, 1792
C_SQ, C_SK, C_SV, C_Z, C_XBC, C_DT, C_G = 1864, 2888, 3016, 3144, 4168, 5704, 5720
IKW = HD + IDX_HEADS


def tile_plan():
    plan = [
        ("ikw", "w_in", 0, KT, C_IK, IKW, 1), ("ckv", "w_in", 0, KT, C_CKV, P, 2), ("iq", "w_in", 0, KT, C_IQ, P, 4),
        ("gate", "w_in", 0, KT, C_G, P, 24),
        ("z", "w_in", 0, KT, C_Z, P, 8), ("q", "w_in", 0, KT, C_Q, P, 8),
        ("sk", "w_in", 0, KT, C_SK, P, 1), ("sv", "w_in", 0, KT, C_SV, P, 1), ("sq", "w_in", 0, KT, C_SQ, P, 8),
        ("dt", "w_in", 0, KT, C_DT, HEADS, 1), ("xbc", "w_in", 0, KT, C_XBC, P, XC),
        ("br0", "w_br_dsa", 0, KT, 0, P, 8), ("br1", "w_br_swa", 0, KT, 0, P, 8), ("br2", "w_br_ssm", 0, KT, 0, P, 8),
        ("out", "w_out", 0, KT, 0, P, 8),
        ("xk", "xa_wkv", 0, KT, 0, P, 8), ("xv", "xa_wkv", 0, KT, D, P, 8), ("xq", "xa_wq", 0, KT, 0, P, 8),
        ("xo", "xa_wo", 0, KT, 0, P, 8),
    ]
    for c in range(0, FT, FC):
        w = min(FC, FT - c)
        plan.append((f"gu{c}", "ffn_w_gate_up", 0, KT, (c * P, DFF + c * P), P, 2 * w))
        plan.append((f"dn{c}", "ffn_w_down", c, w, 0, P, 8))
    return plan


def build(nc, ap, out):
    plan = tile_plan()
    first = {}
    n = 0
    for name, *_, count in plan:
        first[name] = n
        n += count
    n_tiles = n

    ctx = ExitStack()
    with ctx:
        def sem(name):
            return ctx.enter_context(nc.semaphore(name))

        def sb(name, shape, dt=F32, stack=ctx):
            return stack.enter_context(nc.sbuf_tensor(name, shape, dt))

        def dram(name, shape):
            return nc.dram_tensor(name, shape, F32, kind="Internal").ap()

        gate_d = dram("gate_d", (3 * KT, P, S))
        z_d = dram("z_d", (KT, P, S))
        y_d = dram("y_d", (3, KT, P, S))

        AH, AL = sb("AH", [P, KT, S], F32R), sb("AL", [P, KT, S], F32R)
        WH, WL = sb("WH", [P, 2, KT, P], F32R), sb("WL", [P, 2, KT, P], F32R)
        wraw = sb("wraw", [P, 4, KT, P])
        ident, ones, bones = sb("ident", [P, P]), sb("ones", [P, P]), sb("bones", [P, P])
        tri, cmask = sb("tri", [P, P]), sb("cmask", [P, P])
        prow, pcol = sb("prow", [P, P]), sb("pcol", [P, P])
        nsink, dskip = sb("nsink", [P, HEADS]), sb("dskip", [P, HEADS])
        dtb, alog = sb("dtb", [P, HEADS]), sb("alog", [P, HEADS])
        sqb, tmp, rst = sb("sqb", [P, 2, S]), sb("tmp", [P, 2, S]), sb("rst", [P, S])
        small = sb("small", [P, 64])

        g = ExitStack()
        xT0 = sb("xT0", [P, KT, S], F32, g)
        g.close()
        g = ExitStack()
        sc_off = [P * qb * (qb + 1) // 2 for qb in range(NT)]
        scores = sb("scores", [P, P * NT * (NT + 1) // 2], F32, g)
        kh, kl = sb("kh", [P, 3, S], F32R, g), sb("kl", [P, 3, S], F32R, g)
        kvt, svt = sb("kvt", [P, NT, 2 * HD], F32, g), sb("svt", [P, NT, P], F32, g)
        qT = sb("qT", [P, PAIRS, S], F32, g)
        qst = sb("qst", [P, 2, 2, P], F32R, g)
        otok, oT = sb("otok", [P, 2, P], F32, g), sb("oT", [P, 2, P], F32, g)
        swm = sb("swm", [P, 2 * P], F32, g)
        wukv = oT
        m8, ixw = sb("m8", [P, 2, 8], F32, g), sb("ixw", [P, NT, IDX_HEADS], F32, g)
        stat = sb("stat", [P, 2, 8], F32, g)
        g.close()
        iqT, ckvT, ikd = qT[:, 0:4, :], qT[:, 5:7, :], qT[:, 7, :]
        ikh, ikl = kh[:, 1, :], kl[:, 1, :]
        pT = rst
        g = ExitStack()
        xcT = sb("xcT", [P, XC, S], F32, g)
        zt, xtok, ztok = sb("zt", [P, KT, P], F32, g), sb("xtok", [P, D], F32, g), sb("ztok", [P, D], F32, g)
        xdt, xw, btok = sb("xdt", [P, D], F32, g), sb("xw", [P, D], F32, g), sb("btok", [P, 2 * STATE], F32, g)
        st = sb("st", [P, D], F32, g)
        yt = sb("yt", [P, D], F32, g)
        dts = sb("dts", [P, 8, NT, HEADS], F32, g)
        g.close()
        g = ExitStack()
        xT = sb("xT", [P, KT, S], F32, g)
        g2 = ExitStack()
        merged = sb("merged", [P, KT, S], F32, g2)
        g2.close()
        g2 = ExitStack()
        xqT = sb("xqT", [P, KT, S], F32, g2)
        xkT, xv = sb("xkT", [P, KT, N_MEM], F32, g2), sb("xv", [P, MT, D], F32, g2)
        g2.close()
        g2 = ExitStack()
        HH, HL = sb("HH", [P, FC, S], F32R, g2), sb("HL", [P, FC, S], F32R, g2)
        g2.close()
        g.close()

        psG = ctx.enter_context(nc.psum_tensor("psG", [P, 2, S], F32))
        psA = ctx.enter_context(nc.psum_tensor("psA", [P, S], F32))
        psB = ctx.enter_context(nc.psum_tensor("psB", [P, 512], F32))
        psC = ctx.enter_context(nc.psum_tensor("psC", [P, 512], F32))


        s_par, s_const, s_pcol, s_alog = sem("s_par"), sem("s_const"), sem("s_pcol"), sem("s_alog")
        x_in = [sem("x_in0"), sem("x_in1")]
        x_tr, x_cp = sem("x_tr"), sem("x_cp")
        n_sq, n_acc, n_sum, n_rstd, n_out, n_hi, n_lo = (sem(f"n_{x}") for x in ("sq", "acc", "sum", "rstd", "out", "hi", "lo"))
        w_in = [sem(f"w_in{i}") for i in range(4)]
        w_hi, w_lo = sem("w_hi"), sem("w_lo")
        mm = sem("mm")
        free = [sem("free0"), sem("free1")]
        ik_step, kv_sq, kv_pe, kv_ln, kv_done, kp_step = (sem(x) for x in ("ik_step", "kv_sq", "kv_pe", "kv_ln", "kv_done", "kp_step"))
        ix_q, ix_pe, ix_relu, ix_acc, tk_max, tk_rep, masked = (sem(x) for x in ("ix_q", "ix_pe", "ix_relu", "ix_acc", "tk_max", "tk_rep", "masked"))
        g_st = [sem("g_st0"), sem("g_st1")]
        q_sq, q_sum, q_ln, q_rstd, q_done = (sem(f"q_{x}") for x in ("sq", "sum", "ln", "rstd", "done"))
        sv_cp = sem("sv_cp")
        a_q, a_s, a_mx0, a_mx, a_exp, a_snk, a_t, a_cp, a_pv, a_den, a_ri, a_o, a_ot, a_oc = (
            sem(f"a_{x}") for x in ("q", "s", "mx0", "mx", "exp", "snk", "t", "cp", "pv", "den", "ri", "o", "ot", "oc"))
        y_st = [sem("y_st0"), sem("y_st1")]
        dt_step, acv, cv_acc, cv_out = sem("dt_step"), sem("acv"), sem("cv_acc"), sem("cv_out")
        s_zin, s_xt, s_xdt, s_xtok, s_xw, s_zt, s_ztok, s_bt, s_btok, s_g = (
            sem(f"s_{x}") for x in ("zin", "xt", "xdt", "xtok", "xw", "zt", "ztok", "bt", "btok", "g"))
        s_bc, s_df, s_dm, s_e, s_m, s_yd, s_yo, s_upd, s_dec, s_stt, s_y, s_yp, s_ss, s_rs, s_yn, s_ytr, s_ycp, s_yst = (
            sem(f"s_{x}") for x in ("bc", "df", "dm", "e", "m", "yd", "yo", "upd", "dec", "stt", "y", "yp", "ss", "rs", "yn",
                                    "ytr", "ycp", "yst"))
        g_in = [sem("g_in0"), sem("g_in1")]
        b_in = [sem("b_in0"), sem("b_in1")]
        b_hi, b_lo, m_add = sem("b_hi"), sem("b_lo"), sem("m_add")
        xk_sq, xk_sum, xk_ln, xk_rstd, xk_done = (sem(f"xk_{x}") for x in ("sq", "sum", "ln", "rstd", "done"))
        c_s, c_mx0, c_mx, c_exp, c_t, c_cp, c_pv, c_ri, c_o, c_ot, c_hi, c_lo = (
            sem(f"c_{x}") for x in ("s", "mx0", "mx", "exp", "t", "cp", "pv", "ri", "o", "ot", "hi", "lo"))
        f_hi, f_lo = sem("f_hi"), sem("f_lo")
        o_tr, o_cp, o_st = sem("o_tr"), sem("o_cp"), [sem("o_st0"), sem("o_st1")]
        s_off = sem("s_off")
        pool_go, dve_go = sem("pool_go"), sem("dve_go")
        block = ctx.enter_context(nc.Block())
        MIX, XA, FFN, MEM, CW, CB, KVN, SSN, XQN, XKN, DQ, DK, SQ, SK, IW, IB = (
            0, 8, 16, 24, 32, 80, 92, 94, 102, 104, 106, 107, 108, 109, 110, 111)

        ix_units = [(t, h) for t in range(TOPK // P, NT) for h in range(IDX_HEADS)]

        def col(i):
            return pcol[:, i:i + 1]

        def heads3(x, n=NT):
            return x.rearrange("p (t c) -> p t c", t=n)

        def read_out(eng, tile):
            eng.wait_ge(free[tile % 2], tile // 2 + 1)

        def all_read_out(eng, tile):
            read_out(eng, tile - 1)
            read_out(eng, tile - 2)

        def up_tile(n):
            return first[f"gu{n // FC * FC}"] + 2 * (n % FC) + 1

        def wide(x, shape):
            return x.unsqueeze(len(shape) - 1).to_broadcast(shape)

        w_dram = {k: ap[k][0].rearrange("(k p) n -> p k n", p=P)
                  for k in ("w_in", "w_br_dsa", "w_br_swa", "w_br_ssm", "w_out", "xa_wkv", "xa_wq", "xa_wo",
                            "ffn_w_gate_up", "ffn_w_down")}
        x_rows = ap["x"][0].rearrange("(t p) d -> t p d", p=P)
        mem_rows = ap["mem"][0].rearrange("(t p) d -> t p d", p=P)
        out_rows = out[0].rearrange("(t p) d -> t p d", p=P)
        memT = xqT[:, 0:2, :].rearrange("p a (b c) -> p (a b) c", c=N_MEM)
        turns = [(x_rows, NT, xT0), (x_rows, NT, xT), (mem_rows, MT, memT)]
        turn_first = [0, NT, 2 * NT]
        norms = [(xT0, MIX, S), (memT, MEM, N_MEM), (xT, XA, S), (xT, FFN, S)]

        @block.sync
        def _(sp):
            def turn(i):
                src, tiles, _ = turns[i]
                for t in range(tiles):
                    q = turn_first[i] + t
                    if q >= 2:
                        sp.wait_ge(x_tr, q - 1)
                    sp.dma_start(tmp[:, q % 2, :], src[t]).then_inc(x_in[q % 2], 16)

            def weight_tiles(name, lo, hi):
                _, w, k0, kn, c0, width, count = next(x for x in plan if x[0] == name)
                t0 = first[name]

                def one(u, j):
                    slot = (t0 + u) % 4
                    if t0 + u >= 4:
                        sp.wait_ge(w_lo, t0 + u - 3 + 4 * j)
                    if isinstance(c0, tuple):
                        c = c0[u % 2] + P * (u // 2) + 2 * P * j
                    else:
                        c = c0 + P * u + 4 * P * j
                    sp.dma_start(wraw[:, slot, 0:kn, 0:width], w_dram[w][:, k0:k0 + kn, bass.ds(c, width)])\
                        .then_inc(w_in[slot], 16)

                if hi is not None:
                    for u in range(lo, hi):
                        one(u, 0)
                elif count % 4 == 0 and count > 4:
                    with sp.Fori(0, count // 4) as j:
                        for u in range(4):
                            one(u, j)
                else:
                    for u in range(count):
                        one(u, 0)

            def weights(name):
                weight_tiles(name, 0, None)

            sp.wait_ge(s_const, 1)
            for key, at in (("norm_mix", MIX), ("norm_xa", XA), ("norm_ffn", FFN), ("norm_mem", MEM),
                            ("ssm_conv_b", CB), ("dsa_kv_norm", KVN), ("ssm_norm", SSN), ("xa_q_norm", XQN),
                            ("xa_k_norm", XKN)):
                rows = ap[key][0].rearrange("(r c) -> r c", c=P)
                sp.dma_start(prow[at:at + rows.shape[0], :], rows).then_inc(s_par, 16)
            sp.dma_start(prow[CW:CW + CONV * XC, :], ap["ssm_conv_w"][0].rearrange("j (r c) -> (j r) c", c=P))\
                .then_inc(s_par, 16)
            for key, at in (("dsa_q_norm", DQ), ("dsa_k_norm", DK), ("swa_q_norm", SQ), ("swa_k_norm", SK),
                            ("idx_k_ln_w", IW), ("idx_k_ln_b", IB)):
                for half in range(2):
                    sp.dma_start(prow[at:at + 1, half * HD:(half + 1) * HD], ap[key]).then_inc(s_par, 16)
            for key, dst in (("swa_sinks", nsink), ("ssm_d", dskip), ("ssm_dt_bias", dtb), ("ssm_a_log", alog)):
                sp.dma_start(dst[:, :], ap[key][0].partition_broadcast(P)).then_inc(s_par, 16)
            sp.dma_start(wukv[:, :, :], ap["dsa_w_ukv"][0].rearrange("(k p) n -> p k n", p=P)).then_inc(s_par, 16)
            turn(0)
            weights("ikw")
            weights("ckv")
            weights("iq")
            weights("gate")
            weights("z")
            weights("q")
            weights("sk")
            weights("sv")
            weights("sq")
            weights("dt")
            weights("xbc")
            for c in range(NT):
                if c == 0:
                    for i in range(2):
                        sp.wait_ge(g_st[i], 16 * 16)
                else:
                    sp.wait_ge(s_zt, c)
                sp.dma_start(zt[:, :, :], z_d[:, :, c * P:(c + 1) * P].rearrange("k p s -> p k s"))\
                    .then_inc(s_zin, 16)
            weight_tiles("br0", 0, 4)
            for i in range(2):
                sp.wait_ge(y_st[i], 16 * 64)
            sp.wait_ge(s_yst, 16 * NT)
            turn(1)
            sp.wait_ge(x_tr, 2 * NT)
            for b in range(3):
                for k in range(KT):
                    n = KT * b + k
                    if n >= 2:
                        sp.wait_ge(b_lo, n - 1)
                    sp.dma_start(tmp[:, n % 2, :], y_d[b, k]).then_inc(b_in[n % 2], 16)
                for k in range(KT):
                    n = KT * b + k
                    if n >= 2:
                        read_out(sp, first[f"br{b}"] + k - 2)
                    sp.dma_start(sqb[:, n % 2, :], gate_d[n]).then_inc(g_in[n % 2], 16)
                    if k < 4:
                        weight_tiles(f"br{b}", k + 4, k + 5)
                    elif b < 2:
                        weight_tiles(f"br{b + 1}", k - 4, k - 3)
            weights("out")
            sp.wait_ge(b_lo, 3 * KT)
            turn(2)
            weights("xk")
            weights("xv")
            weights("xq")
            weights("xo")
            for c in range(0, FT, FC):
                weights(f"gu{c}")
                weights(f"dn{c}")
            for t in range(NT):
                sp.wait_ge(o_cp, t + 1)
                sp.dma_start(out_rows[t], sqb[:, t % 2, :]).then_inc(o_st[t % 2], 16)
            for i in range(2):
                sp.wait_ge(o_st[i], 16 * NT // 2)

        @block.gpsimd
        def _(pool):
            pool.memset(prow[:, :], 0.0).then_inc(s_const, 1)
            pool.memset(ident[:, :], 0.0).then_inc(s_const, 1)
            pool.memset(ones[:, :], 1.0).then_inc(s_const, 1)
            pool.memset(bones[:, :], 0.0).then_inc(s_const, 1)
            pool.memset(cmask[:, :], 0.0).then_inc(s_const, 1)
            pool.wait_ge(s_const, 5)
            pool.affine_select(out=ident[:, :], in_=ident[:, :], compare_op=ALU.not_equal, fill=1.0, base=0,
                               pattern=[[-1, P]], channel_multiplier=1).then_inc(s_const, 1)
            pool.affine_select(out=tri[:, :], in_=ones[:, :], compare_op=ALU.is_ge, fill=0.0, base=0,
                               pattern=[[1, P]], channel_multiplier=-1).then_inc(s_const, 1)
            pool.affine_select(out=cmask[:, :], in_=cmask[:, :], compare_op=ALU.is_ge, fill=NEG, base=0,
                               pattern=[[1, P]], channel_multiplier=-1).then_inc(s_const, 1)
            for i in range(2):
                pool.wait_ge(s_const, 8 + i)
                pool.memset(bones[i * HD:(i + 1) * HD, i * HD:(i + 1) * HD], 1.0).then_inc(s_const, 1)

            def split(name):
                _, w, k0, kn, c0, width, count = next(x for x in plan if x[0] == name)
                t0 = first[name]

                def one(u, j):
                    raw, two = (t0 + u) % 4, (t0 + u) % 2
                    src = wraw[:, raw, 0:kn, 0:width]
                    hi, lo = WH[:, two, 0:kn, 0:width], WL[:, two, 0:kn, 0:width]
                    if t0 + u >= 2:
                        pool.wait_ge(mm, t0 + u - 1 + 4 * j)
                    pool.wait_ge(w_in[raw], 16 * ((t0 + u) // 4 + 1 + j))
                    pool.sem_inc(pool_go, 1)
                    pool.tensor_copy(hi, src).then_inc(w_hi, 1)
                    pool.wait_ge(w_hi, t0 + u + 1 + 4 * j)
                    pool.tensor_tensor(lo, src, hi.bitcast(F32), ALU.subtract).then_inc(w_lo, 1)

                if count % 4 == 0 and count > 4:
                    with pool.Fori(0, count // 4) as j:
                        for u in range(4):
                            one(u, j)
                else:
                    for u in range(count):
                        one(u, 0)

            def stage(n, src, staged):
                pool.tensor_copy(qst[:, n % 2, :, :], src.unsqueeze(1).to_broadcast([P, 2, P])).then_inc(staged, 1)
                for h in range(2):
                    a, b = slice(h * HD, (h + 1) * HD), slice((1 - h) * HD, (2 - h) * HD)
                    pool.wait_ge(staged, 3 * n + 1 + h)
                    pool.tensor_tensor(qst[b, n % 2, h, :], src[a], qst[a, n % 2, h, :].bitcast(F32), ALU.subtract)\
                        .then_inc(staged, 1)
                pool.wait_ge(staged, 3 * n + 3)

            def stage_indexer():
                for m in range((NT - TOPK // P) * IDX_HEADS // 2):
                    if m == 0:
                        all_read_out(pool, first["gate"])
                    if m >= 2:
                        pool.wait_ge(ix_pe, 2 * m - 2)
                    t, p = TOPK // P + m // (IDX_HEADS // 2), m % (IDX_HEADS // 2)
                    stage(m, iqT[:, p, t * P:(t + 1) * P], ix_q)

            def stage_queries(q0):
                for q in range(q0, q0 + NT * PAIRS):
                    if q == q0:
                        pool.wait_ge(q_done, KT * (q0 // 64 + 1))
                    if q >= 2:
                        pool.wait_ge(a_s, 2 * q - 2)
                    t, p = (q - q0) // PAIRS, q % PAIRS
                    stage(q, qT[:, p, t * P:(t + 1) * P], a_q)

            pool.wait_ge(s_const, 10)
            for name in ("ikw", "ckv", "iq"):
                split(name)
            stage_indexer()
            for name in ("gate", "z", "q", "sk", "sv"):
                split(name)
            stage_queries(0)
            split("sq")
            stage_queries(64)
            for name in ("dt", "xbc"):
                split(name)
            for c in range(NT):
                for q in range(4):
                    n = 4 * c + q
                    pool.wait_ge(s_df, n + 1)
                    pool.tensor_tensor(tmp[:, n % 2, 512:1024].rearrange("p (h l) -> p h l", h=4),
                                       tmp[:, n % 2, 0:512].rearrange("p (h l) -> p h l", h=4),
                                       cmask[:, :].unsqueeze(1).to_broadcast([P, 4, P]), ALU.add).then_inc(s_dm, 1)
                pool.wait_ge(s_xw, c + 1)
                pool.tensor_tensor(heads3(xtok[:, :], HEADS), heads3(xtok[:, :], HEADS),
                                   wide(dskip[:, :], [P, HEADS, HD]), ALU.mult).then_inc(s_yp, 1)
                pool.wait_ge(s_y, c + 1)
                pool.wait_ge(s_yp, 3 * c + 1)
                pool.tensor_tensor(yt[:, :], yt[:, :], xtok[:, :], ALU.add).then_inc(s_yp, 1)
                pool.wait_ge(s_yp, 3 * c + 2)
                pool.wait_ge(s_ztok, c + 1)
                pool.tensor_tensor(yt[:, :], yt[:, :], ztok[:, :], ALU.mult).then_inc(s_yp, 1)
            for name in ("br0", "br1", "br2", "out", "xk", "xv", "xq", "xo"):
                split(name)
            for c in range(0, FT, FC):
                split(f"gu{c}")
                split(f"dn{c}")

        @block.tensor
        def _(pe):
            def turn(i):
                _, tiles, _ = turns[i]
                for t in range(tiles):
                    q = turn_first[i] + t
                    pe.wait_ge(x_in[q % 2], 16 * (q // 2 + 1))
                    if q:
                        pe.wait_ge(x_cp, q)
                    for k in range(KT):
                        last = nc.tensor.transpose(psA[:, k * P:(k + 1) * P], tmp[:, q % 2, k * P:(k + 1) * P], ident[:, :])
                    last.then_inc(x_tr, 1)

            def halves(n):
                return [(h, min(h + 512, n)) for h in range(0, n, 512)]

            def norm(i):
                n = norms[i][2]
                pe.wait_ge(n_acc, (KT - 1) * (i + 1))
                for a, b in halves(n):
                    last = nc.tensor.matmul(psA[:, a:b], ones[:, :], rst[:, a:b], start=True, stop=True)
                last.then_inc(n_sum, 1)

            def channel_tile(i, j, hi=AH, lo=AL, kn=KT, n=S, ready=None):
                w = i % 2
                pe.wait_ge(w_lo, i + 1 + 2 * j)
                if i >= 2:
                    pe.wait_ge(free[w], i // 2 + j)
                for a, b in halves(n):
                    for k in range(kn):
                        if ready is not None and a == 0:
                            pe.wait_ge(ready[0], ready[1] + k + 1)
                        for x, (l, r) in enumerate(((WH, hi), (WH, lo), (WL, hi))):
                            last = nc.tensor.matmul(psG[:, w, a:b], l[:, w, k, :], r[:, k, a:b],
                                                    start=(k == 0 and x == 0), stop=(k == kn - 1 and x == 2))
                last.then_inc(mm, 1)

            def token_tiles(i, width, tiles=NT):
                w = i % 2
                pe.wait_ge(w_lo, i + 1)
                if i >= 2:
                    pe.wait_ge(free[w], i // 2)
                for t in range(tiles):
                    for k in range(KT):
                        for x, (l, r) in enumerate(((AH, WH), (AL, WH), (AH, WL))):
                            last = nc.tensor.matmul(psG[:, w, t * P:t * P + width], l[:, k, t * P:(t + 1) * P], r[:, w, k, 0:width],
                                                    start=(k == 0 and x == 0), stop=(k == KT - 1 and x == 2))
                last.then_inc(mm, 1)

            def gemm(name, ready=None, **kw):
                count = next(x for x in plan if x[0] == name)[-1]
                t0 = first[name]
                channel_tile(t0, 0, ready=ready, **kw)
                channel_tile(t0 + 1, 0, **kw)
                if count > 2:
                    with pe.Fori(1, count // 2) as j:
                        for u in range(2):
                            channel_tile(t0 + u, j, **kw)

            def key_prep(i):
                pe.wait_ge(kp_step, 10 * i + 6)
                for t in range(NT):
                    last = nc.tensor.transpose(psA[:, t * P:(t + 1) * P], rst[:, t * P:(t + 1) * P], ident[:, :])
                last.then_inc(kp_step, 1)

            def normed(name, i0, n, over, sq, ssum, ln, tiles_each, ready=None):
                t0 = first[name]

                def sums(u, j):
                    pe.wait_ge(sq, i0 + u + 1 + 2 * j)
                    if u % tiles_each == 0 and (i0 + u >= tiles_each or not isinstance(j, int)):
                        pe.wait_ge(ln, (i0 + u) // tiles_each + j * (2 // tiles_each))
                    for a, b in halves(n):
                        last = nc.tensor.matmul(psA[:, a:b], over[:, :], sqb[:, u % 2, a:b], start=(u % tiles_each == 0),
                                                stop=(u % tiles_each == tiles_each - 1))
                    last.then_inc(ssum, 1)

                def step(j):
                    for u in (1, 2):
                        channel_tile(t0 + u, j, n=n)
                        sums(u - 1, j)

                channel_tile(t0, 0, n=n, ready=ready)
                step(0)
                with pe.Fori(1, KT // 2 - 1) as j:
                    step(j)
                channel_tile(t0 + KT - 1, 0, n=n)
                sums(KT - 2, 0)
                sums(KT - 1, 0)

            def keys(q, kind, t):
                return (0, t + 1) if kind == "dsa" else (max(0, t - 1), min(t + 1, 2))

            def products(dst, slot, h, hi, lo):
                r = slice(h * HD, (h + 1) * HD)
                for a, b in halves(hi.shape[1]):
                    nc.tensor.matmul(dst[:, a:b], qst[:, slot, h, :], hi[:, a:b], start=True, stop=False)
                    last = nc.tensor.matmul(dst[:, a:b], qst[r, slot, h, :], lo[r, a:b], start=False, stop=True)
                return last

            def att_scores(q, h, pp, kind, t, p, first_static):
                k0, nb = keys(q, kind, t)
                pe.wait_ge(a_q, 3 * (q + 1) + 3 * pp)
                if first_static >= 2:
                    pe.wait_ge(a_mx0, 2 * q + h - 1 + 2 * pp)
                i = 0 if kind == "dsa" else 1 + p // (PAIRS // 2)
                products(psG[:, h, 0:nb * P], q % 2, h, kh[:, i, k0 * P:(k0 + nb) * P], kl[:, i, k0 * P:(k0 + nb) * P]).then_inc(a_s, 1)

            def att_turn(q, h, pp, nb, some_before):
                pe.wait_ge(a_exp, 2 * q + h + 1 + 2 * pp)
                if some_before:
                    pe.wait_ge(a_cp, 2 * q + h + 2 * pp)
                for b in range(nb):
                    last = nc.tensor.transpose(psA[:, b * P:(b + 1) * P], sqb[:, h, b * P:(b + 1) * P], ident[:, :])
                last.then_inc(a_t, 1)

            def att_values(q, h, pp, kind, t, p):
                k0, nb = keys(q, kind, t)
                pe.wait_ge(a_cp, 2 * q + h + 1 + 2 * pp)
                if 2 * q + h >= 4:
                    pe.wait_ge(a_oc, q - 1 + pp)
                o = (psB, psC)[q % 2][:, h * HD:(h + 1) * HD]
                for b in range(nb):
                    if kind == "dsa":
                        v = kvt[:, b, HD:2 * HD]
                    else:
                        v = svt[:, k0 + b, (p // 4) * HD:(p // 4 + 1) * HD]
                    last = nc.tensor.matmul(o, pT[:, b * P:(b + 1) * P], v, start=(b == 0), stop=(b == nb - 1))
                last.then_inc(a_pv, 1)

            def att_out(q, pp):
                pe.wait_ge(a_o, q + 1 + pp)
                nc.tensor.transpose((psB, psC)[q % 2][:, P:2 * P], otok[:, q % 2, :], ident[:, :]).then_inc(a_ot, 1)

            def attention(kind, q0):
                def pair(q, pp, t, p, before, after):
                    att_scores(q, 1, pp, kind, t, p, 2 * q + 1)
                    att_turn(q, 0, pp, keys(q, kind, t)[1], q > 0)
                    if before is not None:
                        att_values(q - 1, 1, pp, kind, *before)
                    if after is not None:
                        att_scores(q + 1, 0, pp, kind, *after, 2 * q + 2)
                    att_turn(q, 1, pp, keys(q, kind, t)[1], True)
                    att_values(q, 0, pp, kind, t, p)
                    if before is not None:
                        att_out(q - 1, pp)

                att_scores(q0, 0, 0, kind, 0, 0, 2 * q0)
                for t in range(NT):
                    q = q0 + PAIRS * t
                    pair(q, 0, t, 0, (t - 1, PAIRS - 1) if t else None, (t, 1))
                    if kind == "dsa" and t:
                        with pe.Fori(0, PAIRS // 2 - 1) as j:
                            for u in (1, 2):
                                pair(q + u, 2 * j, t, u, (t, u - 1), (t, u + 1))
                    else:
                        for p in range(1, PAIRS - 1):
                            pair(q + p, 0, t, p, (t, p - 1), (t, p + 1))
                    pair(q + PAIRS - 1, 0, t, PAIRS - 1, (t, PAIRS - 2), (t + 1, 0) if t < NT - 1 else None)
                q = q0 + NT * PAIRS - 1
                att_values(q, 1, 0, kind, NT - 1, PAIRS - 1)
                att_out(q, 0)

            pe.wait_ge(s_const, 10)
            pe.wait_ge(s_par, 16 * PARAMS)
            nc.tensor.transpose(psB[:, 0:P], prow[:, :], ident[:, :]).then_inc(s_pcol, 1)
            turn(0)
            norm(0)
            pe.wait_ge(n_lo, KT)
            token_tiles(first["ikw"], IKW)
            gemm("ckv")
            gemm("iq")
            all_read_out(pe, first["iq"])
            for t in range(NT):
                for k in range(2):
                    nc.tensor.matmul(psB[:, t:t + 1], sqb[:, k, t * P:(t + 1) * P], ones[:, 0:1], start=(k == 0), stop=(k == 1))
            for t in range(NT):
                for k in range(2):
                    last = nc.tensor.matmul(psA[:, t * P:(t + 1) * P], ckvT[:, k, t * P:(t + 1) * P], wukv[:, k, :],
                                            start=(k == 0), stop=(k == 1))
            last.then_inc(kv_pe, 1)
            pe.wait_ge(ik_step, 10)
            pe.wait_ge(kv_done, 1)
            for t in range(NT):
                last = nc.tensor.transpose(psA[:, t * P:(t + 1) * P], ikd[:, t * P:(t + 1) * P], ident[:, :])
            last.then_inc(ik_step, 1)
            key_prep(0)
            pe.wait_ge(ik_step, 14)
            all_read_out(pe, first["gate"])
            for v, (t, h) in enumerate(ix_units):
                if v >= 2:
                    pe.wait_ge(ix_relu, v - 1)
                pe.wait_ge(ix_q, 3 * (v // 2 + 1))
                n = (t + 1) * P
                products(psG[:, v % 2, 0:n], v // 2 % 2, h % 2, ikh[:, 0:n], ikl[:, 0:n]).then_inc(ix_pe, 1)
            pe.wait_ge(ix_relu, len(ix_units))
            gemm("gate")
            gemm("z")
            normed("q", 0, S, bones, q_sq, q_sum, q_ln, 1)
            token_tiles(first["sk"], P)
            token_tiles(first["sv"], P)
            pe.wait_ge(q_ln, KT)
            key_prep(1)
            key_prep(2)
            all_read_out(pe, first["sq"])
            pe.wait_ge(kp_step, 30)
            attention("dsa", 0)
            pe.wait_ge(a_mx0, 128)
            pe.wait_ge(a_cp, 128)
            normed("sq", KT, S, bones, q_sq, q_sum, q_ln, 1)
            all_read_out(pe, first["dt"])
            pe.wait_ge(q_ln, 2 * KT)
            attention("swa", 64)
            pe.wait_ge(a_mx0, 256)
            token_tiles(first["dt"], HEADS)
            gemm("xbc")
            pe.wait_ge(dt_step, 6)
            pe.wait_ge(a_o, 128)
            a_all = dts[:, 3, :, :].rearrange("p t h -> p (t h)")
            nc.tensor.matmul(psB[:, 0:P], tri[:, :], a_all, start=True, stop=True)
            nc.tensor.matmul(psB[:, P:2 * P], ones[:, :], a_all, start=True, stop=True).then_inc(dt_step, 1)
            pe.wait_ge(cv_out, XC)
            pe.wait_ge(dt_step, 13)
            pe.wait_ge(a_oc, 128)
            all_read_out(pe, first["br0"])
            for c in range(NT):
                cc = slice(c * P, (c + 1) * P)
                if c:
                    pe.wait_ge(s_y, c)
                for k in range(KT):
                    last = nc.tensor.transpose(psG[:, 0, k * P:(k + 1) * P], xcT[:, k, cc], ident[:, :])
                last.then_inc(s_xt, 1)
                pe.wait_ge(s_zin, 16 * (c + 1))
                for k in range(KT):
                    last = nc.tensor.transpose(psG[:, 1, k * P:(k + 1) * P], zt[:, k, :], ident[:, :])
                last.then_inc(s_zt, 1)
                if c:
                    pe.wait_ge(s_ycp, c)
                for g in range(GROUPS):
                    last = nc.tensor.transpose(psA[:, g * P:(g + 1) * P], xcT[:, KT + g, cc], ident[:, :])
                last.then_inc(s_bt, 1)
                for g in range(GROUPS):
                    last = nc.tensor.matmul(psA[:, 512 + g * P:512 + (g + 1) * P], xcT[:, KT + g, cc],
                                            xcT[:, KT + GROUPS + g, cc], start=True, stop=True)
                last.then_inc(s_g, 1)

                def decays(q):
                    n = 4 * c + q
                    if n >= 2:
                        pe.wait_ge(s_df, n - 1)
                    bank = (psB, psC)[n % 2]
                    for i in range(4):
                        h = 4 * q + i
                        last = nc.tensor.matmul(bank[:, i * P:(i + 1) * P], dts[:, 3, c, h:h + 1].to_broadcast([P, P]),
                                                tri[:, :], start=True, stop=True)
                    last.then_inc(s_bc, 1)

                def within(q):
                    n = 4 * c + q
                    pe.wait_ge(s_m, n + 1)
                    if q == 0:
                        pe.wait_ge(s_xdt, c + 1)
                        pe.wait_ge(s_xtok, c + 1)
                        pe.wait_ge(s_xw, c + 1)
                    for i in range(4):
                        h = 4 * q + i
                        last = nc.tensor.matmul(psG[:, 0, h * HD:(h + 1) * HD], sqb[:, n % 2, 512 + i * P:512 + (i + 1) * P],
                                                xdt[:, h * HD:(h + 1) * HD], start=True, stop=True)
                    last.then_inc(s_yd, 1)

                decays(0)
                decays(1)
                within(0)
                decays(2)
                within(1)
                decays(3)
                within(2)
                within(3)
                if c:
                    pe.wait_ge(s_ztok, c + 1)
                    pe.wait_ge(s_stt, 2 * c)
                    for g in range(GROUPS):
                        last = nc.tensor.matmul(psG[:, 1, g * 512:(g + 1) * 512], xcT[:, KT + GROUPS + g, cc],
                                                st[:, g * 512:(g + 1) * 512], start=True, stop=True)
                    last.then_inc(s_yo, 1)
                if c < NT - 1:
                    for g in range(GROUPS):
                        if g == 0:
                            pe.wait_ge(s_btok, c + 1)
                        else:
                            pe.wait_ge(s_stt, 2 * c + 1)
                        nc.tensor.matmul(psA[:, 0:512], btok[:, g * P:(g + 1) * P], xw[:, g * 512:(g + 1) * 512],
                                         start=True, stop=True).then_inc(s_upd, 1)
                    pe.wait_ge(s_stt, 2 * c + 2)
                pe.wait_ge(s_btok, c + 1)
                pe.wait_ge(s_yn, 2 * c + 2)
                for k in range(KT):
                    last = nc.tensor.transpose(psA[:, k * P:(k + 1) * P], yt[:, k * P:(k + 1) * P], ident[:, :])
                last.then_inc(s_ytr, 1)
            pe.wait_ge(s_y, NT)
            pe.wait_ge(s_ycp, NT)
            turn(1)
            for b in range(3):
                gemm(f"br{b}", ready=(b_lo, KT * b))
            gemm("out", ready=(b_lo, 3 * KT))
            turn(2)
            norm(1)
            normed("xk", 0, N_MEM, ones, xk_sq, xk_sum, xk_ln, 2, ready=(n_lo, KT))
            for i in range(KT):
                token_tiles(first["xv"] + i, P, MT)
            pe.wait_ge(xk_ln, XH)
            norm(2)
            normed("xq", KT, S, ones, xk_sq, xk_sum, xk_ln, 2, ready=(n_lo, 2 * KT))
            units = NT * XH
            pe.wait_ge(xk_done, 4 * XH)
            all_read_out(pe, first["xo"])

            def cross(w):
                return slice((w // XH) * P, (w // XH + 1) * P), w % XH, w % 2

            for w in range(units + 3):
                if w < units:
                    tt, h, z = cross(w)
                    if w >= 2:
                        pe.wait_ge(c_exp, w - 1)
                    for i in range(2):
                        last = nc.tensor.matmul(psG[:, z, 0:N_MEM], xqT[:, 2 * h + i, tt], xkT[:, 2 * h + i, :],
                                                start=(i == 0), stop=(i == 1))
                    last.then_inc(c_s, 1)
                if 1 <= w <= units:
                    tt, h, z = cross(w - 1)
                    pe.wait_ge(c_exp, w)
                    if w >= 3:
                        pe.wait_ge(c_cp, w - 2)
                    for i in range(MT):
                        last = nc.tensor.transpose(psA[:, z * 512 + i * P:z * 512 + (i + 1) * P],
                                                   sqb[:, z, i * P:(i + 1) * P], ident[:, :])
                    last.then_inc(c_t, 1)
                if 2 <= w <= units + 1:
                    tt, h, z = cross(w - 2)
                    pe.wait_ge(c_cp, w - 1)
                    if w >= 4:
                        pe.wait_ge(c_o, w - 3)
                    for i in range(MT):
                        last = nc.tensor.matmul((psB, psC)[z][:, 0:XD], tmp[:, z, i * P:(i + 1) * P],
                                                xv[:, i, h * XD:(h + 1) * XD], start=(i == 0), stop=(i == MT - 1))
                    last.then_inc(c_pv, 1)
                if 3 <= w:
                    tt, h, z = cross(w - 3)
                    pe.wait_ge(c_o, w - 2)
                    if w >= 5:
                        pe.wait_ge(c_lo, w - 4)
                    for i in range(2):
                        last = nc.tensor.transpose(psG[:, z, 512 + i * P:512 + (i + 1) * P],
                                                   tmp[:, z, 512 + i * P:512 + (i + 1) * P], ident[:, :])
                    last.then_inc(c_ot, 1)
            pe.wait_ge(c_lo, units)
            gemm("xo")
            norm(3)
            for c in range(0, FT, FC):
                gemm(f"gu{c}", ready=None if c else (n_lo, 3 * KT))
                gemm(f"dn{c}", ready=(f_lo, c), hi=HH, lo=HL, kn=min(FC, FT - c))
            all_read_out(pe, n_tiles)
            for t in range(NT):
                if t:
                    pe.wait_ge(o_cp, t)
                for k in range(KT):
                    last = nc.tensor.transpose(psA[:, k * P:(k + 1) * P], xT[:, k, t * P:(t + 1) * P], ident[:, :])
                last.then_inc(o_tr, 1)


        @block.scalar
        def _(act):
            def norm(i):
                src, _, n = norms[i]
                if i == 0:
                    act.wait_ge(x_cp, NT)
                elif i == 1:
                    act.wait_ge(x_cp, 2 * NT + MT)
                elif i == 2:
                    act.wait_ge(xk_done, KT)
                for k in range(KT):
                    if i >= 2:
                        read_out(act, first["out" if i == 2 else "xo"] + k)
                    if k >= 3:
                        act.wait_ge(n_acc, (KT - 1) * i + k - 2)
                    dst = sqb[:, k % 2, 0:n] if k else rst[:, 0:n]
                    act.activation(dst, src[:, k, 0:n], ACT.Square).then_inc(n_sq, 1)
                act.wait_ge(n_sum, i + 1)
                act.activation(rst[:, 0:n], psA[:, 0:n], ACT.Ln, scale=1.0 / D, bias=EPS).then_inc(n_rstd, 1)
                act.wait_ge(n_rstd, 2 * i + 1)
                act.activation(rst[:, 0:n], rst[:, 0:n], ACT.Exp, scale=-0.5).then_inc(n_rstd, 1)
                act.wait_ge(mm, (0, first["xk"], first["xq"], first["gu0"])[i])
                for k in range(KT):
                    act.wait_ge(n_out, KT * i + k + 1)
                    act.activation(AH[:, k, 0:n], tmp[:, k % 2, 0:n], ACT.Copy).then_inc(n_hi, 1)

            def stored(name, func, dst, m0):
                t0 = first[name]
                count = next(x for x in plan if x[0] == name)[-1]

                def pair(j):
                    for u in range(2):
                        w, z = (t0 + u) % 2, (m0 + u) % 2
                        act.wait_ge(mm, t0 + u + 1 + 2 * j)
                        if m0 + u >= 2 or not isinstance(j, int):
                            act.wait_ge(g_st[z], 16 * ((m0 + u) // 2 + j))
                        act.activation(sqb[:, z, :], psG[:, w, :], func).then_inc(free[w], 1)
                        act.wait_ge(free[w], (t0 + u) // 2 + 1 + j)
                        act.dma_start(dst[bass.ds(u + 2 * j, 1)].rearrange("a p s -> (a p) s"), sqb[:, z, :]).then_inc(g_st[z], 16)

                pair(0)
                with act.Fori(1, count // 2) as j:
                    pair(j)

            def head_norms(name, i0, n, sq, ssum, ln, rstd, done, each, scale):
                t0 = first[name]

                def square(u, j):
                    act.wait_ge(mm, t0 + u + 1 + 2 * j)
                    if i0 + u >= 2:
                        act.wait_ge(ssum, i0 + u - 1 + 2 * j)
                    act.activation(sqb[:, u % 2, 0:n], psG[:, (t0 + u) % 2, 0:n], ACT.Square).then_inc(sq, 1)

                def root(u, j):
                    if u % each != each - 1:
                        return
                    g = (i0 + u) // each
                    gj = j * (2 // each)
                    act.wait_ge(ssum, i0 + u + 1 + 2 * j)
                    if g >= 1 or not isinstance(j, int):
                        act.wait_ge(done, g * each + gj * each)
                    act.activation(rst[:, 0:n], psA[:, 0:n], ACT.Ln, scale=scale, bias=EPS).then_inc(ln, 1)
                    act.wait_ge(ln, g + 1 + gj)
                    act.activation(rst[:, 0:n], rst[:, 0:n], ACT.Exp, scale=-0.5).then_inc(rstd, 1)

                def step(j):
                    for u in (1, 2):
                        square(u, j)
                        root(u - 1, j)

                square(0, 0)
                step(0)
                with act.Fori(1, KT // 2 - 1) as j:
                    step(j)
                square(KT - 1, 0)
                root(KT - 2, 0)
                root(KT - 1, 0)

            def key_root(i):
                act.wait_ge(kp_step, 10 * i + 2)
                act.activation(small[:, 8:16], small[:, 0:8], ACT.Ln, scale=1.0 / HD, bias=EPS).then_inc(kp_step, 1)
                act.wait_ge(kp_step, 10 * i + 3)
                act.activation(small[:, 8:16], small[:, 8:16], ACT.Exp, scale=-0.5).then_inc(kp_step, 1)
                act.wait_ge(kp_step, 10 * i + 8)
                act.activation(kh[:, i, :], rst[:, :], ACT.Copy).then_inc(kp_step, 1)

            nc.scalar.preload_act_table_set("natural_log_exp_and_others")
            act.wait_ge(s_par, 16 * PARAMS)
            act.activation(alog[:, :], alog[:, :], ACT.Exp).then_inc(s_alog, 1)
            norm(0)
            act.wait_ge(mm, 1)
            act.wait_ge(n_lo, KT)
            act.activation(heads3(tmp[:, 0, :])[:, :, 0:IKW], heads3(psG[:, 0, :])[:, :, 0:IKW], ACT.Copy).then_inc(free[0], 1)
            for k in range(2):
                act.wait_ge(mm, first["ckv"] + k + 1)
                act.activation(sqb[:, k, :], psG[:, (first["ckv"] + k) % 2, :], ACT.Square).then_inc(kv_sq, 1)
            for k in range(4):
                i = first["iq"] + k
                act.wait_ge(mm, i + 1)
                act.activation(iqT[:, k, :], psG[:, i % 2, :], ACT.Copy).then_inc(free[i % 2], 1)
            act.wait_ge(kv_pe, 1)
            act.activation(small[:, 0:8], psB[:, 0:NT], ACT.Ln, scale=1.0 / KV_RANK, bias=EPS).then_inc(kv_ln, 1)
            act.wait_ge(kv_ln, 1)
            act.activation(small[:, 0:8], small[:, 0:8], ACT.Exp, scale=-0.5).then_inc(kv_ln, 1)
            act.wait_ge(ik_step, 5)
            act.activation(small[:, 24:32], small[:, 16:24], ACT.Ln, scale=1.0 / HD, bias=EPS).then_inc(ik_step, 1)
            act.wait_ge(ik_step, 6)
            act.activation(small[:, 24:32], small[:, 24:32], ACT.Exp, scale=-0.5).then_inc(ik_step, 1)
            act.wait_ge(ik_step, 12)
            act.activation(ikh, ikd, ACT.Copy).then_inc(ik_step, 1)
            key_root(0)
            for v, (t, h) in enumerate(ix_units):
                n = (t + 1) * P
                act.wait_ge(ix_pe, v + 1)
                if v >= 2:
                    act.wait_ge(ix_acc, v - 1)
                else:
                    act.wait_ge(kp_step, 6)
                act.activation(tmp[:, v % 2, 0:n], psG[:, v % 2, 0:n], ACT.Relu).then_inc(ix_relu, 1)
            stored("gate", ACT.Sigmoid, gate_d, 0)
            stored("z", ACT.Silu, z_d, 24)
            for i in range(2):
                act.wait_ge(g_st[i], 16 * 16)
            head_norms("q", 0, S, q_sq, q_sum, q_ln, q_rstd, q_done, 1, 1.0 / HD)
            act.wait_ge(q_done, KT)
            act.wait_ge(mm, first["sk"] + 1)
            act.activation(tmp[:, 1, :], psG[:, first["sk"] % 2, :], ACT.Copy).then_inc(free[first["sk"] % 2], 1)
            act.wait_ge(mm, first["sv"] + 1)
            act.activation(svt[:, :, :], heads3(psG[:, first["sv"] % 2, :]), ACT.Copy).then_inc(free[first["sv"] % 2], 1)
            key_root(1)
            key_root(2)

            def att_exp(q, h, pp, n, swa):
                act.wait_ge(a_mx, 2 * q + h + 1 + 2 * pp)
                if 2 * q + h >= 2:
                    act.wait_ge(a_t, 2 * q + h - 1 + 2 * pp)
                act.activation(sqb[:, h, 0:n], tmp[:, h, 0:n], ACT.Exp, bias=stat[:, h, 0:1], scale=AT_SCALE,
                               accum_out=stat[:, q % 2, 4 + h:5 + h]).then_inc(a_exp, 1)
                if swa is not None:
                    act.activation(stat[:, q % 2, 6 + h:7 + h], nsink[:, swa + h:swa + h + 1], ACT.Exp,
                                   bias=stat[:, h, 0:1], scale=-1.0).then_inc(a_snk, 1)

            def att_copy(q, pp, n):
                act.wait_ge(a_t, 2 * q + 1 + 2 * pp)
                if q > 0:
                    act.wait_ge(a_pv, 2 * q + 2 * pp)
                act.activation(pT[:, 0:n], psA[:, 0:n], ACT.Copy).then_inc(a_cp, 1)

            def att_store(q, pp, b, t, p):
                z = q % 2
                act.wait_ge(a_ot, q + 1 + pp)
                if q >= 2:
                    act.wait_ge(y_st[z], 16 * (q // 2) + 8 * pp)
                act.activation(oT[:, z, :], (psB, psC)[z][:, P:2 * P], ACT.Copy).then_inc(a_oc, 1)
                act.wait_ge(a_oc, q + 1 + pp)
                act.dma_start(y_d[b, bass.ds(p + pp, 1), :, t * P:(t + 1) * P].rearrange("a p s -> (a p) s"), oT[:, z, :])\
                    .then_inc(y_st[z], 16)

            def attention(kind, q0, b):
                def nk(t):
                    return P * (t + 1 if kind == "dsa" else min(t + 1, 2))

                def sink(p):
                    return 2 * p if kind == "swa" else None

                def pair(q, pp, t, p, before, after):
                    att_exp(q, 1, pp, nk(t), sink(p))
                    att_copy(q, pp, nk(t))
                    if after is not None:
                        att_exp(q + 1, 0, pp, nk(after[0]), sink(after[1]))
                    if before is not None:
                        att_store(q - 1, pp, b, *before)

                att_exp(q0, 0, 0, nk(0), sink(0))
                for t in range(NT):
                    q = q0 + PAIRS * t
                    pair(q, 0, t, 0, (t - 1, PAIRS - 1) if t else None, (t, 1))
                    if kind == "dsa" and t:
                        with act.Fori(0, PAIRS // 2 - 1) as j:
                            for u in (1, 2):
                                pair(q + u, 2 * j, t, u, (t, u - 1), (t, u + 1))
                    else:
                        for p in range(1, PAIRS - 1):
                            pair(q + p, 0, t, p, (t, p - 1), (t, p + 1))
                    pair(q + PAIRS - 1, 0, t, PAIRS - 1, (t, PAIRS - 2), (t + 1, 0) if t < NT - 1 else None)
                att_store(q0 + NT * PAIRS - 1, 0, b, NT - 1, PAIRS - 1)

            act.wait_ge(masked, NT)
            attention("dsa", 0, 0)
            head_norms("sq", KT, S, q_sq, q_sum, q_ln, q_rstd, q_done, 1, 1.0 / HD)
            attention("swa", 64, 1)
            for i in range(2):
                act.wait_ge(y_st[i], 16 * 64)
            i = first["dt"]
            act.wait_ge(mm, i + 1)
            act.activation(dts[:, 0, :, :], heads3(psG[:, i % 2, :])[:, :, 0:HEADS], ACT.Copy).then_inc(free[i % 2], 1)
            act.wait_ge(dt_step, 2)
            act.activation(dts[:, 2, :, :], dts[:, 2, :, :], ACT.Exp, scale=-1.0).then_inc(dt_step, 1)
            act.wait_ge(dt_step, 3)
            act.activation(dts[:, 2, :, :], dts[:, 2, :, :], ACT.Ln, bias=1.0).then_inc(dt_step, 1)
            with act.Fori(0, XC // 2) as j:
                for u in range(2):
                    i = first["xbc"] + u
                    act.wait_ge(free[i % 2], i // 2 + 1 + j)
                    act.activation(xcT[:, bass.ds(u + 2 * j, 1), :].rearrange("p a s -> p (a s)"), tmp[:, u, :], ACT.Silu)\
                        .then_inc(cv_out, 1)
            act.wait_ge(dt_step, 9)
            ends = psB[:, P:2 * P].rearrange("p (t h) -> p t h", t=NT)
            act.activation(dts[:, 5, :, :], ends, ACT.Exp).then_inc(dt_step, 1)
            act.wait_ge(dt_step, 10)
            act.activation(dts[:, 6, :, :], dts[:, 4, :, :], ACT.Exp).then_inc(dt_step, 1)
            act.wait_ge(dt_step, 11)
            act.activation(dts[:, 7, :, :], dts[:, 7, :, :], ACT.Exp).then_inc(dt_step, 1)
            for c in range(NT):
                act.wait_ge(s_xt, c + 1)
                if c:
                    act.wait_ge(s_yp, 3 * c)
                act.activation(xtok[:, :], psG[:, 0, :], ACT.Copy).then_inc(s_xtok, 1)
                act.wait_ge(s_zt, c + 1)
                act.activation(ztok[:, :], psG[:, 1, :], ACT.Copy).then_inc(s_ztok, 1)
                for q in range(4):
                    n = 4 * c + q
                    act.wait_ge(s_dm, n + 1)
                    if n >= 2:
                        act.wait_ge(s_m, n - 1)
                    act.activation(sqb[:, n % 2, 0:512], tmp[:, n % 2, 512:1024], ACT.Exp).then_inc(s_e, 1)
                act.wait_ge(s_ss, 2 * c + 2)
                act.activation(small[:, 34:36], small[:, 32:34], ACT.Ln, scale=1.0 / 512, bias=EPS).then_inc(s_rs, 1)
                act.wait_ge(s_rs, 2 * c + 1)
                act.activation(small[:, 34:36], small[:, 34:36], ACT.Exp, scale=-0.5).then_inc(s_rs, 1)
                act.wait_ge(s_ycp, c + 1)
                act.dma_start(y_d[2, :, :, c * P:(c + 1) * P].rearrange("k p s -> p k s"), heads3(rst[:, :])).then_inc(s_yst, 16)
            for b in range(4):
                act.wait_ge(mm, first[("br0", "br1", "br2", "out")[b]])
                for k in range(KT):
                    n = KT * b + k
                    if b < 3:
                        act.wait_ge(b_in[n % 2], 16 * (n // 2 + 1))
                    else:
                        act.wait_ge(m_add, KT + k + 1)
                    src = tmp[:, n % 2, :] if b < 3 else merged[:, k, :]
                    act.activation(AH[:, k, :], src, ACT.Copy).then_inc(b_hi, 1)
            norm(1)
            head_norms("xk", 0, N_MEM, xk_sq, xk_sum, xk_ln, xk_rstd, xk_done, 2, 1.0 / XD)
            for k in range(KT):
                i = first["xv"] + k
                act.wait_ge(mm, i + 1)
                act.activation(xv[:, :, k * P:(k + 1) * P], heads3(psG[:, i % 2, 0:MT * P], MT), ACT.Copy).then_inc(free[i % 2], 1)
            norm(2)
            head_norms("xq", KT, S, xk_sq, xk_sum, xk_ln, xk_rstd, xk_done, 2, 1.0 / XD)
            units = NT * XH
            for w in range(units + 3):
                if w < units:
                    z = w % 2
                    act.wait_ge(c_mx, w + 1)
                    if w >= 2:
                        act.wait_ge(c_t, w - 1)
                    act.activation(sqb[:, z, 0:N_MEM], psG[:, z, 0:N_MEM], ACT.Exp, bias=small[:, 40 + z:41 + z],
                                   scale=XA_SCALE, accum_out=small[:, 42 + z:43 + z]).then_inc(c_exp, 1)
                if 1 <= w <= units:
                    z = (w - 1) % 2
                    act.wait_ge(c_t, w)
                    if w >= 3:
                        act.wait_ge(c_pv, w - 2)
                    act.activation(tmp[:, z, 0:N_MEM], psA[:, z * 512:z * 512 + N_MEM], ACT.Copy).then_inc(c_cp, 1)
                if w >= 3:
                    t, h, z = (w - 3) // XH, (w - 3) % XH, (w - 3) % 2
                    act.wait_ge(c_ot, w - 2)
                    act.activation(AH[:, 2 * h:2 * h + 2, t * P:(t + 1) * P], heads3(psG[:, z, 512:768], 2), ACT.Copy)\
                        .then_inc(c_hi, 1)
            norm(3)
            for c in range(0, FT, FC):
                t0 = first[f"gu{c}"]
                for k in range(min(FC, FT - c)):
                    n = c + k
                    act.wait_ge(mm, t0 + 2 * k + 1)
                    if n >= 2:
                        read_out(act, up_tile(n - 2))
                    act.activation(sqb[:, n % 2, :], psG[:, (t0 + 2 * k) % 2, :], ACT.Silu).then_inc(free[(t0 + 2 * k) % 2], 1)
                    read_out(act, up_tile(n))
                    act.activation(HH[:, k, :], tmp[:, n % 2, :], ACT.Copy).then_inc(f_hi, 1)
            for t in range(NT):
                act.wait_ge(o_tr, t + 1)
                if t >= 2:
                    act.wait_ge(o_st[t % 2], 16 * (t // 2))
                act.activation(sqb[:, t % 2, :], psA[:, :], ACT.Copy).then_inc(o_cp, 1)

        @block.vector
        def _(dve):
            def turn(i):
                _, tiles, dst = turns[i]
                for t in range(tiles):
                    q = turn_first[i] + t
                    dve.wait_ge(x_tr, q + 1)
                    dve.tensor_copy(dst[:, :, t * P:(t + 1) * P], heads3(psA[:, :])).then_inc(x_cp, 1)

            def add_squares(i, k):
                n = norms[i][2]
                m = (KT - 1) * i + k
                dve.wait_ge(n_sq, KT * i + k + 1)
                if k > 1:
                    dve.wait_ge(n_acc, m - 1)
                dve.tensor_tensor(rst[:, 0:n], rst[:, 0:n], sqb[:, k % 2, 0:n], ALU.add).then_inc(n_acc, 1)

            def norm(i):
                src, gain, n = norms[i]
                if i < 3:
                    for k in range(1, KT):
                        add_squares(i, k)
                dve.wait_ge(n_rstd, 2 * i + 2)

                def scaled(k):
                    if k >= 2:
                        dve.wait_ge(n_lo, KT * i + k - 1)
                    dve.scalar_tensor_tensor(out=tmp[:, k % 2, 0:n], in0=src[:, k, 0:n], scalar=col(gain + k), in1=rst[:, 0:n],
                                             op0=ALU.mult, op1=ALU.mult).then_inc(n_out, 1)

                scaled(0)
                for k in range(KT):
                    if k < KT - 1:
                        scaled(k + 1)
                    dve.wait_ge(n_hi, KT * i + k + 1)
                    dve.tensor_tensor(AL[:, k, 0:n], tmp[:, k % 2, 0:n], AH[:, k, 0:n].bitcast(F32), ALU.subtract).then_inc(n_lo, 1)

            def head_norms(name, i0, n, dst, gain, sq, rstd, done, each):
                t0 = first[name]

                def at(u, j):
                    return dst[:, bass.ds(u + 2 * j, 1), :].rearrange("p a s -> p (a s)") if not isinstance(j, int) else dst[:, u, :]

                def gained(u, j):
                    dve.wait_ge(sq, i0 + u + 1 + 2 * j)
                    dve.tensor_scalar(at(u, j), psG[:, (t0 + u) % 2, 0:n], col(gain + u % each), None, ALU.mult)\
                        .then_inc(free[(t0 + u) % 2], 1)

                def divided(u, j):
                    if u % each != each - 1:
                        return
                    dve.wait_ge(rstd, (i0 + u) // each + 1 + j * (2 // each))
                    dve.wait_ge(free[(t0 + u) % 2], (t0 + u) // 2 + 1 + j)
                    for v in range(u - each + 1, u + 1):
                        dve.tensor_tensor(at(v, j), at(v, j), rst[:, 0:n], ALU.mult).then_inc(done, 1)

                gained(0, 0)
                with dve.Fori(0, KT // 2 - 1) as j:
                    for u in (1, 2):
                        gained(u, j)
                        divided(u - 1, j)
                gained(KT - 1, 0)
                divided(KT - 2, 0)
                divided(KT - 1, 0)

            def key_norm(i, kr):
                dve.tensor_tensor(tmp[:, 0, 0:512].rearrange("p (t c) -> p t c", t=NT), kr, kr, ALU.mult).then_inc(kp_step, 1)
                dve.wait_ge(kp_step, 10 * i + 1)
                dve.tensor_reduce(small[:, 0:8], tmp[:, 0, 0:512].rearrange("p (t c) -> p t c", t=NT), AXX, ALU.add)\
                    .then_inc(kp_step, 1)
                dve.wait_ge(kp_step, 10 * i + 4)
                for half in range(2):
                    dve.tensor_tensor(heads3(rst[:, :])[:, :, half * HD:(half + 1) * HD], kr, wide(small[:, 8:16], [P, NT, HD]),
                                      ALU.mult).then_inc(kp_step, 1)

            def key_gain(i, gain):
                dve.wait_ge(kp_step, 10 * i + 7)
                dve.tensor_scalar(rst[:, :], psA[:, :], col(gain), None, ALU.mult).then_inc(kp_step, 1)
                dve.wait_ge(kp_step, 10 * i + 9)
                dve.tensor_tensor(kl[:, i, :], rst[:, :], kh[:, i, :].bitcast(F32), ALU.subtract).then_inc(kp_step, 1)

            dve.wait_ge(s_pcol, 1)
            dve.tensor_copy(pcol[:, :], psB[:, 0:P]).then_inc(s_pcol, 1)
            dve.tensor_scalar(nsink[:, :], nsink[:, :], -1.0, None, ALU.mult).then_inc(s_pcol, 1)
            dve.wait_ge(s_alog, 1)
            dve.tensor_scalar(alog[:, :], alog[:, :], -1.0, None, ALU.mult).then_inc(s_alog, 1)
            dve.memset(swm[:, :], NEG).then_inc(s_pcol, 1)
            dve.wait_ge(s_pcol, 4)
            dve.memset(swm[0:HD, HD:HD + P], 0.0).then_inc(s_pcol, 1)
            dve.memset(swm[HD:P, P:2 * P], 0.0).then_inc(s_pcol, 1)
            dve.wait_ge(s_pcol, 6)
            turn(0)
            norm(0)
            for k in range(2):
                i = first["ckv"] + k
                dve.wait_ge(kv_sq, k + 1)
                dve.tensor_scalar(ckvT[:, k, :], psG[:, i % 2, :], col(KVN + k), None, ALU.mult).then_inc(free[i % 2], 1)
            ikr, ikc = heads3(tmp[:, 0, :]), heads3(tmp[:, 1, :])[:, :, 0:HD]
            dve.wait_ge(free[0], 1)
            dve.tensor_reduce(small[:, 16:24], ikr[:, :, 0:HD], AXX, ALU.add).then_inc(ik_step, 1)
            dve.wait_ge(ik_step, 1)
            dve.tensor_scalar(small[:, 16:24], small[:, 16:24], 1.0 / HD, None, ALU.mult).then_inc(ik_step, 1)
            dve.wait_ge(ik_step, 2)
            dve.tensor_tensor(ikc, ikr[:, :, 0:HD], wide(small[:, 16:24], [P, NT, HD]), ALU.subtract).then_inc(ik_step, 1)
            dve.wait_ge(ik_step, 3)
            sq3 = rst[:, 0:512].rearrange("p (t c) -> p t c", t=NT)
            dve.tensor_tensor(sq3, ikc, ikc, ALU.mult).then_inc(ik_step, 1)
            dve.wait_ge(ik_step, 4)
            dve.tensor_reduce(small[:, 16:24], sq3, AXX, ALU.add).then_inc(ik_step, 1)
            dve.wait_ge(ik_step, 7)
            for half in range(2):
                dve.tensor_tensor(heads3(ikd)[:, :, half * HD:(half + 1) * HD], ikc, wide(small[:, 24:32], [P, NT, HD]),
                                  ALU.mult).then_inc(ik_step, 1)
            dve.tensor_scalar(ixw[:, :, :], ikr[:, :, HD:IKW], IDX_SCALE, None, ALU.mult).then_inc(ik_step, 1)
            dve.wait_ge(kv_ln, 2)
            dve.tensor_tensor(kvt[:, :, :], heads3(psA[:, :]), wide(small[:, 0:8], [P, NT, P]), ALU.mult).then_inc(kv_done, 1)
            dve.wait_ge(kv_done, 1)
            dve.wait_ge(ik_step, 11)
            dve.tensor_scalar(ikd, psA[:, :], col(IW), col(IB), ALU.mult, ALU.add).then_inc(ik_step, 1)
            dve.wait_ge(ik_step, 13)
            dve.tensor_tensor(ikl, ikd, ikh.bitcast(F32), ALU.subtract).then_inc(ik_step, 1)
            key_norm(0, kvt[:, :, 0:HD])
            key_gain(0, DK)
            for v, (t, h) in enumerate(ix_units):
                n = (t + 1) * P
                sc = scores[:, sc_off[t]:sc_off[t] + n]
                dve.wait_ge(ix_relu, v + 1)
                if h == 0:
                    dve.tensor_scalar(sc, tmp[:, v % 2, 0:n], ixw[:, t, h:h + 1], None, ALU.mult).then_inc(ix_acc, 1)
                else:
                    dve.wait_ge(ix_acc, v)
                    dve.scalar_tensor_tensor(out=sc, in0=tmp[:, v % 2, 0:n], scalar=ixw[:, t, h:h + 1], in1=sc,
                                             op0=ALU.mult, op1=ALU.add).then_inc(ix_acc, 1)
            def late(t):
                end = sc_off[t] + (t + 1) * P
                return scores[0:HD, end - HD:end]

            for t in range(TOPK // P):
                dve.memset(scores[:, sc_off[t]:sc_off[t] + (t + 1) * P], 0.0).then_inc(tk_max, 1)
                dve.wait_ge(tk_max, t + 1)
                dve.memset(late(t), NEG).then_inc(masked, 1)
            dve.wait_ge(ix_acc, len(ix_units))
            for i in range((NT - TOPK // P) // 2):
                two = (TOPK // P + i, NT - 1 - i)
                m0 = TOPK // P + 2 * (TOPK // 8) * i
                r0 = (2 + 2 * (TOPK // 8)) * i
                sc = [scores[:, sc_off[t]:sc_off[t] + (t + 1) * P] for t in two]
                for t in two:
                    dve.memset(late(t), BARRED).then_inc(tk_rep, 1)
                with dve.Fori(0, TOPK // 8) as j:
                    for v in range(2):
                        dve.wait_ge(tk_rep, r0 + v + 1 + 2 * j)
                        dve.sem_inc(dve_go, 1)
                        dve.max(m8[:, v, :], sc[v]).then_inc(tk_max, 1)
                    for v in range(2):
                        dve.wait_ge(tk_max, m0 + v + 1 + 2 * j)
                        dve.sem_inc(dve_go, 1)
                        dve.match_replace(out=sc[v], in_to_replace=m8[:, v, :], in_values=sc[v], imm_value=TAKEN)\
                            .then_inc(tk_rep, 1)
                for v in range(2):
                    dve.wait_ge(tk_rep, r0 + v + 1 + 2 * (TOPK // 8))
                    dve.tensor_scalar(sc[v], sc[v], 0.5 * (TAKEN + BARRED), NEG, ALU.is_gt, ALU.mult).then_inc(masked, 1)
            head_norms("q", 0, S, qT, DQ, q_sq, q_rstd, q_done, 1)
            for i in (1, 2):
                dve.wait_ge(free[first["sk"] % 2], first["sk"] // 2 + 1)
                dve.wait_ge(free[first["sv"] % 2], first["sv"] // 2 + 1)
                key_norm(i, heads3(tmp[:, 1, :])[:, :, (i - 1) * HD:i * HD])
                key_gain(i, SK)

            def att_max(q, h, pp, mask, n, swa):
                u = 2 * q + h
                dve.wait_ge(a_s, u + 1 + 2 * pp)
                if u >= 2:
                    dve.wait_ge(a_exp, u - 1 + 2 * pp)
                if swa is not None and u >= 130:
                    dve.wait_ge(a_snk, u - 129)
                dve.sem_inc(dve_go, 1)
                dve.tensor_tensor_reduce(out=tmp[:, h, 0:n], in0=psG[:, h, 0:n], in1=mask, scale=1.0, scalar=TAKEN,
                                         op0=ALU.add, op1=ALU.max, accum_out=stat[:, h, 1:2]).then_inc(a_mx0, 1)
                dve.wait_ge(a_mx0, u + 1 + 2 * pp)
                if swa is None:
                    dve.tensor_scalar(stat[:, h, 0:1], stat[:, h, 1:2], -AT_SCALE, None, ALU.mult).then_inc(a_mx, 1)
                else:
                    dve.tensor_scalar(stat[:, h, 0:1], stat[:, h, 1:2], -AT_SCALE, nsink[:, swa + h:swa + h + 1],
                                      ALU.mult, ALU.min).then_inc(a_mx, 1)

            def att_copy(q, pp, n):
                dve.wait_ge(a_t, 2 * q + 2 + 2 * pp)
                dve.wait_ge(a_pv, 2 * q + 1 + 2 * pp)
                dve.tensor_copy(pT[:, 0:n], psA[:, 0:n]).then_inc(a_cp, 1)

            def att_div(q, pp, swa):
                z = q % 2
                dve.wait_ge(a_pv, 2 * q + 2 + 2 * pp)
                if q >= 2:
                    dve.wait_ge(a_ot, q - 1 + pp)
                if swa:
                    dve.wait_ge(a_snk, 2 * (q - 64) + 2)
                    dve.tensor_tensor(stat[:, z, 4:6], stat[:, z, 4:6], stat[:, z, 6:8], ALU.add).then_inc(a_den, 1)
                    dve.wait_ge(a_den, q - 64 + 1)
                dve.reciprocal(stat[:, z, 2:4], stat[:, z, 4:6]).then_inc(a_ri, 1)
                dve.wait_ge(a_ri, q + 1 + pp)
                dve.tensor_tensor(otok[:, z, :].rearrange("p (h c) -> p h c", h=2),
                                  (psB, psC)[z][:, 0:P].rearrange("p (h c) -> p h c", h=2),
                                  wide(stat[:, z, 2:4], [P, 2, HD]), ALU.mult).then_inc(a_o, 1)

            def attention(kind, q0):
                def nk(t):
                    return P * (t + 1 if kind == "dsa" else min(t + 1, 2))

                def mask(t):
                    if kind == "dsa":
                        return scores[:, sc_off[t]:sc_off[t] + nk(t)]
                    return swm[:, 2 * P - nk(t):2 * P]

                def sink(p):
                    return 2 * p if kind == "swa" else None

                def pair(q, pp, t, p, before, after):
                    att_max(q, 1, pp, mask(t), nk(t), sink(p))
                    if before is not None:
                        att_div(q - 1, pp, kind == "swa")
                    if after is not None:
                        att_max(q + 1, 0, pp, mask(after[0]), nk(after[0]), sink(after[1]))
                    att_copy(q, pp, nk(t))

                att_max(q0, 0, 0, mask(0), nk(0), sink(0))
                for t in range(NT):
                    q = q0 + PAIRS * t
                    pair(q, 0, t, 0, (t - 1, PAIRS - 1) if t else None, (t, 1))
                    if kind == "dsa" and t:
                        with dve.Fori(0, PAIRS // 2 - 1) as j:
                            for u in (1, 2):
                                pair(q + u, 2 * j, t, u, (t, u - 1), (t, u + 1))
                    else:
                        for p in range(1, PAIRS - 1):
                            pair(q + p, 0, t, p, (t, p - 1), (t, p + 1))
                    pair(q + PAIRS - 1, 0, t, PAIRS - 1, (t, PAIRS - 2), (t + 1, 0) if t < NT - 1 else None)
                att_div(q0 + NT * PAIRS - 1, 0, kind == "swa")

            attention("dsa", 0)
            head_norms("sq", KT, S, qT, SQ, q_sq, q_rstd, q_done, 1)
            attention("swa", 64)
            dve.wait_ge(free[first["dt"] % 2], first["dt"] // 2 + 1)
            dve.tensor_tensor(dts[:, 1, :, :], dts[:, 0, :, :], dtb[:, :].unsqueeze(1).to_broadcast([P, NT, HEADS]), ALU.add)\
                .then_inc(dt_step, 1)
            dve.wait_ge(dt_step, 1)
            dve.scalar_tensor_tensor(out=dts[:, 2, :, :], in0=dts[:, 1, :, :], scalar=-1.0, in1=dts[:, 1, :, :],
                                     op0=ALU.mult, op1=ALU.max).then_inc(dt_step, 1)
            dve.wait_ge(dt_step, 4)
            dve.scalar_tensor_tensor(out=dts[:, 0, :, :], in0=dts[:, 1, :, :], scalar=0.0, in1=dts[:, 2, :, :],
                                     op0=ALU.max, op1=ALU.add).then_inc(dt_step, 1)
            dve.wait_ge(dt_step, 5)
            dve.wait_ge(s_alog, 2)
            dve.tensor_tensor(dts[:, 3, :, :], dts[:, 0, :, :], alog[:, :].unsqueeze(1).to_broadcast([P, NT, HEADS]), ALU.mult)\
                .then_inc(dt_step, 1)
            def convolve(j):
                for u in range(2):
                    i = first["xbc"] + u
                    k = u + 2 * j
                    ps, acc = psG[:, i % 2, :], tmp[:, u, :]
                    dve.wait_ge(mm, i + 1 + 2 * j)
                    if not isinstance(j, int):
                        dve.wait_ge(cv_out, u - 1 + 2 * j)
                    dve.tensor_scalar(acc, ps, pcol[:, bass.ds(CW + (CONV - 1) * XC + k, 1)], pcol[:, bass.ds(CB + k, 1)],
                                      ALU.mult, ALU.add).then_inc(cv_acc, 1)
                    for tap in range(CONV - 2, -1, -1):
                        back = CONV - 1 - tap
                        dve.wait_ge(cv_acc, 3 * u + back + 6 * j)
                        ins = dve.scalar_tensor_tensor(out=acc[:, back:], in0=ps[:, 0:S - back],
                                                       scalar=pcol[:, bass.ds(CW + tap * XC + k, 1)], in1=acc[:, back:],
                                                       op0=ALU.mult, op1=ALU.add)
                        ins.then_inc(cv_acc if tap else free[i % 2], 1)

            convolve(0)
            with dve.Fori(1, XC // 2) as j:
                convolve(j)
            dve.wait_ge(dt_step, 7)
            dve.tensor_copy(dts[:, 4, :, :], psB[:, 0:P].rearrange("p (t h) -> p t h", t=NT)).then_inc(dt_step, 1)
            dve.wait_ge(dt_step, 8)
            dve.tensor_tensor(dts[:, 7, :, :], psB[:, P:2 * P].rearrange("p (t h) -> p t h", t=NT), dts[:, 4, :, :], ALU.subtract)\
                .then_inc(dt_step, 1)
            dve.wait_ge(dt_step, 12)
            dve.tensor_tensor(dts[:, 7, :, :], dts[:, 7, :, :], dts[:, 0, :, :], ALU.mult).then_inc(dt_step, 1)
            dve.wait_ge(cv_out, XC)
            dve.wait_ge(dt_step, 13)
            for c in range(NT):
                def by_head(i, h0=0, h1=HEADS):
                    return wide(dts[:, i, c, h0:h1], [P, h1 - h0, HD])

                dve.wait_ge(s_xtok, c + 1)
                dve.tensor_tensor(heads3(xdt[:, :], HEADS), heads3(xtok[:, :], HEADS), by_head(0), ALU.mult).then_inc(s_xdt, 1)
                if c:
                    dve.wait_ge(s_upd, 2 * c)
                dve.tensor_tensor(heads3(xw[:, :], HEADS), heads3(xtok[:, :], HEADS), by_head(7), ALU.mult).then_inc(s_xw, 1)
                dve.wait_ge(s_bt, c + 1)
                dve.tensor_copy(btok[:, :], psA[:, 0:2 * STATE]).then_inc(s_btok, 1)

                def differences(q):
                    n = 4 * c + q
                    dve.wait_ge(s_bc, n + 1)
                    if n >= 2:
                        dve.wait_ge(s_e, n - 1)
                    dve.tensor_tensor(tmp[:, n % 2, 0:512].rearrange("p (h l) -> p h l", h=4),
                                      (psB, psC)[n % 2][:, :].rearrange("p (h l) -> p h l", h=4),
                                      wide(dts[:, 4, c, 4 * q:4 * q + 4], [P, 4, P]), ALU.subtract).then_inc(s_df, 1)

                def weigh(q):
                    n = 4 * c + q
                    dve.wait_ge(s_e, n + 1)
                    if n >= 2:
                        dve.wait_ge(s_yd, n - 1)
                    if q == 0:
                        dve.wait_ge(s_g, c + 1)
                    g = 512 + (q // 2) * P
                    dve.tensor_tensor(sqb[:, n % 2, 512:1024].rearrange("p (h l) -> p h l", h=4),
                                      sqb[:, n % 2, 0:512].rearrange("p (h l) -> p h l", h=4),
                                      psA[:, g:g + P].unsqueeze(1).to_broadcast([P, 4, P]), ALU.mult).then_inc(s_m, 1)

                differences(0)
                differences(1)
                weigh(0)
                differences(2)
                weigh(1)
                differences(3)
                weigh(2)
                weigh(3)
                if c:
                    dve.wait_ge(s_ytr, c)
                    dve.wait_ge(s_yo, c)
                    dve.tensor_tensor(heads3(yt[:, :], HEADS), heads3(psG[:, 1, :], HEADS), by_head(6), ALU.mult).then_inc(s_off, 1)
                    dve.wait_ge(s_off, c)
                    dve.wait_ge(s_yd, 4 * c + 4)
                    dve.tensor_tensor(yt[:, :], yt[:, :], psG[:, 0, :], ALU.add).then_inc(s_y, 1)
                else:
                    dve.wait_ge(s_yd, 4)
                    dve.wait_ge(s_ztok, 1)
                    dve.tensor_copy(yt[:, :], psG[:, 0, :]).then_inc(s_y, 1)
                if c < NT - 1:
                    for g in range(GROUPS):
                        sg = st[:, g * 512:(g + 1) * 512]
                        if c:
                            dve.tensor_tensor(heads3(sg, 8), heads3(sg, 8), by_head(5, 8 * g, 8 * g + 8), ALU.mult).then_inc(s_dec, 1)
                            dve.wait_ge(s_dec, 2 * c - 1 + g)
                        dve.wait_ge(s_upd, 2 * c + g + 1)
                        if c:
                            dve.tensor_tensor(sg, sg, psA[:, 0:512], ALU.add).then_inc(s_stt, 1)
                        else:
                            dve.tensor_copy(sg, psA[:, 0:512]).then_inc(s_stt, 1)
                dve.wait_ge(s_yp, 3 * c + 3)
                for g in range(GROUPS):
                    yg = yt[:, g * 512:(g + 1) * 512]
                    if c and g == 0:
                        dve.wait_ge(s_yst, 16 * c)
                    dve.tensor_tensor_reduce(out=rst[:, g * 512:(g + 1) * 512], in0=yg, in1=yg, scale=1.0, scalar=0.0,
                                             op0=ALU.mult, op1=ALU.add, accum_out=small[:, 32 + g:33 + g]).then_inc(s_ss, 1)
                dve.wait_ge(s_rs, 2 * c + 2)
                for g in range(GROUPS):
                    yg = yt[:, g * 512:(g + 1) * 512]
                    dve.tensor_scalar(yg, yg, small[:, 34 + g:35 + g], None, ALU.mult).then_inc(s_yn, 1)
                dve.wait_ge(s_ytr, c + 1)
                dve.tensor_tensor(heads3(rst[:, :]), heads3(psA[:, :]), wide(pcol[:, SSN:SSN + KT], [P, KT, P]), ALU.mult)\
                    .then_inc(s_ycp, 1)
            turn(1)

            def split_mixer(b):
                for k in range(KT):
                    n = KT * b + k
                    dve.wait_ge(b_hi, n + 1)
                    src = tmp[:, n % 2, :] if b < 3 else merged[:, k, :]
                    dve.tensor_tensor(AL[:, k, :], src, AH[:, k, :].bitcast(F32), ALU.subtract).then_inc(b_lo, 1)

            for b in range(3):
                split_mixer(b)
                for k in range(KT):
                    n = KT * b + k
                    i = first[f"br{b}"] + k
                    dve.wait_ge(g_in[n % 2], 16 * (n // 2 + 1))
                    dve.wait_ge(mm, i + 1)
                    if b == 0:
                        dve.tensor_tensor(merged[:, k, :], psG[:, i % 2, :], sqb[:, n % 2, :], ALU.mult).then_inc(free[i % 2], 1)
                    else:
                        if n > KT:
                            dve.wait_ge(m_add, n - KT)
                        dve.tensor_tensor(rst[:, :], psG[:, i % 2, :], sqb[:, n % 2, :], ALU.mult).then_inc(free[i % 2], 1)
                        dve.wait_ge(free[i % 2], i // 2 + 1)
                        dve.tensor_tensor(merged[:, k, :], merged[:, k, :], rst[:, :], ALU.add).then_inc(m_add, 1)
            dve.wait_ge(m_add, 2 * KT)
            split_mixer(3)

            def residual(name):
                for k in range(KT):
                    i = first[name] + k
                    dve.wait_ge(mm, i + 1)
                    dve.tensor_tensor(xT[:, k, :], psG[:, i % 2, :], xT[:, k, :], ALU.add).then_inc(free[i % 2], 1)
                    if name == "xo" and k >= 2:
                        add_squares(3, k - 1)
                if name == "xo":
                    add_squares(3, KT - 1)

            residual("out")
            turn(2)
            norm(1)
            head_norms("xk", 0, N_MEM, xkT, XKN, xk_sq, xk_rstd, xk_done, 2)
            norm(2)
            head_norms("xq", KT, S, xqT, XQN, xk_sq, xk_rstd, xk_done, 2)
            units = NT * XH
            for w in range(units + 3):
                if 2 <= w <= units + 1:
                    z = w % 2
                    dve.wait_ge(c_exp, w - 1)
                    dve.reciprocal(small[:, 46 + z:47 + z], small[:, 42 + z:43 + z]).then_inc(c_ri, 1)
                if w < units:
                    z = w % 2
                    dve.wait_ge(c_s, w + 1)
                    if w >= 2:
                        dve.wait_ge(c_exp, w - 1)
                    dve.tensor_reduce(small[:, 44 + z:45 + z], psG[:, z, 0:N_MEM], AXX, ALU.max).then_inc(c_mx0, 1)
                    dve.wait_ge(c_mx0, w + 1)
                    dve.tensor_scalar(small[:, 40 + z:41 + z], small[:, 44 + z:45 + z], -XA_SCALE, None, ALU.mult).then_inc(c_mx, 1)
                if 2 <= w <= units + 1:
                    z = w % 2
                    dve.wait_ge(c_ri, w - 1)
                    dve.wait_ge(c_pv, w - 1)
                    if w >= 4:
                        dve.wait_ge(c_ot, w - 3)
                    dve.tensor_scalar(tmp[:, z, 512:768], (psB, psC)[z][:, 0:XD], small[:, 46 + z:47 + z], None, ALU.mult)\
                        .then_inc(c_o, 1)
                if w >= 3:
                    t, h, z = (w - 3) // XH, (w - 3) % XH, (w - 3) % 2
                    a = (slice(None), slice(2 * h, 2 * h + 2), slice(t * P, (t + 1) * P))
                    dve.wait_ge(c_hi, w - 2)
                    dve.tensor_tensor(AL[a], heads3(psG[:, z, 512:768], 2), AH[a].bitcast(F32), ALU.subtract).then_inc(c_lo, 1)
            residual("xo")
            norm(3)
            for c in range(0, FT, FC):
                for k in range(min(FC, FT - c)):
                    n = c + k
                    i = up_tile(n)
                    dve.wait_ge(mm, i + 1)
                    read_out(dve, i - 1)
                    if n >= 2:
                        dve.wait_ge(f_lo, n - 1)
                    dve.tensor_tensor(tmp[:, n % 2, :], psG[:, i % 2, :], sqb[:, n % 2, :], ALU.mult).then_inc(free[i % 2], 1)
                    dve.wait_ge(f_hi, n + 1)
                    dve.tensor_tensor(HL[:, k, :], tmp[:, n % 2, :], HH[:, k, :].bitcast(F32), ALU.subtract).then_inc(f_lo, 1)
                residual(f"dn{c}")


NAMES = ["x", "mem", "norm_mix", "w_in", "dsa_kv_norm", "dsa_w_ukv", "dsa_q_norm", "dsa_k_norm", "idx_k_ln_w", "idx_k_ln_b",
         "swa_q_norm", "swa_k_norm", "swa_sinks", "ssm_conv_w", "ssm_conv_b", "ssm_dt_bias", "ssm_a_log", "ssm_d",
         "ssm_norm", "w_br_dsa", "w_br_swa", "w_br_ssm", "w_out", "norm_xa", "norm_mem", "xa_wq", "xa_wkv", "xa_q_norm",
         "xa_k_norm", "xa_wo", "norm_ffn", "ffn_w_gate_up", "ffn_w_down"]


def kernel(**inputs):
    import numpy as np
    import concourse.bacc as bacc
    from concourse.bass_utils import run_bass_kernel_spmd

    nc = bacc.Bacc("TRN2", target_bir_lowering=False, num_devices=1)
    arrays, ap = {}, {}
    for name in NAMES:
        a = np.ascontiguousarray(inputs[name])
        arrays[f"in_{name}"] = a
        ap[name] = nc.dram_tensor(f"in_{name}", a.shape, mybir.dt.from_np(a.dtype), kind="ExternalInput").ap()
    out = nc.dram_tensor("out_x", (1, S, D), F32, kind="ExternalOutput").ap()
    build(nc, ap, out)
    r = run_bass_kernel_spmd(nc, [arrays], core_ids=[0])
    return r.results[0]["out_x"]
```

```python
from contextlib import ExitStack

import concourse.bass as bass
from concourse import mybir

F32 = mybir.dt.float32
F32R = mybir.dt.float32r
ALU = mybir.AluOpType
ACT = mybir.ActivationFunctionType
AXX = mybir.AxisListType.X

P = 128
D = 1024
S = 1024
KT = D // P
NT = S // P
CHUNK = 64
EPS = 1e-6
HD = 64
HEADS = 16
PAIRS = HEADS // 2
KV_RANK = 256
IDX_HEADS = 8
TOPK = 256
GROUPS = 2
STATE = 128
XC = (D + 2 * GROUPS * STATE) // P
CONV = 4
N_MEM = 256
MT = N_MEM // P
XH = 4
XD = D // XH
DFF = 2816
FT = DFF // P
FC = 4
FCH = -(-FT // FC)
PARAMS = 9 + 1 + 12 + 4 + 1
NEG = -1e30
TAKEN = -3e38
BARRED = -1e38
AT_SCALE = HD ** -0.5
XA_SCALE = XD ** -0.5
IDX_SCALE = IDX_HEADS ** -0.5 * HD ** -0.5

C_Q, C_CKV, C_IQ, C_IK = 0, 1024, 1280, 1792
C_SQ, C_SK, C_SV, C_Z, C_XBC, C_DT, C_G = 1864, 2888, 3016, 3144, 4168, 5704, 5720
IKW = HD + IDX_HEADS


def tile_plan():
    plan = [
        ("xk", "xa_wkv", 0, KT, 0, P, 8), ("xv", "xa_wkv", 0, KT, D, P, 8),
        ("ikw", "w_in", 0, KT, C_IK, IKW, 1), ("ckv", "w_in", 0, KT, C_CKV, P, 2), ("iq", "w_in", 0, KT, C_IQ, P, 4),
        ("gate", "w_in", 0, KT, C_G, P, 24),
        ("z", "w_in", 0, KT, C_Z, P, 8), ("q", "w_in", 0, KT, C_Q, P, 8),
        ("sk", "w_in", 0, KT, C_SK, P, 1), ("sv", "w_in", 0, KT, C_SV, P, 1), ("sq", "w_in", 0, KT, C_SQ, P, 8),
        ("dt", "w_in", 0, KT, C_DT, HEADS, 1), ("xbc", "w_in", 0, KT, C_XBC, P, XC),
        ("br0", "w_br_dsa", 0, KT, 0, P, 8), ("br1", "w_br_swa", 0, KT, 0, P, 8), ("br2", "w_br_ssm", 0, KT, 0, P, 8),
        ("out", "w_out", 0, KT, 0, P, 8),
        ("xq", "xa_wq", 0, KT, 0, P, 8),
        ("xo", "xa_wo", 0, KT, 0, P, 8),
    ]
    for c in range(0, FT, FC):
        w = min(FC, FT - c)
        plan.append((f"gu{c}", "ffn_w_gate_up", 0, KT, (c * P, DFF + c * P), P, 2 * w))
        plan.append((f"dn{c}", "ffn_w_down", c, w, 0, P, 8))
    return plan


def build(nc, ap, out):
    plan = tile_plan()
    first = {}
    n = 0
    for name, *_, count in plan:
        first[name] = n
        n += count
    n_tiles = n

    ctx = ExitStack()
    with ctx:
        def sem(name):
            return ctx.enter_context(nc.semaphore(name))

        def sb(name, shape, dt=F32, stack=ctx):
            return stack.enter_context(nc.sbuf_tensor(name, shape, dt))

        def dram(name, shape):
            return nc.dram_tensor(name, shape, F32, kind="Internal").ap()

        gate_d = dram("gate_d", (3 * KT, P, S))
        z_d = dram("z_d", (KT, P, S))
        y_d = dram("y_d", (3, KT, P, S))

        x_d = dram("x_d", (KT, P, S))
        xk_d = dram("xk_d", (P, KT, N_MEM))
        xv_d = dram("xv_d", (P, MT, D))

        AH, AL = sb("AH", [P, KT, S], F32R), sb("AL", [P, KT, S], F32R)
        WH, WL = sb("WH", [P, 2, KT, P], F32R), sb("WL", [P, 2, KT, P], F32R)
        wraw = sb("wraw", [P, 4, KT, P])
        ident, ones, bones = sb("ident", [P, P]), sb("ones", [P, P]), sb("bones", [P, P])
        tri, cmask = sb("tri", [P, P]), sb("cmask", [P, P])
        prow, pcol = sb("prow", [P, P]), sb("pcol", [P, P])
        nsink, dskip = sb("nsink", [P, HEADS]), sb("dskip", [P, HEADS])
        dtb, alog = sb("dtb", [P, HEADS]), sb("alog", [P, HEADS])
        sqb, tmp, rst = sb("sqb", [P, 2, S]), sb("tmp", [P, 2, S]), sb("rst", [P, S])
        small = sb("small", [P, 64])

        g = ExitStack()
        xT0 = sb("xT0", [P, KT, S], F32, g)
        memT = sb("memT", [P, KT, N_MEM], F32, g)
        MH, ML = sb("MH", [P, KT, N_MEM], F32R, g), sb("ML", [P, KT, N_MEM], F32R, g)
        xk0, xv0 = sb("xk0", [P, KT, N_MEM], F32, g), sb("xv0", [P, MT, D], F32, g)
        msq, mtmp, mrst = sb("msq", [P, 2, N_MEM], F32, g), sb("mtmp", [P, 2, N_MEM], F32, g), sb("mrst", [P, N_MEM], F32, g)
        g.close()
        g = ExitStack()
        sc_off = [P * qb * (qb + 1) // 2 for qb in range(NT)]
        scores = sb("scores", [P, P * NT * (NT + 1) // 2], F32, g)
        kh, kl = sb("kh", [P, 3, S], F32R, g), sb("kl", [P, 3, S], F32R, g)
        kvt, svt = sb("kvt", [P, NT, 2 * HD], F32, g), sb("svt", [P, NT, P], F32, g)
        qT = sb("qT", [P, PAIRS, S], F32, g)
        qst = sb("qst", [P, 2, 2, P], F32R, g)
        otok, oT = sb("otok", [P, 2, P], F32, g), sb("oT", [P, 2, P], F32, g)
        swm = sb("swm", [P, 2 * P], F32, g)
        wukv = oT
        m8, ixw = sb("m8", [P, 2, 8], F32, g), sb("ixw", [P, NT, IDX_HEADS], F32, g)
        stat = sb("stat", [P, 2, 8], F32, g)
        g.close()
        iqT, ckvT, ikd = qT[:, 0:4, :], qT[:, 5:7, :], qT[:, 7, :]
        ikh, ikl = kh[:, 1, :], kl[:, 1, :]
        g = ExitStack()
        xcT = sb("xcT", [P, XC, S], F32, g)
        zt, xtok, ztok = sb("zt", [P, KT, P], F32, g), sb("xtok", [P, D], F32, g), sb("ztok", [P, D], F32, g)
        xdt, xw, btok = sb("xdt", [P, D], F32, g), sb("xw", [P, D], F32, g), sb("btok", [P, 2 * STATE], F32, g)
        st = sb("st", [P, D], F32, g)
        yt = sb("yt", [P, D], F32, g)
        dts = sb("dts", [P, 8, NT, HEADS], F32, g)
        g.close()
        g = ExitStack()
        xT = sb("xT", [P, KT, S], F32, g)
        g2 = ExitStack()
        merged = sb("merged", [P, KT, S], F32, g2)
        g2.close()
        g2 = ExitStack()
        xqT = sb("xqT", [P, KT, S], F32, g2)
        xkT, xv = sb("xkT", [P, KT, N_MEM], F32, g2), sb("xv", [P, MT, D], F32, g2)
        g2.close()
        g2 = ExitStack()
        HH, HL = sb("HH", [P, FC, S], F32R, g2), sb("HL", [P, FC, S], F32R, g2)
        g2.close()
        g.close()

        psG = ctx.enter_context(nc.psum_tensor("psG", [P, 2, S], F32))
        psA = ctx.enter_context(nc.psum_tensor("psA", [P, S], F32))
        psB = ctx.enter_context(nc.psum_tensor("psB", [P, 512], F32))
        psC = ctx.enter_context(nc.psum_tensor("psC", [P, 512], F32))


        s_par, s_const, s_pcol, s_alog = sem("s_par"), sem("s_const"), sem("s_pcol"), sem("s_alog")
        x_in = [sem("x_in0"), sem("x_in1")]
        x_tr, x_cp = sem("x_tr"), sem("x_cp")
        n_sq, n_acc, n_sum, n_rstd, n_out, n_hi, n_lo = (sem(f"n_{x}") for x in ("sq", "acc", "sum", "rstd", "out", "hi", "lo"))
        w_in = [sem(f"w_in{i}") for i in range(4)]
        w_hi, w_lo = sem("w_hi"), sem("w_lo")
        mm = sem("mm")
        free = [sem("free0"), sem("free1")]
        ik_step, kv_sq, kv_pe, kv_ln, kv_done, kp_step = (sem(x) for x in ("ik_step", "kv_sq", "kv_pe", "kv_ln", "kv_done", "kp_step"))
        ix_q, ix_pe, ix_relu, ix_acc, tk_max, tk_rep, masked = (sem(x) for x in ("ix_q", "ix_pe", "ix_relu", "ix_acc", "tk_max", "tk_rep", "masked"))
        g_st = [sem("g_st0"), sem("g_st1")]
        q_sq, q_sum, q_ln, q_rstd, q_done = (sem(f"q_{x}") for x in ("sq", "sum", "ln", "rstd", "done"))
        sv_cp = sem("sv_cp")
        a_q, a_s, a_mx0, a_mx, a_exp, a_snk, a_pv, a_den, a_ri, a_o, a_ot, a_oc = (
            sem(f"a_{x}") for x in ("q", "s", "mx0", "mx", "exp", "snk", "pv", "den", "ri", "o", "ot", "oc"))
        a_t, a_cp = [sem("a_t0"), sem("a_t1")], [sem("a_cp0"), sem("a_cp1")]
        y_st = [sem("y_st0"), sem("y_st1")]
        dt_step, acv, cv_acc, cv_out = sem("dt_step"), sem("acv"), sem("cv_acc"), sem("cv_out")
        s_zin, s_xt, s_xdt, s_xtok, s_xw, s_zt, s_ztok, s_bt, s_btok, s_g = (
            sem(f"s_{x}") for x in ("zin", "xt", "xdt", "xtok", "xw", "zt", "ztok", "bt", "btok", "g"))
        s_bc, s_df, s_dm, s_e, s_m, s_yd, s_yo, s_upd, s_dec, s_stt, s_y, s_yp, s_ss, s_rs, s_yn, s_ytr, s_ycp, s_yst = (
            sem(f"s_{x}") for x in ("bc", "df", "dm", "e", "m", "yd", "yo", "upd", "dec", "stt", "y", "yp", "ss", "rs", "yn",
                                    "ytr", "ycp", "yst"))
        g_in = [sem("g_in0"), sem("g_in1")]
        b_in = [sem("b_in0"), sem("b_in1")]
        b_hi, b_lo, m_add = sem("b_hi"), sem("b_lo"), sem("m_add")
        xk_sq, xk_sum, xk_ln, xk_rstd, xk_done = (sem(f"xk_{x}") for x in ("sq", "sum", "ln", "rstd", "done"))
        c_s, c_mx0, c_mx, c_exp, c_t, c_cp, c_pv, c_ri, c_o, c_ot, c_hi, c_lo = (
            sem(f"c_{x}") for x in ("s", "mx0", "mx", "exp", "t", "cp", "pv", "ri", "o", "ot", "hi", "lo"))
        f_hi, f_lo = sem("f_hi"), sem("f_lo")
        o_tr, o_cp, o_st = sem("o_tr"), sem("o_cp"), [sem("o_st0"), sem("o_st1")]
        s_off, m_st, x_back, xkv_back = sem("s_off"), sem("m_st"), sem("x_back"), sem("xkv_back")
        pool_go, dve_go = sem("pool_go"), sem("dve_go")
        block = ctx.enter_context(nc.Block())
        MIX, XA, FFN, MEM, CW, CB, KVN, SSN, XQN, XKN, DQ, DK, SQ, SK, IW, IB = (
            0, 8, 16, 24, 32, 80, 92, 94, 102, 104, 106, 107, 108, 109, 110, 111)

        ix_units = [(t, h) for t in range(TOPK // P, NT) for h in range(IDX_HEADS)]

        def col(i):
            return pcol[:, i:i + 1]

        def heads3(x, n=NT):
            return x.rearrange("p (t c) -> p t c", t=n)

        def read_out(eng, tile):
            eng.wait_ge(free[tile % 2], tile // 2 + 1)

        def all_read_out(eng, tile):
            read_out(eng, tile - 1)
            read_out(eng, tile - 2)

        def nk(kind, t):
            return P * (t + 1 if kind == "dsa" else min(t + 1, 2))

        def long(kind, t):
            return kind == "dsa" and (t + 1) * P > 512

        def turns_of(kind, q, h, t, nb):
            pairs, short = NT * PAIRS, 512 // P * PAIRS
            if long(kind, t):
                n = short + 2 * (q - short) + h
                return [(0, 0, 4, n), (1, 4, nb, n)]
            return [(h, 0, nb, q if kind == "dsa" else 2 * pairs - short + q - pairs)]

        def up_tile(n):
            return first[f"gu{n // FC * FC}"] + 2 * (n % FC) + 1

        def wide(x, shape):
            return x.unsqueeze(len(shape) - 1).to_broadcast(shape)

        w_dram = {k: ap[k][0].rearrange("(k p) n -> p k n", p=P)
                  for k in ("w_in", "w_br_dsa", "w_br_swa", "w_br_ssm", "w_out", "xa_wkv", "xa_wq", "xa_wo",
                            "ffn_w_gate_up", "ffn_w_down")}
        x_rows = ap["x"][0].rearrange("(t p) d -> t p d", p=P)
        mem_rows = ap["mem"][0].rearrange("(t p) d -> t p d", p=P)
        out_rows = out[0].rearrange("(t p) d -> t p d", p=P)
        turns = [(mem_rows, MT, memT), (x_rows, NT, xT0)]
        turn_first = [0, MT]
        norms = [(memT, MEM, N_MEM, msq, mrst, mtmp, MH, ML)] + [
            (src, gain, S, sqb, rst, tmp, AH, AL) for src, gain in ((xT0, MIX), (xT, XA), (xT, FFN))]

        @block.sync
        def _(sp):
            def turn(i):
                src, tiles, _ = turns[i]
                for t in range(tiles):
                    q = turn_first[i] + t
                    if q >= 2:
                        sp.wait_ge(x_tr, q - 1)
                    sp.dma_start(tmp[:, q % 2, :], src[t]).then_inc(x_in[q % 2], 16)

            def weight_tiles(name, lo, hi):
                _, w, k0, kn, c0, width, count = next(x for x in plan if x[0] == name)
                t0 = first[name]

                def one(u, j):
                    slot = (t0 + u) % 4
                    if t0 + u >= 4:
                        sp.wait_ge(w_lo, t0 + u - 3 + 4 * j)
                    if isinstance(c0, tuple):
                        c = c0[u % 2] + P * (u // 2) + 2 * P * j
                    else:
                        c = c0 + P * u + 4 * P * j
                    sp.dma_start(wraw[:, slot, 0:kn, 0:width], w_dram[w][:, k0:k0 + kn, bass.ds(c, width)])\
                        .then_inc(w_in[slot], 16)

                if hi is not None:
                    for u in range(lo, hi):
                        one(u, 0)
                elif count % 4 == 0 and count > 4:
                    for u in range(4):
                        one(u, 0)
                    with sp.Fori(0, count // 4 - 1) as j:
                        for u in range(4, 8):
                            one(u, j)
                else:
                    for u in range(count):
                        one(u, 0)

            def weights(name):
                weight_tiles(name, 0, None)

            sp.wait_ge(s_const, 1)
            for key, at in (("norm_mix", MIX), ("norm_xa", XA), ("norm_ffn", FFN), ("norm_mem", MEM),
                            ("ssm_conv_b", CB), ("dsa_kv_norm", KVN), ("ssm_norm", SSN), ("xa_q_norm", XQN),
                            ("xa_k_norm", XKN)):
                rows = ap[key][0].rearrange("(r c) -> r c", c=P)
                sp.dma_start(prow[at:at + rows.shape[0], :], rows).then_inc(s_par, 16)
            sp.dma_start(prow[CW:CW + CONV * XC, :], ap["ssm_conv_w"][0].rearrange("j (r c) -> (j r) c", c=P))\
                .then_inc(s_par, 16)
            for key, at in (("dsa_q_norm", DQ), ("dsa_k_norm", DK), ("swa_q_norm", SQ), ("swa_k_norm", SK),
                            ("idx_k_ln_w", IW), ("idx_k_ln_b", IB)):
                for half in range(2):
                    sp.dma_start(prow[at:at + 1, half * HD:(half + 1) * HD], ap[key]).then_inc(s_par, 16)
            for key, dst in (("swa_sinks", nsink), ("ssm_d", dskip), ("ssm_dt_bias", dtb), ("ssm_a_log", alog)):
                sp.dma_start(dst[:, :], ap[key][0].partition_broadcast(P)).then_inc(s_par, 16)
            sp.dma_start(wukv[:, :, :], ap["dsa_w_ukv"][0].rearrange("(k p) n -> p k n", p=P)).then_inc(s_par, 16)
            turn(0)
            weight_tiles("xk", 0, 4)
            turn(1)
            weight_tiles("xk", 4, 8)
            sp.wait_ge(x_cp, MT + NT)
            sp.dma_start(x_d.rearrange("k p s -> p k s"), xT0[:, :, :]).then_inc(m_st, 16)
            weights("xv")
            weights("ikw")
            weights("ckv")
            weights("iq")
            weights("gate")
            weights("z")
            weights("q")
            weights("sk")
            weights("sv")
            weights("sq")
            weights("dt")
            weights("xbc")
            for c in range(NT):
                if c == 0:
                    for i in range(2):
                        sp.wait_ge(g_st[i], 16 * 16)
                else:
                    sp.wait_ge(s_zt, c)
                sp.dma_start(zt[:, :, :], z_d[:, :, c * P:(c + 1) * P].rearrange("k p s -> p k s"))\
                    .then_inc(s_zin, 16)
            weight_tiles("br0", 0, 4)
            for i in range(2):
                sp.wait_ge(y_st[i], 16 * 64)
            sp.wait_ge(s_yst, 16 * NT)
            sp.dma_start(xT[:, :, :], x_d.rearrange("k p s -> p k s")).then_inc(x_back, 16)
            for b in range(3):
                for k in range(KT):
                    n = KT * b + k
                    if n >= 2:
                        sp.wait_ge(b_lo, n - 1)
                    sp.dma_start(tmp[:, n % 2, :], y_d[b, k]).then_inc(b_in[n % 2], 16)
                for k in range(KT):
                    n = KT * b + k
                    if n >= 2:
                        read_out(sp, first[f"br{b}"] + k - 2)
                    sp.dma_start(sqb[:, n % 2, :], gate_d[n]).then_inc(g_in[n % 2], 16)
                    if k < 4:
                        weight_tiles(f"br{b}", k + 4, k + 5)
                    elif b < 2:
                        weight_tiles(f"br{b + 1}", k - 4, k - 3)
            sp.dma_start(xkT[:, :, :], xk_d).then_inc(xkv_back, 16)
            sp.dma_start(xv[:, :, :], xv_d).then_inc(xkv_back, 16)
            weights("out")
            weights("xq")
            weights("xo")
            for c in range(0, FT, FC):
                weights(f"gu{c}")
                weights(f"dn{c}")
            for t in range(NT):
                sp.wait_ge(o_cp, t + 1)
                sp.dma_start(out_rows[t], sqb[:, t % 2, :]).then_inc(o_st[t % 2], 16)
            for i in range(2):
                sp.wait_ge(o_st[i], 16 * NT // 2)

        @block.gpsimd
        def _(pool):
            pool.memset(prow[:, :], 0.0).then_inc(s_const, 1)
            pool.memset(ident[:, :], 0.0).then_inc(s_const, 1)
            pool.memset(ones[:, :], 1.0).then_inc(s_const, 1)
            pool.memset(bones[:, :], 0.0).then_inc(s_const, 1)
            pool.memset(cmask[:, :], 0.0).then_inc(s_const, 1)
            pool.wait_ge(s_const, 5)
            pool.affine_select(out=ident[:, :], in_=ident[:, :], compare_op=ALU.not_equal, fill=1.0, base=0,
                               pattern=[[-1, P]], channel_multiplier=1).then_inc(s_const, 1)
            pool.affine_select(out=tri[:, :], in_=ones[:, :], compare_op=ALU.is_ge, fill=0.0, base=0,
                               pattern=[[1, P]], channel_multiplier=-1).then_inc(s_const, 1)
            pool.affine_select(out=cmask[:, :], in_=cmask[:, :], compare_op=ALU.is_ge, fill=NEG, base=0,
                               pattern=[[1, P]], channel_multiplier=-1).then_inc(s_const, 1)
            for i in range(2):
                pool.wait_ge(s_const, 8 + i)
                pool.memset(bones[i * HD:(i + 1) * HD, i * HD:(i + 1) * HD], 1.0).then_inc(s_const, 1)

            def split(name):
                _, w, k0, kn, c0, width, count = next(x for x in plan if x[0] == name)
                t0 = first[name]

                def one(u, j):
                    raw, two = (t0 + u) % 4, (t0 + u) % 2
                    src = wraw[:, raw, 0:kn, 0:width]
                    hi, lo = WH[:, two, 0:kn, 0:width], WL[:, two, 0:kn, 0:width]
                    if t0 + u >= 2:
                        pool.wait_ge(mm, t0 + u - 1 + 4 * j)
                    pool.wait_ge(w_in[raw], 16 * ((t0 + u) // 4 + 1 + j))
                    pool.sem_inc(pool_go, 1)
                    pool.tensor_copy(hi, src).then_inc(w_hi, 1)
                    pool.wait_ge(w_hi, t0 + u + 1 + 4 * j)
                    pool.tensor_tensor(lo, src, hi.bitcast(F32), ALU.subtract).then_inc(w_lo, 1)

                if count % 4 == 0 and count > 4:
                    for u in range(4):
                        one(u, 0)
                    with pool.Fori(0, count // 4 - 1) as j:
                        for u in range(4, 8):
                            one(u, j)
                else:
                    for u in range(count):
                        one(u, 0)

            def stage(n, src, staged):
                pool.tensor_copy(qst[:, n % 2, :, :], src.unsqueeze(1).to_broadcast([P, 2, P])).then_inc(staged, 1)
                for h in range(2):
                    a, b = slice(h * HD, (h + 1) * HD), slice((1 - h) * HD, (2 - h) * HD)
                    pool.wait_ge(staged, 3 * n + 1 + h)
                    pool.tensor_tensor(qst[b, n % 2, h, :], src[a], qst[a, n % 2, h, :].bitcast(F32), ALU.subtract)\
                        .then_inc(staged, 1)
                pool.wait_ge(staged, 3 * n + 3)

            def stage_indexer():
                for m in range((NT - TOPK // P) * IDX_HEADS // 2):
                    if m == 0:
                        all_read_out(pool, first["gate"])
                    if m >= 2:
                        pool.wait_ge(ix_pe, 2 * m - 2)
                    t, p = TOPK // P + m // (IDX_HEADS // 2), m % (IDX_HEADS // 2)
                    stage(m, iqT[:, p, t * P:(t + 1) * P], ix_q)

            def stage_queries(q0):
                for q in range(q0, q0 + NT * PAIRS):
                    if q == q0:
                        pool.wait_ge(q_done, KT * (q0 // 64 + 1))
                    if q >= 2:
                        pool.wait_ge(a_s, 2 * q - 2)
                    t, p = (q - q0) // PAIRS, q % PAIRS
                    stage(q, qT[:, p, t * P:(t + 1) * P], a_q)

            pool.wait_ge(s_const, 10)
            for name in ("xk", "xv", "ikw", "ckv", "iq"):
                split(name)
            stage_indexer()
            for name in ("gate", "z", "q", "sk", "sv"):
                split(name)
            stage_queries(0)
            split("sq")
            stage_queries(64)
            for name in ("dt", "xbc"):
                split(name)
            for c in range(NT):
                for q in range(4):
                    n = 4 * c + q
                    pool.wait_ge(s_df, n + 1)
                    pool.tensor_tensor(tmp[:, n % 2, 512:1024].rearrange("p (h l) -> p h l", h=4),
                                       tmp[:, n % 2, 0:512].rearrange("p (h l) -> p h l", h=4),
                                       cmask[:, :].unsqueeze(1).to_broadcast([P, 4, P]), ALU.add).then_inc(s_dm, 1)
                pool.wait_ge(s_xw, c + 1)
                pool.tensor_tensor(heads3(xtok[:, :], HEADS), heads3(xtok[:, :], HEADS),
                                   wide(dskip[:, :], [P, HEADS, HD]), ALU.mult).then_inc(s_yp, 1)
                pool.wait_ge(s_y, c + 1)
                pool.wait_ge(s_yp, 3 * c + 1)
                pool.tensor_tensor(yt[:, :], yt[:, :], xtok[:, :], ALU.add).then_inc(s_yp, 1)
                pool.wait_ge(s_yp, 3 * c + 2)
                pool.wait_ge(s_ztok, c + 1)
                pool.tensor_tensor(yt[:, :], yt[:, :], ztok[:, :], ALU.mult).then_inc(s_yp, 1)
            for name in ("br0", "br1", "br2", "out", "xq", "xo"):
                split(name)
            for c in range(0, FT, FC):
                split(f"gu{c}")
                split(f"dn{c}")

        @block.tensor
        def _(pe):
            def turn(i):
                _, tiles, _ = turns[i]
                for t in range(tiles):
                    q = turn_first[i] + t
                    pe.wait_ge(x_in[q % 2], 16 * (q // 2 + 1))
                    if q:
                        pe.wait_ge(x_cp, q)
                    for k in range(KT):
                        last = nc.tensor.transpose(psA[:, k * P:(k + 1) * P], tmp[:, q % 2, k * P:(k + 1) * P], ident[:, :])
                    last.then_inc(x_tr, 1)

            def halves(n):
                return [(h, min(h + 512, n)) for h in range(0, n, 512)]

            def norm(i):
                n, acc = norms[i][2], norms[i][4]
                pe.wait_ge(n_acc, (KT - 1) * (i + 1))
                for a, b in halves(n):
                    last = nc.tensor.matmul(psA[:, a:b], ones[:, :], acc[:, a:b], start=True, stop=True)
                last.then_inc(n_sum, 1)

            def channel_tile(i, j, hi=AH, lo=AL, kn=KT, n=S, ready=None):
                w = i % 2
                pe.wait_ge(w_lo, i + 1 + 2 * j)
                if i >= 2:
                    pe.wait_ge(free[w], i // 2 + j)
                for a, b in halves(n):
                    for k in range(kn):
                        if ready is not None and a == 0:
                            pe.wait_ge(ready[0], ready[1] + k + 1)
                        for x, (l, r) in enumerate(((WH, hi), (WH, lo), (WL, hi))):
                            last = nc.tensor.matmul(psG[:, w, a:b], l[:, w, k, :], r[:, k, a:b],
                                                    start=(k == 0 and x == 0), stop=(k == kn - 1 and x == 2))
                last.then_inc(mm, 1)

            def token_tiles(i, width, tiles=NT, hi=AH, lo=AL):
                w = i % 2
                pe.wait_ge(w_lo, i + 1)
                if i >= 2:
                    pe.wait_ge(free[w], i // 2)
                for t in range(tiles):
                    for k in range(KT):
                        for x, (l, r) in enumerate(((hi, WH), (lo, WH), (hi, WL))):
                            last = nc.tensor.matmul(psG[:, w, t * P:t * P + width], l[:, k, t * P:(t + 1) * P], r[:, w, k, 0:width],
                                                    start=(k == 0 and x == 0), stop=(k == KT - 1 and x == 2))
                last.then_inc(mm, 1)

            def gemm(name, ready=None, **kw):
                count = next(x for x in plan if x[0] == name)[-1]
                t0 = first[name]
                channel_tile(t0, 0, ready=ready, **kw)
                channel_tile(t0 + 1, 0, **kw)
                if count > 2:
                    with pe.Fori(0, count // 2 - 1) as j:
                        for u in (2, 3):
                            channel_tile(t0 + u, j, **kw)

            def key_prep(i):
                pe.wait_ge(kp_step, 10 * i + 6)
                for t in range(NT):
                    last = nc.tensor.transpose(psA[:, t * P:(t + 1) * P], rst[:, t * P:(t + 1) * P], ident[:, :])
                last.then_inc(kp_step, 1)

            def normed(name, i0, n, over, sq, ssum, ln, tiles_each, squares=sqb, ready=None, **kw):
                t0 = first[name]

                def sums(u, j):
                    pe.wait_ge(sq, i0 + u + 1 + 2 * j)
                    if u % tiles_each == 0 and i0 + u >= tiles_each:
                        pe.wait_ge(ln, (i0 + u) // tiles_each + j * (2 // tiles_each))
                    for a, b in halves(n):
                        last = nc.tensor.matmul(psA[:, a:b], over[:, :], squares[:, u % 2, a:b], start=(u % tiles_each == 0),
                                                stop=(u % tiles_each == tiles_each - 1))
                    last.then_inc(ssum, 1)

                def step(u, j):
                    channel_tile(t0 + u, j, n=n, **kw)
                    sums(u - 1, j)

                channel_tile(t0, 0, n=n, ready=ready, **kw)
                step(1, 0)
                step(2, 0)
                with pe.Fori(0, KT // 2 - 2) as j:
                    step(3, j)
                    step(4, j)
                channel_tile(t0 + KT - 1, 0, n=n, **kw)
                sums(KT - 2, 0)
                sums(KT - 1, 0)

            def keys(q, kind, t):
                return (0, t + 1) if kind == "dsa" else (max(0, t - 1), min(t + 1, 2))

            def products(dst, slot, h, hi, lo):
                r = slice(h * HD, (h + 1) * HD)
                for a, b in halves(hi.shape[1]):
                    nc.tensor.matmul(dst[:, a:b], qst[:, slot, h, :], hi[:, a:b], start=True, stop=False)
                    last = nc.tensor.matmul(dst[:, a:b], qst[r, slot, h, :], lo[r, a:b], start=False, stop=True)
                return last

            def att_scores(q, h, pp, kind, t, p, first_static):
                k0, nb = keys(q, kind, t)
                pe.wait_ge(a_q, 3 * (q + 1) + 3 * pp)
                if first_static >= 2:
                    pe.wait_ge(a_mx0, 2 * q + h - 1 + 2 * pp)
                i = 0 if kind == "dsa" else 1 + p // (PAIRS // 2)
                products(psG[:, h, 0:nb * P], q % 2, h, kh[:, i, k0 * P:(k0 + nb) * P], kl[:, i, k0 * P:(k0 + nb) * P]).then_inc(a_s, 1)

            def att_turn(q, h, pp, kind, t):
                pe.wait_ge(a_exp, 2 * q + h + 1 + 2 * pp)
                for bank, b0, b1, n in turns_of(kind, q, h, t, keys(q, kind, t)[1]):
                    if n:
                        pe.wait_ge(a_cp[bank], n + (2 if long(kind, t) else 1) * pp)
                    for b in range(b0, b1):
                        last = nc.tensor.transpose(psA[:, bank * 512 + (b - b0) * P:bank * 512 + (b - b0 + 1) * P],
                                                   tmp[:, h, b * P:(b + 1) * P], ident[:, :])
                    last.then_inc(a_t[bank], 1)

            def att_values(q, h, pp, kind, t, p):
                k0, nb = keys(q, kind, t)
                if 2 * q + h >= 4:
                    pe.wait_ge(a_oc, q - 1 + pp)
                o = (psB, psC)[q % 2][:, h * HD:(h + 1) * HD]
                for bank, b0, b1, n in turns_of(kind, q, h, t, nb):
                    pe.wait_ge(a_cp[bank], n + 1 + (2 if long(kind, t) else 1) * pp)
                    for b in range(b0, b1):
                        if kind == "dsa":
                            v = kvt[:, b, HD:2 * HD]
                        else:
                            v = svt[:, k0 + b, (p // 4) * HD:(p // 4 + 1) * HD]
                        last = nc.tensor.matmul(o, sqb[:, h, b * P:(b + 1) * P], v, start=(b == 0), stop=(b == nb - 1))
                last.then_inc(a_pv, 1)

            def att_out(q, pp):
                pe.wait_ge(a_o, q + 1 + pp)
                nc.tensor.transpose((psB, psC)[q % 2][:, P:2 * P], otok[:, q % 2, :], ident[:, :]).then_inc(a_ot, 1)

            def attention(kind, q0):
                def pair(q, pp, t, p, before, after):
                    att_scores(q, 1, pp, kind, t, p, 2 * q + 1)
                    att_turn(q, 0, pp, kind, t)
                    if before is not None:
                        att_values(q - 1, 1, pp, kind, *before)
                    if after is not None:
                        att_scores(q + 1, 0, pp, kind, *after, 2 * q + 2)
                    att_values(q, 0, pp, kind, t, p)
                    att_turn(q, 1, pp, kind, t)
                    if before is not None:
                        att_out(q - 1, pp)

                att_scores(q0, 0, 0, kind, 0, 0, 2 * q0)
                for t in range(NT):
                    q = q0 + PAIRS * t
                    pair(q, 0, t, 0, (t - 1, PAIRS - 1) if t else None, (t, 1))
                    if kind == "dsa" and t:
                        with pe.Fori(0, PAIRS // 2 - 1) as j:
                            for u in (1, 2):
                                pair(q + u, 2 * j, t, u, (t, u - 1), (t, u + 1))
                    else:
                        for p in range(1, PAIRS - 1):
                            pair(q + p, 0, t, p, (t, p - 1), (t, p + 1))
                    pair(q + PAIRS - 1, 0, t, PAIRS - 1, (t, PAIRS - 2), (t + 1, 0) if t < NT - 1 else None)
                q = q0 + NT * PAIRS - 1
                att_values(q, 1, 0, kind, NT - 1, PAIRS - 1)
                att_out(q, 0)

            pe.wait_ge(s_const, 10)
            pe.wait_ge(s_par, 16 * PARAMS)
            nc.tensor.transpose(psB[:, 0:P], prow[:, :], ident[:, :]).then_inc(s_pcol, 1)
            turn(0)
            pe.wait_ge(x_cp, MT)
            norm(0)
            pe.wait_ge(n_rstd, 1)
            turn(1)
            pe.wait_ge(x_cp, MT + NT)
            normed("xk", 0, N_MEM, ones, xk_sq, xk_sum, xk_ln, 2, squares=msq, ready=(n_lo, 0), hi=MH, lo=ML)
            pe.wait_ge(xk_ln, XH)
            norm(1)
            for i in range(KT):
                token_tiles(first["xv"] + i, P, MT, MH, ML)
            pe.wait_ge(n_lo, 2 * KT)
            token_tiles(first["ikw"], IKW)
            gemm("ckv")
            gemm("iq")
            all_read_out(pe, first["iq"])
            for t in range(NT):
                for k in range(2):
                    nc.tensor.matmul(psB[:, t:t + 1], sqb[:, k, t * P:(t + 1) * P], ones[:, 0:1], start=(k == 0), stop=(k == 1))
            for t in range(NT):
                for k in range(2):
                    last = nc.tensor.matmul(psA[:, t * P:(t + 1) * P], ckvT[:, k, t * P:(t + 1) * P], wukv[:, k, :],
                                            start=(k == 0), stop=(k == 1))
            last.then_inc(kv_pe, 1)
            pe.wait_ge(ik_step, 10)
            pe.wait_ge(kv_done, 1)
            for t in range(NT):
                last = nc.tensor.transpose(psA[:, t * P:(t + 1) * P], ikd[:, t * P:(t + 1) * P], ident[:, :])
            last.then_inc(ik_step, 1)
            key_prep(0)
            pe.wait_ge(ik_step, 14)
            all_read_out(pe, first["gate"])
            for v, (t, h) in enumerate(ix_units):
                if v >= 2:
                    pe.wait_ge(ix_relu, v - 1)
                pe.wait_ge(ix_q, 3 * (v // 2 + 1))
                n = (t + 1) * P
                products(psG[:, v % 2, 0:n], v // 2 % 2, h % 2, ikh[:, 0:n], ikl[:, 0:n]).then_inc(ix_pe, 1)
            pe.wait_ge(ix_relu, len(ix_units))
            gemm("gate")
            gemm("z")
            normed("q", 0, S, bones, q_sq, q_sum, q_ln, 1)
            token_tiles(first["sk"], P)
            token_tiles(first["sv"], P)
            pe.wait_ge(q_ln, KT)
            key_prep(1)
            key_prep(2)
            all_read_out(pe, first["sq"])
            pe.wait_ge(kp_step, 30)
            attention("dsa", 0)
            pe.wait_ge(a_mx0, 128)
            normed("sq", KT, S, bones, q_sq, q_sum, q_ln, 1)
            all_read_out(pe, first["dt"])
            pe.wait_ge(q_ln, 2 * KT)
            attention("swa", 64)
            pe.wait_ge(a_mx0, 256)
            token_tiles(first["dt"], HEADS)
            gemm("xbc")
            pe.wait_ge(dt_step, 6)
            pe.wait_ge(a_o, 128)
            a_all = dts[:, 3, :, :].rearrange("p t h -> p (t h)")
            nc.tensor.matmul(psB[:, 0:P], tri[:, :], a_all, start=True, stop=True)
            nc.tensor.matmul(psB[:, P:2 * P], ones[:, :], a_all, start=True, stop=True).then_inc(dt_step, 1)
            pe.wait_ge(cv_out, XC)
            pe.wait_ge(dt_step, 13)
            pe.wait_ge(a_oc, 128)
            all_read_out(pe, first["br0"])
            for c in range(NT):
                cc = slice(c * P, (c + 1) * P)
                if c:
                    pe.wait_ge(s_y, c)
                for k in range(KT):
                    last = nc.tensor.transpose(psG[:, 0, k * P:(k + 1) * P], xcT[:, k, cc], ident[:, :])
                last.then_inc(s_xt, 1)
                pe.wait_ge(s_zin, 16 * (c + 1))
                for k in range(KT):
                    last = nc.tensor.transpose(psG[:, 1, k * P:(k + 1) * P], zt[:, k, :], ident[:, :])
                last.then_inc(s_zt, 1)
                if c:
                    pe.wait_ge(s_ycp, c)
                for g in range(GROUPS):
                    last = nc.tensor.transpose(psA[:, g * P:(g + 1) * P], xcT[:, KT + g, cc], ident[:, :])
                last.then_inc(s_bt, 1)
                for g in range(GROUPS):
                    last = nc.tensor.matmul(psA[:, 512 + g * P:512 + (g + 1) * P], xcT[:, KT + g, cc],
                                            xcT[:, KT + GROUPS + g, cc], start=True, stop=True)
                last.then_inc(s_g, 1)

                def decays(q):
                    n = 4 * c + q
                    if n >= 2:
                        pe.wait_ge(s_df, n - 1)
                    bank = (psB, psC)[n % 2]
                    for i in range(4):
                        h = 4 * q + i
                        last = nc.tensor.matmul(bank[:, i * P:(i + 1) * P], dts[:, 3, c, h:h + 1].to_broadcast([P, P]),
                                                tri[:, :], start=True, stop=True)
                    last.then_inc(s_bc, 1)

                def within(q):
                    n = 4 * c + q
                    pe.wait_ge(s_m, n + 1)
                    if q == 0:
                        pe.wait_ge(s_xdt, c + 1)
                        pe.wait_ge(s_xtok, c + 1)
                        pe.wait_ge(s_xw, c + 1)
                    for i in range(4):
                        h = 4 * q + i
                        last = nc.tensor.matmul(psG[:, 0, h * HD:(h + 1) * HD], sqb[:, n % 2, 512 + i * P:512 + (i + 1) * P],
                                                xdt[:, h * HD:(h + 1) * HD], start=True, stop=True)
                    last.then_inc(s_yd, 1)

                decays(0)
                decays(1)
                within(0)
                decays(2)
                within(1)
                decays(3)
                within(2)
                within(3)
                if c:
                    pe.wait_ge(s_ztok, c + 1)
                    pe.wait_ge(s_stt, 2 * c)
                    for g in range(GROUPS):
                        last = nc.tensor.matmul(psG[:, 1, g * 512:(g + 1) * 512], xcT[:, KT + GROUPS + g, cc],
                                                st[:, g * 512:(g + 1) * 512], start=True, stop=True)
                    last.then_inc(s_yo, 1)
                if c < NT - 1:
                    for g in range(GROUPS):
                        if g == 0:
                            pe.wait_ge(s_btok, c + 1)
                        else:
                            pe.wait_ge(s_stt, 2 * c + 1)
                        nc.tensor.matmul(psA[:, 0:512], btok[:, g * P:(g + 1) * P], xw[:, g * 512:(g + 1) * 512],
                                         start=True, stop=True).then_inc(s_upd, 1)
                    pe.wait_ge(s_stt, 2 * c + 2)
                pe.wait_ge(s_btok, c + 1)
                pe.wait_ge(s_yn, 2 * c + 2)
                for k in range(KT):
                    last = nc.tensor.transpose(psA[:, k * P:(k + 1) * P], yt[:, k * P:(k + 1) * P], ident[:, :])
                last.then_inc(s_ytr, 1)
            pe.wait_ge(s_y, NT)
            pe.wait_ge(s_ycp, NT)
            for b in range(3):
                gemm(f"br{b}", ready=(b_lo, KT * b))
            gemm("out", ready=(b_lo, 3 * KT))
            norm(2)
            normed("xq", KT, S, ones, xk_sq, xk_sum, xk_ln, 2, ready=(n_lo, 2 * KT))
            units = NT * XH
            pe.wait_ge(xk_done, 4 * XH)
            pe.wait_ge(xkv_back, 32)
            all_read_out(pe, first["xo"])

            def cross(w):
                return slice((w // XH) * P, (w // XH + 1) * P), w % XH, w % 2

            for w in range(units + 3):
                if w < units:
                    tt, h, z = cross(w)
                    if w >= 2:
                        pe.wait_ge(c_exp, w - 1)
                    for i in range(2):
                        last = nc.tensor.matmul(psG[:, z, 0:N_MEM], xqT[:, 2 * h + i, tt], xkT[:, 2 * h + i, :],
                                                start=(i == 0), stop=(i == 1))
                    last.then_inc(c_s, 1)
                if 1 <= w <= units:
                    tt, h, z = cross(w - 1)
                    pe.wait_ge(c_exp, w)
                    if w >= 3:
                        pe.wait_ge(c_cp, w - 2)
                    for i in range(MT):
                        last = nc.tensor.transpose(psA[:, z * 512 + i * P:z * 512 + (i + 1) * P],
                                                   sqb[:, z, i * P:(i + 1) * P], ident[:, :])
                    last.then_inc(c_t, 1)
                if 2 <= w <= units + 1:
                    tt, h, z = cross(w - 2)
                    pe.wait_ge(c_cp, w - 1)
                    if w >= 4:
                        pe.wait_ge(c_o, w - 3)
                    for i in range(MT):
                        last = nc.tensor.matmul((psB, psC)[z][:, 0:XD], tmp[:, z, i * P:(i + 1) * P],
                                                xv[:, i, h * XD:(h + 1) * XD], start=(i == 0), stop=(i == MT - 1))
                    last.then_inc(c_pv, 1)
                if 3 <= w:
                    tt, h, z = cross(w - 3)
                    pe.wait_ge(c_o, w - 2)
                    if w >= 5:
                        pe.wait_ge(c_lo, w - 4)
                    for i in range(2):
                        last = nc.tensor.transpose(psG[:, z, 512 + i * P:512 + (i + 1) * P],
                                                   tmp[:, z, 512 + i * P:512 + (i + 1) * P], ident[:, :])
                    last.then_inc(c_ot, 1)
            pe.wait_ge(c_lo, units)
            gemm("xo")
            norm(3)
            for c in range(0, FT, FC):
                gemm(f"gu{c}", ready=None if c else (n_lo, 3 * KT))
                gemm(f"dn{c}", ready=(f_lo, c), hi=HH, lo=HL, kn=min(FC, FT - c))
            all_read_out(pe, n_tiles)
            for t in range(NT):
                if t:
                    pe.wait_ge(o_cp, t)
                for k in range(KT):
                    last = nc.tensor.transpose(psA[:, k * P:(k + 1) * P], xT[:, k, t * P:(t + 1) * P], ident[:, :])
                last.then_inc(o_tr, 1)


        @block.scalar
        def _(act):
            def norm_squares(i):
                src, _, n, sq, acc = norms[i][:5]
                if i < 2:
                    act.wait_ge(x_cp, turn_first[i] + turns[i][1])
                for k in range(KT):
                    if i >= 2:
                        read_out(act, first["out" if i == 2 else "xo"] + k)
                    if k >= 3:
                        act.wait_ge(n_acc, (KT - 1) * i + k - 2)
                    act.activation(sq[:, k % 2, 0:n] if k else acc[:, 0:n], src[:, k, 0:n], ACT.Square).then_inc(n_sq, 1)

            def norm_root(i):
                n, acc = norms[i][2], norms[i][4]
                act.wait_ge(n_sum, i + 1)
                act.activation(acc[:, 0:n], psA[:, 0:n], ACT.Ln, scale=1.0 / D, bias=EPS).then_inc(n_rstd, 1)
                act.wait_ge(n_rstd, 2 * i + 1)
                act.activation(acc[:, 0:n], acc[:, 0:n], ACT.Exp, scale=-0.5).then_inc(n_rstd, 1)
                if i >= 2:
                    act.wait_ge(mm, first["xq" if i == 2 else "gu0"])

            def norm_round(i, k):
                n, scaled, hi = norms[i][2], norms[i][5], norms[i][6]
                act.wait_ge(n_out, KT * i + k + 1)
                act.activation(hi[:, k, 0:n], scaled[:, k % 2, 0:n], ACT.Copy).then_inc(n_hi, 1)

            def norm(i):
                norm_squares(i)
                norm_root(i)
                for k in range(KT):
                    norm_round(i, k)

            def stored(name, func, dst, m0):
                t0 = first[name]
                count = next(x for x in plan if x[0] == name)[-1]

                def pair(us, j):
                    for u in us:
                        w, z = (t0 + u) % 2, (m0 + u) % 2
                        act.wait_ge(mm, t0 + u + 1 + 2 * j)
                        if m0 + u >= 2:
                            act.wait_ge(g_st[z], 16 * ((m0 + u) // 2 + j))
                        act.activation(sqb[:, z, :], psG[:, w, :], func).then_inc(free[w], 1)
                        act.wait_ge(free[w], (t0 + u) // 2 + 1 + j)
                        act.dma_start(dst[bass.ds(u + 2 * j, 1)].rearrange("a p s -> (a p) s"), sqb[:, z, :]).then_inc(g_st[z], 16)

                pair((0, 1), 0)
                with act.Fori(0, count // 2 - 1) as j:
                    pair((2, 3), j)

            def head_norms(name, i0, n, sq, ssum, ln, rstd, done, each, scale, squares=sqb, root_of=rst):
                t0 = first[name]

                def square(u, j):
                    act.wait_ge(mm, t0 + u + 1 + 2 * j)
                    if i0 + u >= 2:
                        act.wait_ge(ssum, i0 + u - 1 + 2 * j)
                    act.activation(squares[:, u % 2, 0:n], psG[:, (t0 + u) % 2, 0:n], ACT.Square).then_inc(sq, 1)

                def root(u, j):
                    if u % each != each - 1:
                        return
                    g = (i0 + u) // each
                    gj = j * (2 // each)
                    act.wait_ge(ssum, i0 + u + 1 + 2 * j)
                    if g >= 1:
                        act.wait_ge(done, g * each + gj * each)
                    act.activation(root_of[:, 0:n], psA[:, 0:n], ACT.Ln, scale=scale, bias=EPS).then_inc(ln, 1)
                    act.wait_ge(ln, g + 1 + gj)
                    act.activation(root_of[:, 0:n], root_of[:, 0:n], ACT.Exp, scale=-0.5).then_inc(rstd, 1)

                square(0, 0)
                for u in (1, 2):
                    square(u, 0)
                    root(u - 1, 0)
                with act.Fori(0, KT // 2 - 2) as j:
                    for u in (3, 4):
                        square(u, j)
                        root(u - 1, j)
                square(KT - 1, 0)
                root(KT - 2, 0)
                root(KT - 1, 0)

            def key_root(i):
                act.wait_ge(kp_step, 10 * i + 2)
                act.activation(small[:, 8:16], small[:, 0:8], ACT.Ln, scale=1.0 / HD, bias=EPS).then_inc(kp_step, 1)
                act.wait_ge(kp_step, 10 * i + 3)
                act.activation(small[:, 8:16], small[:, 8:16], ACT.Exp, scale=-0.5).then_inc(kp_step, 1)
                act.wait_ge(kp_step, 10 * i + 8)
                act.activation(kh[:, i, :], rst[:, :], ACT.Copy).then_inc(kp_step, 1)

            nc.scalar.preload_act_table_set("natural_log_exp_and_others")
            act.wait_ge(s_par, 16 * PARAMS)
            act.activation(alog[:, :], alog[:, :], ACT.Exp).then_inc(s_alog, 1)
            norm(0)
            norm_squares(1)
            head_norms("xk", 0, N_MEM, xk_sq, xk_sum, xk_ln, xk_rstd, xk_done, 2, 1.0 / XD, msq, mrst)
            norm_root(1)
            for k in range(KT):
                norm_round(1, k)
                i = first["xv"] + k
                act.wait_ge(mm, i + 1)
                act.activation(xv0[:, :, k * P:(k + 1) * P], heads3(psG[:, i % 2, 0:MT * P], MT), ACT.Copy).then_inc(free[i % 2], 1)
            act.wait_ge(xk_done, KT)
            act.dma_start(xk_d, xk0[:, :, :]).then_inc(m_st, 16)
            all_read_out(act, first["ikw"])
            act.dma_start(xv_d, xv0[:, :, :]).then_inc(m_st, 16)
            i = first["ikw"]
            act.wait_ge(mm, i + 1)
            act.wait_ge(n_lo, 2 * KT)
            act.activation(heads3(tmp[:, 0, :])[:, :, 0:IKW], heads3(psG[:, i % 2, :])[:, :, 0:IKW], ACT.Copy).then_inc(free[i % 2], 1)
            act.wait_ge(m_st, 48)
            for k in range(2):
                act.wait_ge(mm, first["ckv"] + k + 1)
                act.activation(sqb[:, k, :], psG[:, (first["ckv"] + k) % 2, :], ACT.Square).then_inc(kv_sq, 1)
            for k in range(4):
                i = first["iq"] + k
                act.wait_ge(mm, i + 1)
                act.activation(iqT[:, k, :], psG[:, i % 2, :], ACT.Copy).then_inc(free[i % 2], 1)
            act.wait_ge(kv_pe, 1)
            act.activation(small[:, 0:8], psB[:, 0:NT], ACT.Ln, scale=1.0 / KV_RANK, bias=EPS).then_inc(kv_ln, 1)
            act.wait_ge(kv_ln, 1)
            act.activation(small[:, 0:8], small[:, 0:8], ACT.Exp, scale=-0.5).then_inc(kv_ln, 1)
            act.wait_ge(ik_step, 5)
            act.activation(small[:, 24:32], small[:, 16:24], ACT.Ln, scale=1.0 / HD, bias=EPS).then_inc(ik_step, 1)
            act.wait_ge(ik_step, 6)
            act.activation(small[:, 24:32], small[:, 24:32], ACT.Exp, scale=-0.5).then_inc(ik_step, 1)
            act.wait_ge(ik_step, 12)
            act.activation(ikh, ikd, ACT.Copy).then_inc(ik_step, 1)
            key_root(0)
            for v, (t, h) in enumerate(ix_units):
                n = (t + 1) * P
                act.wait_ge(ix_pe, v + 1)
                if v >= 2:
                    act.wait_ge(ix_acc, v - 1)
                else:
                    act.wait_ge(kp_step, 6)
                act.activation(tmp[:, v % 2, 0:n], psG[:, v % 2, 0:n], ACT.Relu).then_inc(ix_relu, 1)
            stored("gate", ACT.Sigmoid, gate_d, 0)
            stored("z", ACT.Silu, z_d, 24)
            for i in range(2):
                act.wait_ge(g_st[i], 16 * 16)
            head_norms("q", 0, S, q_sq, q_sum, q_ln, q_rstd, q_done, 1, 1.0 / HD)
            act.wait_ge(q_done, KT)
            act.wait_ge(mm, first["sk"] + 1)
            act.activation(tmp[:, 1, :], psG[:, first["sk"] % 2, :], ACT.Copy).then_inc(free[first["sk"] % 2], 1)
            act.wait_ge(mm, first["sv"] + 1)
            act.activation(svt[:, :, :], heads3(psG[:, first["sv"] % 2, :]), ACT.Copy).then_inc(free[first["sv"] % 2], 1)
            key_root(1)
            key_root(2)

            def att_exp(q, h, pp, n, swa):
                act.wait_ge(a_mx, 2 * q + h + 1 + 2 * pp)
                act.activation(tmp[:, h, 0:n], tmp[:, h, 0:n], ACT.Exp, bias=stat[:, h, 0:1], scale=AT_SCALE,
                               accum_out=stat[:, q % 2, 4 + h:5 + h]).then_inc(a_exp, 1)
                if swa is not None:
                    act.activation(stat[:, q % 2, 6 + h:7 + h], nsink[:, swa + h:swa + h + 1], ACT.Exp,
                                   bias=stat[:, h, 0:1], scale=-1.0).then_inc(a_snk, 1)

            def att_copy(q, h, pp, kind, t):
                for bank, b0, b1, n in turns_of(kind, q, h, t, nk(kind, t) // P):
                    if bank == 0:
                        act.wait_ge(a_t[0], n + 1 + (2 if long(kind, t) else 1) * pp)
                        if q > 0:
                            act.wait_ge(a_pv, 2 * q + h - 1 + 2 * pp)
                        act.activation(sqb[:, h, b0 * P:b1 * P], psA[:, 0:(b1 - b0) * P], ACT.Copy).then_inc(a_cp[0], 1)

            def att_store(q, pp, b, t, p):
                z = q % 2
                act.wait_ge(a_ot, q + 1 + pp)
                if q >= 2:
                    act.wait_ge(y_st[z], 16 * (q // 2) + 8 * pp)
                act.activation(oT[:, z, :], (psB, psC)[z][:, P:2 * P], ACT.Copy).then_inc(a_oc, 1)
                act.wait_ge(a_oc, q + 1 + pp)
                act.dma_start(y_d[b, bass.ds(p + pp, 1), :, t * P:(t + 1) * P].rearrange("a p s -> (a p) s"), oT[:, z, :])\
                    .then_inc(y_st[z], 16)

            def attention(kind, q0, b):
                def sink(p):
                    return 2 * p if kind == "swa" else None

                def pair(q, pp, t, p, before, after):
                    att_copy(q, 0, pp, kind, t)
                    att_exp(q, 1, pp, nk(kind, t), sink(p))
                    if after is not None:
                        att_exp(q + 1, 0, pp, nk(kind, after[0]), sink(after[1]))
                    att_copy(q, 1, pp, kind, t)
                    if before is not None:
                        att_store(q - 1, pp, b, *before)

                att_exp(q0, 0, 0, nk(kind, 0), sink(0))
                for t in range(NT):
                    q = q0 + PAIRS * t
                    pair(q, 0, t, 0, (t - 1, PAIRS - 1) if t else None, (t, 1))
                    if kind == "dsa" and t:
                        with act.Fori(0, PAIRS // 2 - 1) as j:
                            for u in (1, 2):
                                pair(q + u, 2 * j, t, u, (t, u - 1), (t, u + 1))
                    else:
                        for p in range(1, PAIRS - 1):
                            pair(q + p, 0, t, p, (t, p - 1), (t, p + 1))
                    pair(q + PAIRS - 1, 0, t, PAIRS - 1, (t, PAIRS - 2), (t + 1, 0) if t < NT - 1 else None)
                att_store(q0 + NT * PAIRS - 1, 0, b, NT - 1, PAIRS - 1)

            act.wait_ge(masked, NT)
            attention("dsa", 0, 0)
            head_norms("sq", KT, S, q_sq, q_sum, q_ln, q_rstd, q_done, 1, 1.0 / HD)
            attention("swa", 64, 1)
            for i in range(2):
                act.wait_ge(y_st[i], 16 * 64)
            i = first["dt"]
            act.wait_ge(mm, i + 1)
            act.activation(dts[:, 0, :, :], heads3(psG[:, i % 2, :])[:, :, 0:HEADS], ACT.Copy).then_inc(free[i % 2], 1)
            act.wait_ge(dt_step, 2)
            act.activation(dts[:, 2, :, :], dts[:, 2, :, :], ACT.Exp, scale=-1.0).then_inc(dt_step, 1)
            act.wait_ge(dt_step, 3)
            act.activation(dts[:, 2, :, :], dts[:, 2, :, :], ACT.Ln, bias=1.0).then_inc(dt_step, 1)
            with act.Fori(0, XC // 2) as j:
                for u in range(2):
                    i = first["xbc"] + u
                    act.wait_ge(free[i % 2], i // 2 + 1 + j)
                    act.activation(xcT[:, bass.ds(u + 2 * j, 1), :].rearrange("p a s -> p (a s)"), tmp[:, u, :], ACT.Silu)\
                        .then_inc(cv_out, 1)
            act.wait_ge(dt_step, 9)
            ends = psB[:, P:2 * P].rearrange("p (t h) -> p t h", t=NT)
            act.activation(dts[:, 5, :, :], ends, ACT.Exp).then_inc(dt_step, 1)
            act.wait_ge(dt_step, 10)
            act.activation(dts[:, 6, :, :], dts[:, 4, :, :], ACT.Exp).then_inc(dt_step, 1)
            act.wait_ge(dt_step, 11)
            act.activation(dts[:, 7, :, :], dts[:, 7, :, :], ACT.Exp).then_inc(dt_step, 1)
            for c in range(NT):
                act.wait_ge(s_xt, c + 1)
                if c:
                    act.wait_ge(s_yp, 3 * c)
                act.activation(xtok[:, :], psG[:, 0, :], ACT.Copy).then_inc(s_xtok, 1)
                act.wait_ge(s_zt, c + 1)
                act.activation(ztok[:, :], psG[:, 1, :], ACT.Copy).then_inc(s_ztok, 1)
                for q in range(4):
                    n = 4 * c + q
                    act.wait_ge(s_dm, n + 1)
                    if n >= 2:
                        act.wait_ge(s_m, n - 1)
                    act.activation(sqb[:, n % 2, 0:512], tmp[:, n % 2, 512:1024], ACT.Exp).then_inc(s_e, 1)
                act.wait_ge(s_ss, 2 * c + 2)
                act.activation(small[:, 34:36], small[:, 32:34], ACT.Ln, scale=1.0 / 512, bias=EPS).then_inc(s_rs, 1)
                act.wait_ge(s_rs, 2 * c + 1)
                act.activation(small[:, 34:36], small[:, 34:36], ACT.Exp, scale=-0.5).then_inc(s_rs, 1)
                act.wait_ge(s_ycp, c + 1)
                act.dma_start(y_d[2, :, :, c * P:(c + 1) * P].rearrange("k p s -> p k s"), heads3(rst[:, :])).then_inc(s_yst, 16)
            for b in range(4):
                act.wait_ge(mm, first[("br0", "br1", "br2", "out")[b]])
                for k in range(KT):
                    n = KT * b + k
                    if b < 3:
                        act.wait_ge(b_in[n % 2], 16 * (n // 2 + 1))
                    else:
                        act.wait_ge(m_add, KT + k + 1)
                    src = tmp[:, n % 2, :] if b < 3 else merged[:, k, :]
                    act.activation(AH[:, k, :], src, ACT.Copy).then_inc(b_hi, 1)
            norm(2)
            head_norms("xq", KT, S, xk_sq, xk_sum, xk_ln, xk_rstd, xk_done, 2, 1.0 / XD)
            units = NT * XH
            for w in range(units + 3):
                if w < units:
                    z = w % 2
                    act.wait_ge(c_mx, w + 1)
                    if w >= 2:
                        act.wait_ge(c_t, w - 1)
                    act.activation(sqb[:, z, 0:N_MEM], psG[:, z, 0:N_MEM], ACT.Exp, bias=small[:, 40 + z:41 + z],
                                   scale=XA_SCALE, accum_out=small[:, 42 + z:43 + z]).then_inc(c_exp, 1)
                if 1 <= w <= units:
                    z = (w - 1) % 2
                    act.wait_ge(c_t, w)
                    if w >= 3:
                        act.wait_ge(c_pv, w - 2)
                    act.activation(tmp[:, z, 0:N_MEM], psA[:, z * 512:z * 512 + N_MEM], ACT.Copy).then_inc(c_cp, 1)
                if w >= 3:
                    t, h, z = (w - 3) // XH, (w - 3) % XH, (w - 3) % 2
                    act.wait_ge(c_ot, w - 2)
                    act.activation(AH[:, 2 * h:2 * h + 2, t * P:(t + 1) * P], heads3(psG[:, z, 512:768], 2), ACT.Copy)\
                        .then_inc(c_hi, 1)
            norm(3)
            for c in range(0, FT, FC):
                t0 = first[f"gu{c}"]
                for k in range(min(FC, FT - c)):
                    n = c + k
                    act.wait_ge(mm, t0 + 2 * k + 1)
                    if n >= 2:
                        read_out(act, up_tile(n - 2))
                    act.activation(sqb[:, n % 2, :], psG[:, (t0 + 2 * k) % 2, :], ACT.Silu).then_inc(free[(t0 + 2 * k) % 2], 1)
                    read_out(act, up_tile(n))
                    act.activation(HH[:, k, :], tmp[:, n % 2, :], ACT.Copy).then_inc(f_hi, 1)
            for t in range(NT):
                act.wait_ge(o_tr, t + 1)
                if t >= 2:
                    act.wait_ge(o_st[t % 2], 16 * (t // 2))
                act.activation(sqb[:, t % 2, :], psA[:, :], ACT.Copy).then_inc(o_cp, 1)

        @block.vector
        def _(dve):
            def turn(i):
                _, tiles, dst = turns[i]
                for t in range(tiles):
                    q = turn_first[i] + t
                    dve.wait_ge(x_tr, q + 1)
                    dve.tensor_copy(dst[:, :, t * P:(t + 1) * P], heads3(psA[:, :])).then_inc(x_cp, 1)

            def add_squares(i, k):
                n, sq, acc = norms[i][2:5]
                dve.wait_ge(n_sq, KT * i + k + 1)
                if k > 1:
                    dve.wait_ge(n_acc, (KT - 1) * i + k - 1)
                dve.tensor_tensor(acc[:, 0:n], acc[:, 0:n], sq[:, k % 2, 0:n], ALU.add).then_inc(n_acc, 1)

            def norm(i):
                src, gain, n, _, acc, scaled, hi, lo = norms[i]
                dve.wait_ge(n_rstd, 2 * i + 2)

                def scale(k):
                    if k >= 2:
                        dve.wait_ge(n_lo, KT * i + k - 1)
                    dve.scalar_tensor_tensor(out=scaled[:, k % 2, 0:n], in0=src[:, k, 0:n], scalar=col(gain + k), in1=acc[:, 0:n],
                                             op0=ALU.mult, op1=ALU.mult).then_inc(n_out, 1)

                scale(0)
                for k in range(KT):
                    if k < KT - 1:
                        scale(k + 1)
                    dve.wait_ge(n_hi, KT * i + k + 1)
                    dve.tensor_tensor(lo[:, k, 0:n], scaled[:, k % 2, 0:n], hi[:, k, 0:n].bitcast(F32), ALU.subtract).then_inc(n_lo, 1)

            def head_norms(name, i0, n, dst, gain, sq, rstd, done, each, root_of=rst):
                t0 = first[name]

                def at(u, j):
                    return dst[:, bass.ds(u + 2 * j, 1), :].rearrange("p a s -> p (a s)") if not isinstance(j, int) else dst[:, u, :]

                def gained(u, j):
                    dve.wait_ge(sq, i0 + u + 1 + 2 * j)
                    dve.tensor_scalar(at(u, j), psG[:, (t0 + u) % 2, 0:n], col(gain + u % each), None, ALU.mult)\
                        .then_inc(free[(t0 + u) % 2], 1)

                def divided(u, j):
                    if u % each != each - 1:
                        return
                    dve.wait_ge(rstd, (i0 + u) // each + 1 + j * (2 // each))
                    dve.wait_ge(free[(t0 + u) % 2], (t0 + u) // 2 + 1 + j)
                    for v in range(u - each + 1, u + 1):
                        dve.tensor_tensor(at(v, j), at(v, j), root_of[:, 0:n], ALU.mult).then_inc(done, 1)

                gained(0, 0)
                with dve.Fori(0, KT // 2 - 1) as j:
                    for u in (1, 2):
                        gained(u, j)
                        divided(u - 1, j)
                gained(KT - 1, 0)
                divided(KT - 2, 0)
                divided(KT - 1, 0)

            def key_norm(i, kr):
                dve.tensor_tensor(tmp[:, 0, 0:512].rearrange("p (t c) -> p t c", t=NT), kr, kr, ALU.mult).then_inc(kp_step, 1)
                dve.wait_ge(kp_step, 10 * i + 1)
                dve.tensor_reduce(small[:, 0:8], tmp[:, 0, 0:512].rearrange("p (t c) -> p t c", t=NT), AXX, ALU.add)\
                    .then_inc(kp_step, 1)
                dve.wait_ge(kp_step, 10 * i + 4)
                for half in range(2):
                    dve.tensor_tensor(heads3(rst[:, :])[:, :, half * HD:(half + 1) * HD], kr, wide(small[:, 8:16], [P, NT, HD]),
                                      ALU.mult).then_inc(kp_step, 1)

            def key_gain(i, gain):
                dve.wait_ge(kp_step, 10 * i + 7)
                dve.tensor_scalar(rst[:, :], psA[:, :], col(gain), None, ALU.mult).then_inc(kp_step, 1)
                dve.wait_ge(kp_step, 10 * i + 9)
                dve.tensor_tensor(kl[:, i, :], rst[:, :], kh[:, i, :].bitcast(F32), ALU.subtract).then_inc(kp_step, 1)

            dve.wait_ge(s_pcol, 1)
            dve.tensor_copy(pcol[:, :], psB[:, 0:P]).then_inc(s_pcol, 1)
            dve.tensor_scalar(nsink[:, :], nsink[:, :], -1.0, None, ALU.mult).then_inc(s_pcol, 1)
            dve.wait_ge(s_alog, 1)
            dve.tensor_scalar(alog[:, :], alog[:, :], -1.0, None, ALU.mult).then_inc(s_alog, 1)
            dve.memset(swm[:, :], NEG).then_inc(s_pcol, 1)
            dve.wait_ge(s_pcol, 4)
            dve.memset(swm[0:HD, HD:HD + P], 0.0).then_inc(s_pcol, 1)
            dve.memset(swm[HD:P, P:2 * P], 0.0).then_inc(s_pcol, 1)
            dve.wait_ge(s_pcol, 6)
            turn(0)
            for k in range(1, KT):
                add_squares(0, k)
            norm(0)
            turn(1)
            for k in range(1, KT):
                add_squares(1, k)
            head_norms("xk", 0, N_MEM, xk0, XKN, xk_sq, xk_rstd, xk_done, 2, mrst)
            norm(1)
            dve.wait_ge(m_st, 48)
            for k in range(2):
                i = first["ckv"] + k
                dve.wait_ge(kv_sq, k + 1)
                dve.tensor_scalar(ckvT[:, k, :], psG[:, i % 2, :], col(KVN + k), None, ALU.mult).then_inc(free[i % 2], 1)
            ikr, ikc = heads3(tmp[:, 0, :]), heads3(tmp[:, 1, :])[:, :, 0:HD]
            read_out(dve, first["ikw"])
            dve.tensor_reduce(small[:, 16:24], ikr[:, :, 0:HD], AXX, ALU.add).then_inc(ik_step, 1)
            dve.wait_ge(ik_step, 1)
            dve.tensor_scalar(small[:, 16:24], small[:, 16:24], 1.0 / HD, None, ALU.mult).then_inc(ik_step, 1)
            dve.wait_ge(ik_step, 2)
            dve.tensor_tensor(ikc, ikr[:, :, 0:HD], wide(small[:, 16:24], [P, NT, HD]), ALU.subtract).then_inc(ik_step, 1)
            dve.wait_ge(ik_step, 3)
            sq3 = rst[:, 0:512].rearrange("p (t c) -> p t c", t=NT)
            dve.tensor_tensor(sq3, ikc, ikc, ALU.mult).then_inc(ik_step, 1)
            dve.wait_ge(ik_step, 4)
            dve.tensor_reduce(small[:, 16:24], sq3, AXX, ALU.add).then_inc(ik_step, 1)
            dve.wait_ge(ik_step, 7)
            for half in range(2):
                dve.tensor_tensor(heads3(ikd)[:, :, half * HD:(half + 1) * HD], ikc, wide(small[:, 24:32], [P, NT, HD]),
                                  ALU.mult).then_inc(ik_step, 1)
            dve.tensor_scalar(ixw[:, :, :], ikr[:, :, HD:IKW], IDX_SCALE, None, ALU.mult).then_inc(ik_step, 1)
            dve.wait_ge(kv_ln, 2)
            dve.tensor_tensor(kvt[:, :, :], heads3(psA[:, :]), wide(small[:, 0:8], [P, NT, P]), ALU.mult).then_inc(kv_done, 1)
            dve.wait_ge(kv_done, 1)
            dve.wait_ge(ik_step, 11)
            dve.tensor_scalar(ikd, psA[:, :], col(IW), col(IB), ALU.mult, ALU.add).then_inc(ik_step, 1)
            dve.wait_ge(ik_step, 13)
            dve.tensor_tensor(ikl, ikd, ikh.bitcast(F32), ALU.subtract).then_inc(ik_step, 1)
            key_norm(0, kvt[:, :, 0:HD])
            key_gain(0, DK)
            for v, (t, h) in enumerate(ix_units):
                n = (t + 1) * P
                sc = scores[:, sc_off[t]:sc_off[t] + n]
                dve.wait_ge(ix_relu, v + 1)
                if h == 0:
                    dve.tensor_scalar(sc, tmp[:, v % 2, 0:n], ixw[:, t, h:h + 1], None, ALU.mult).then_inc(ix_acc, 1)
                else:
                    dve.wait_ge(ix_acc, v)
                    dve.scalar_tensor_tensor(out=sc, in0=tmp[:, v % 2, 0:n], scalar=ixw[:, t, h:h + 1], in1=sc,
                                             op0=ALU.mult, op1=ALU.add).then_inc(ix_acc, 1)
            def late(t):
                end = sc_off[t] + (t + 1) * P
                return scores[0:HD, end - HD:end]

            for t in range(TOPK // P):
                dve.memset(scores[:, sc_off[t]:sc_off[t] + (t + 1) * P], 0.0).then_inc(tk_max, 1)
                dve.wait_ge(tk_max, t + 1)
                dve.memset(late(t), NEG).then_inc(masked, 1)
            dve.wait_ge(ix_acc, len(ix_units))
            for i in range((NT - TOPK // P) // 2):
                two = (TOPK // P + i, NT - 1 - i)
                m0 = TOPK // P + 2 * (TOPK // 8) * i
                r0 = (2 + 2 * (TOPK // 8)) * i
                sc = [scores[:, sc_off[t]:sc_off[t] + (t + 1) * P] for t in two]
                for t in two:
                    dve.memset(late(t), BARRED).then_inc(tk_rep, 1)
                with dve.Fori(0, TOPK // 8) as j:
                    for v in range(2):
                        dve.wait_ge(tk_rep, r0 + v + 1 + 2 * j)
                        dve.sem_inc(dve_go, 1)
                        dve.max(m8[:, v, :], sc[v]).then_inc(tk_max, 1)
                    for v in range(2):
                        dve.wait_ge(tk_max, m0 + v + 1 + 2 * j)
                        dve.sem_inc(dve_go, 1)
                        dve.match_replace(out=sc[v], in_to_replace=m8[:, v, :], in_values=sc[v], imm_value=TAKEN)\
                            .then_inc(tk_rep, 1)
                for v in range(2):
                    dve.wait_ge(tk_rep, r0 + v + 1 + 2 * (TOPK // 8))
                    dve.tensor_scalar(sc[v], sc[v], 0.5 * (TAKEN + BARRED), NEG, ALU.is_gt, ALU.mult).then_inc(masked, 1)
            head_norms("q", 0, S, qT, DQ, q_sq, q_rstd, q_done, 1)
            for i in (1, 2):
                dve.wait_ge(free[first["sk"] % 2], first["sk"] // 2 + 1)
                dve.wait_ge(free[first["sv"] % 2], first["sv"] // 2 + 1)
                key_norm(i, heads3(tmp[:, 1, :])[:, :, (i - 1) * HD:i * HD])
                key_gain(i, SK)

            def att_max(q, h, pp, kind, t, p):
                u = 2 * q + h
                n = nk(kind, t)
                mask = scores[:, sc_off[t]:sc_off[t] + n] if kind == "dsa" else swm[:, 2 * P - n:2 * P]
                swa = 2 * p if kind == "swa" else None
                dve.wait_ge(a_s, u + 1 + 2 * pp)
                if q % (NT * PAIRS):
                    before = t if p else t - 1
                    bank, _, _, m = turns_of(kind, q - 1, h, before, nk(kind, before) // P)[-1]
                    dve.wait_ge(a_t[bank], m + 1 + (2 if long(kind, before) else 1) * pp)
                if swa is not None and u >= 130:
                    dve.wait_ge(a_snk, u - 129)
                dve.sem_inc(dve_go, 1)
                dve.tensor_tensor_reduce(out=tmp[:, h, 0:n], in0=psG[:, h, 0:n], in1=mask, scale=1.0, scalar=TAKEN,
                                         op0=ALU.add, op1=ALU.max, accum_out=stat[:, h, 1:2]).then_inc(a_mx0, 1)
                dve.wait_ge(a_mx0, u + 1 + 2 * pp)
                if swa is None:
                    dve.tensor_scalar(stat[:, h, 0:1], stat[:, h, 1:2], -AT_SCALE, None, ALU.mult).then_inc(a_mx, 1)
                else:
                    dve.tensor_scalar(stat[:, h, 0:1], stat[:, h, 1:2], -AT_SCALE, nsink[:, swa + h:swa + h + 1],
                                      ALU.mult, ALU.min).then_inc(a_mx, 1)

            def att_copy(q, h, pp, kind, t):
                for bank, b0, b1, n in turns_of(kind, q, h, t, nk(kind, t) // P):
                    if bank == 1:
                        dve.wait_ge(a_t[1], n + 1 + (2 if long(kind, t) else 1) * pp)
                        if q > 0:
                            dve.wait_ge(a_pv, 2 * q + h - 1 + 2 * pp)
                        dve.tensor_copy(sqb[:, h, b0 * P:b1 * P], psA[:, 512:512 + (b1 - b0) * P]).then_inc(a_cp[1], 1)

            def att_div(q, pp, swa):
                z = q % 2
                dve.wait_ge(a_pv, 2 * q + 2 + 2 * pp)
                if q >= 2:
                    dve.wait_ge(a_ot, q - 1 + pp)
                if swa:
                    dve.wait_ge(a_snk, 2 * (q - 64) + 2)
                    dve.tensor_tensor(stat[:, z, 4:6], stat[:, z, 4:6], stat[:, z, 6:8], ALU.add).then_inc(a_den, 1)
                    dve.wait_ge(a_den, q - 64 + 1)
                dve.reciprocal(stat[:, z, 2:4], stat[:, z, 4:6]).then_inc(a_ri, 1)
                dve.wait_ge(a_ri, q + 1 + pp)
                dve.tensor_tensor(otok[:, z, :].rearrange("p (h c) -> p h c", h=2),
                                  (psB, psC)[z][:, 0:P].rearrange("p (h c) -> p h c", h=2),
                                  wide(stat[:, z, 2:4], [P, 2, HD]), ALU.mult).then_inc(a_o, 1)

            def attention(kind, q0):
                def pair(q, pp, t, p, before, after):
                    att_max(q, 1, pp, kind, t, p)
                    att_copy(q, 0, pp, kind, t)
                    if before is not None:
                        att_div(q - 1, pp, kind == "swa")
                    if after is not None:
                        att_max(q + 1, 0, pp, kind, *after)
                    att_copy(q, 1, pp, kind, t)

                att_max(q0, 0, 0, kind, 0, 0)
                for t in range(NT):
                    q = q0 + PAIRS * t
                    pair(q, 0, t, 0, (t - 1, PAIRS - 1) if t else None, (t, 1))
                    if kind == "dsa" and t:
                        with dve.Fori(0, PAIRS // 2 - 1) as j:
                            for u in (1, 2):
                                pair(q + u, 2 * j, t, u, (t, u - 1), (t, u + 1))
                    else:
                        for p in range(1, PAIRS - 1):
                            pair(q + p, 0, t, p, (t, p - 1), (t, p + 1))
                    pair(q + PAIRS - 1, 0, t, PAIRS - 1, (t, PAIRS - 2), (t + 1, 0) if t < NT - 1 else None)
                att_div(q0 + NT * PAIRS - 1, 0, kind == "swa")

            attention("dsa", 0)
            head_norms("sq", KT, S, qT, SQ, q_sq, q_rstd, q_done, 1)
            attention("swa", 64)
            dve.wait_ge(free[first["dt"] % 2], first["dt"] // 2 + 1)
            dve.tensor_tensor(dts[:, 1, :, :], dts[:, 0, :, :], dtb[:, :].unsqueeze(1).to_broadcast([P, NT, HEADS]), ALU.add)\
                .then_inc(dt_step, 1)
            dve.wait_ge(dt_step, 1)
            dve.scalar_tensor_tensor(out=dts[:, 2, :, :], in0=dts[:, 1, :, :], scalar=-1.0, in1=dts[:, 1, :, :],
                                     op0=ALU.mult, op1=ALU.max).then_inc(dt_step, 1)
            dve.wait_ge(dt_step, 4)
            dve.scalar_tensor_tensor(out=dts[:, 0, :, :], in0=dts[:, 1, :, :], scalar=0.0, in1=dts[:, 2, :, :],
                                     op0=ALU.max, op1=ALU.add).then_inc(dt_step, 1)
            dve.wait_ge(dt_step, 5)
            dve.wait_ge(s_alog, 2)
            dve.tensor_tensor(dts[:, 3, :, :], dts[:, 0, :, :], alog[:, :].unsqueeze(1).to_broadcast([P, NT, HEADS]), ALU.mult)\
                .then_inc(dt_step, 1)
            def convolve(j):
                for u in range(2):
                    i = first["xbc"] + u
                    k = u + 2 * j
                    ps, acc = psG[:, i % 2, :], tmp[:, u, :]
                    dve.wait_ge(mm, i + 1 + 2 * j)
                    if not isinstance(j, int):
                        dve.wait_ge(cv_out, u - 1 + 2 * j)
                    dve.tensor_scalar(acc, ps, pcol[:, bass.ds(CW + (CONV - 1) * XC + k, 1)], pcol[:, bass.ds(CB + k, 1)],
                                      ALU.mult, ALU.add).then_inc(cv_acc, 1)
                    for tap in range(CONV - 2, -1, -1):
                        back = CONV - 1 - tap
                        dve.wait_ge(cv_acc, 3 * u + back + 6 * j)
                        ins = dve.scalar_tensor_tensor(out=acc[:, back:], in0=ps[:, 0:S - back],
                                                       scalar=pcol[:, bass.ds(CW + tap * XC + k, 1)], in1=acc[:, back:],
                                                       op0=ALU.mult, op1=ALU.add)
                        ins.then_inc(cv_acc if tap else free[i % 2], 1)

            convolve(0)
            with dve.Fori(1, XC // 2) as j:
                convolve(j)
            dve.wait_ge(dt_step, 7)
            dve.tensor_copy(dts[:, 4, :, :], psB[:, 0:P].rearrange("p (t h) -> p t h", t=NT)).then_inc(dt_step, 1)
            dve.wait_ge(dt_step, 8)
            dve.tensor_tensor(dts[:, 7, :, :], psB[:, P:2 * P].rearrange("p (t h) -> p t h", t=NT), dts[:, 4, :, :], ALU.subtract)\
                .then_inc(dt_step, 1)
            dve.wait_ge(dt_step, 12)
            dve.tensor_tensor(dts[:, 7, :, :], dts[:, 7, :, :], dts[:, 0, :, :], ALU.mult).then_inc(dt_step, 1)
            dve.wait_ge(cv_out, XC)
            dve.wait_ge(dt_step, 13)
            for c in range(NT):
                def by_head(i, h0=0, h1=HEADS):
                    return wide(dts[:, i, c, h0:h1], [P, h1 - h0, HD])

                dve.wait_ge(s_xtok, c + 1)
                dve.tensor_tensor(heads3(xdt[:, :], HEADS), heads3(xtok[:, :], HEADS), by_head(0), ALU.mult).then_inc(s_xdt, 1)
                if c:
                    dve.wait_ge(s_upd, 2 * c)
                dve.tensor_tensor(heads3(xw[:, :], HEADS), heads3(xtok[:, :], HEADS), by_head(7), ALU.mult).then_inc(s_xw, 1)
                dve.wait_ge(s_bt, c + 1)
                dve.tensor_copy(btok[:, :], psA[:, 0:2 * STATE]).then_inc(s_btok, 1)

                def differences(q):
                    n = 4 * c + q
                    dve.wait_ge(s_bc, n + 1)
                    if n >= 2:
                        dve.wait_ge(s_e, n - 1)
                    dve.tensor_tensor(tmp[:, n % 2, 0:512].rearrange("p (h l) -> p h l", h=4),
                                      (psB, psC)[n % 2][:, :].rearrange("p (h l) -> p h l", h=4),
                                      wide(dts[:, 4, c, 4 * q:4 * q + 4], [P, 4, P]), ALU.subtract).then_inc(s_df, 1)

                def weigh(q):
                    n = 4 * c + q
                    dve.wait_ge(s_e, n + 1)
                    if n >= 2:
                        dve.wait_ge(s_yd, n - 1)
                    if q == 0:
                        dve.wait_ge(s_g, c + 1)
                    g = 512 + (q // 2) * P
                    dve.tensor_tensor(sqb[:, n % 2, 512:1024].rearrange("p (h l) -> p h l", h=4),
                                      sqb[:, n % 2, 0:512].rearrange("p (h l) -> p h l", h=4),
                                      psA[:, g:g + P].unsqueeze(1).to_broadcast([P, 4, P]), ALU.mult).then_inc(s_m, 1)

                differences(0)
                differences(1)
                weigh(0)
                differences(2)
                weigh(1)
                differences(3)
                weigh(2)
                weigh(3)
                if c:
                    dve.wait_ge(s_ytr, c)
                    dve.wait_ge(s_yo, c)
                    dve.tensor_tensor(heads3(yt[:, :], HEADS), heads3(psG[:, 1, :], HEADS), by_head(6), ALU.mult).then_inc(s_off, 1)
                    dve.wait_ge(s_off, c)
                    dve.wait_ge(s_yd, 4 * c + 4)
                    dve.tensor_tensor(yt[:, :], yt[:, :], psG[:, 0, :], ALU.add).then_inc(s_y, 1)
                else:
                    dve.wait_ge(s_yd, 4)
                    dve.wait_ge(s_ztok, 1)
                    dve.tensor_copy(yt[:, :], psG[:, 0, :]).then_inc(s_y, 1)
                if c < NT - 1:
                    for g in range(GROUPS):
                        sg = st[:, g * 512:(g + 1) * 512]
                        if c:
                            dve.tensor_tensor(heads3(sg, 8), heads3(sg, 8), by_head(5, 8 * g, 8 * g + 8), ALU.mult).then_inc(s_dec, 1)
                            dve.wait_ge(s_dec, 2 * c - 1 + g)
                        dve.wait_ge(s_upd, 2 * c + g + 1)
                        if c:
                            dve.tensor_tensor(sg, sg, psA[:, 0:512], ALU.add).then_inc(s_stt, 1)
                        else:
                            dve.tensor_copy(sg, psA[:, 0:512]).then_inc(s_stt, 1)
                dve.wait_ge(s_yp, 3 * c + 3)
                for g in range(GROUPS):
                    yg = yt[:, g * 512:(g + 1) * 512]
                    if c and g == 0:
                        dve.wait_ge(s_yst, 16 * c)
                    dve.tensor_tensor_reduce(out=rst[:, g * 512:(g + 1) * 512], in0=yg, in1=yg, scale=1.0, scalar=0.0,
                                             op0=ALU.mult, op1=ALU.add, accum_out=small[:, 32 + g:33 + g]).then_inc(s_ss, 1)
                dve.wait_ge(s_rs, 2 * c + 2)
                for g in range(GROUPS):
                    yg = yt[:, g * 512:(g + 1) * 512]
                    dve.tensor_scalar(yg, yg, small[:, 34 + g:35 + g], None, ALU.mult).then_inc(s_yn, 1)
                dve.wait_ge(s_ytr, c + 1)
                dve.tensor_tensor(heads3(rst[:, :]), heads3(psA[:, :]), wide(pcol[:, SSN:SSN + KT], [P, KT, P]), ALU.mult)\
                    .then_inc(s_ycp, 1)

            def split_mixer(b):
                for k in range(KT):
                    n = KT * b + k
                    dve.wait_ge(b_hi, n + 1)
                    src = tmp[:, n % 2, :] if b < 3 else merged[:, k, :]
                    dve.tensor_tensor(AL[:, k, :], src, AH[:, k, :].bitcast(F32), ALU.subtract).then_inc(b_lo, 1)

            for b in range(3):
                split_mixer(b)
                for k in range(KT):
                    n = KT * b + k
                    i = first[f"br{b}"] + k
                    dve.wait_ge(g_in[n % 2], 16 * (n // 2 + 1))
                    dve.wait_ge(mm, i + 1)
                    if b == 0:
                        dve.tensor_tensor(merged[:, k, :], psG[:, i % 2, :], sqb[:, n % 2, :], ALU.mult).then_inc(free[i % 2], 1)
                    else:
                        if n > KT:
                            dve.wait_ge(m_add, n - KT)
                        dve.tensor_tensor(rst[:, :], psG[:, i % 2, :], sqb[:, n % 2, :], ALU.mult).then_inc(free[i % 2], 1)
                        dve.wait_ge(free[i % 2], i // 2 + 1)
                        dve.tensor_tensor(merged[:, k, :], merged[:, k, :], rst[:, :], ALU.add).then_inc(m_add, 1)
            dve.wait_ge(m_add, 2 * KT)
            split_mixer(3)

            def residual(name):
                norm_after = {"out": 2, "xo": 3}.get(name)
                for k in range(KT):
                    i = first[name] + k
                    dve.wait_ge(mm, i + 1)
                    dve.tensor_tensor(xT[:, k, :], psG[:, i % 2, :], xT[:, k, :], ALU.add).then_inc(free[i % 2], 1)
                    if norm_after and k >= 2:
                        add_squares(norm_after, k - 1)
                if norm_after:
                    add_squares(norm_after, KT - 1)

            dve.wait_ge(x_back, 16)
            residual("out")
            norm(2)
            head_norms("xq", KT, S, xqT, XQN, xk_sq, xk_rstd, xk_done, 2)
            units = NT * XH
            for w in range(units + 3):
                if 2 <= w <= units + 1:
                    z = w % 2
                    dve.wait_ge(c_exp, w - 1)
                    dve.reciprocal(small[:, 46 + z:47 + z], small[:, 42 + z:43 + z]).then_inc(c_ri, 1)
                if w < units:
                    z = w % 2
                    dve.wait_ge(c_s, w + 1)
                    if w >= 2:
                        dve.wait_ge(c_exp, w - 1)
                    dve.tensor_reduce(small[:, 44 + z:45 + z], psG[:, z, 0:N_MEM], AXX, ALU.max).then_inc(c_mx0, 1)
                    dve.wait_ge(c_mx0, w + 1)
                    dve.tensor_scalar(small[:, 40 + z:41 + z], small[:, 44 + z:45 + z], -XA_SCALE, None, ALU.mult).then_inc(c_mx, 1)
                if 2 <= w <= units + 1:
                    z = w % 2
                    dve.wait_ge(c_ri, w - 1)
                    dve.wait_ge(c_pv, w - 1)
                    if w >= 4:
                        dve.wait_ge(c_ot, w - 3)
                    dve.tensor_scalar(tmp[:, z, 512:768], (psB, psC)[z][:, 0:XD], small[:, 46 + z:47 + z], None, ALU.mult)\
                        .then_inc(c_o, 1)
                if w >= 3:
                    t, h, z = (w - 3) // XH, (w - 3) % XH, (w - 3) % 2
                    a = (slice(None), slice(2 * h, 2 * h + 2), slice(t * P, (t + 1) * P))
                    dve.wait_ge(c_hi, w - 2)
                    dve.tensor_tensor(AL[a], heads3(psG[:, z, 512:768], 2), AH[a].bitcast(F32), ALU.subtract).then_inc(c_lo, 1)
            residual("xo")
            norm(3)
            for c in range(0, FT, FC):
                for k in range(min(FC, FT - c)):
                    n = c + k
                    i = up_tile(n)
                    dve.wait_ge(mm, i + 1)
                    read_out(dve, i - 1)
                    if n >= 2:
                        dve.wait_ge(f_lo, n - 1)
                    dve.tensor_tensor(tmp[:, n % 2, :], psG[:, i % 2, :], sqb[:, n % 2, :], ALU.mult).then_inc(free[i % 2], 1)
                    dve.wait_ge(f_hi, n + 1)
                    dve.tensor_tensor(HL[:, k, :], tmp[:, n % 2, :], HH[:, k, :].bitcast(F32), ALU.subtract).then_inc(f_lo, 1)
                residual(f"dn{c}")


NAMES = ["x", "mem", "norm_mix", "w_in", "dsa_kv_norm", "dsa_w_ukv", "dsa_q_norm", "dsa_k_norm", "idx_k_ln_w", "idx_k_ln_b",
         "swa_q_norm", "swa_k_norm", "swa_sinks", "ssm_conv_w", "ssm_conv_b", "ssm_dt_bias", "ssm_a_log", "ssm_d",
         "ssm_norm", "w_br_dsa", "w_br_swa", "w_br_ssm", "w_out", "norm_xa", "norm_mem", "xa_wq", "xa_wkv", "xa_q_norm",
         "xa_k_norm", "xa_wo", "norm_ffn", "ffn_w_gate_up", "ffn_w_down"]


def kernel(**inputs):
    import numpy as np
    import concourse.bacc as bacc
    from concourse.bass_utils import run_bass_kernel_spmd

    nc = bacc.Bacc("TRN2", target_bir_lowering=False, num_devices=1)
    arrays, ap = {}, {}
    for name in NAMES:
        a = np.ascontiguousarray(inputs[name])
        arrays[f"in_{name}"] = a
        ap[name] = nc.dram_tensor(f"in_{name}", a.shape, mybir.dt.from_np(a.dtype), kind="ExternalInput").ap()
    out = nc.dram_tensor("out_x", (1, S, D), F32, kind="ExternalOutput").ap()
    build(nc, ap, out)
    r = run_bass_kernel_spmd(nc, [arrays], core_ids=[0])
    return r.results[0]["out_x"]
```

```python
from contextlib import ExitStack

import concourse.bass as bass
from concourse import mybir

F32 = mybir.dt.float32
F32R = mybir.dt.float32r
ALU = mybir.AluOpType
ACT = mybir.ActivationFunctionType
AXX = mybir.AxisListType.X

P = 128
D = 1024
S = 1024
KT = D // P
NT = S // P
CHUNK = 64
EPS = 1e-6
HD = 64
HEADS = 16
PAIRS = HEADS // 2
KV_RANK = 256
IDX_HEADS = 8
TOPK = 256
GROUPS = 2
STATE = 128
XC = (D + 2 * GROUPS * STATE) // P
CONV = 4
N_MEM = 256
MT = N_MEM // P
XH = 4
XD = D // XH
DFF = 2816
FT = DFF // P
FC = 4
FCH = -(-FT // FC)
PARAMS = 9 + 1 + 12 + 4 + 1
NEG = -1e30
TAKEN = -3e38
BARRED = -1e38
AT_SCALE = HD ** -0.5
XA_SCALE = XD ** -0.5
IDX_SCALE = IDX_HEADS ** -0.5 * HD ** -0.5

C_Q, C_CKV, C_IQ, C_IK = 0, 1024, 1280, 1792
C_SQ, C_SK, C_SV, C_Z, C_XBC, C_DT, C_G = 1864, 2888, 3016, 3144, 4168, 5704, 5720
IKW = HD + IDX_HEADS


def tile_plan():
    plan = [
        ("xk", "xa_wkv", 0, KT, 0, P, 8), ("xv", "xa_wkv", 0, KT, D, P, 8),
        ("ikw", "w_in", 0, KT, C_IK, P, 1), ("ckv", "w_in", 0, KT, C_CKV, P, 2), ("iq", "w_in", 0, KT, C_IQ, P, 4),
        ("gate", "w_in", 0, KT, C_G, P, 24),
        ("z", "w_in", 0, KT, C_Z, P, 8), ("q", "w_in", 0, KT, C_Q, P, 8),
        ("sk", "w_in", 0, KT, C_SK, P, 1), ("sv", "w_in", 0, KT, C_SV, P, 1), ("sq", "w_in", 0, KT, C_SQ, P, 8),
        ("dt", "w_in", 0, KT, C_DT, P, 1), ("xbc", "w_in", 0, KT, C_XBC, P, XC),
        ("br0", "w_br_dsa", 0, KT, 0, P, 8), ("br1", "w_br_swa", 0, KT, 0, P, 8), ("br2", "w_br_ssm", 0, KT, 0, P, 8),
        ("out", "w_out", 0, KT, 0, P, 8),
        ("xq", "xa_wq", 0, KT, 0, P, 8),
        ("xo", "xa_wo", 0, KT, 0, P, 8),
    ]
    for c in range(0, FT, FC):
        w = min(FC, FT - c)
        plan.append((f"gu{c}", "ffn_w_gate_up", 0, KT, (c * P, DFF + c * P), P, 2 * w))
        plan.append((f"dn{c}", "ffn_w_down", c, w, 0, P, 8))
    return plan


def build(nc, ap, out):
    plan = tile_plan()
    first = {}
    n = 0
    for name, *_, count in plan:
        first[name] = n
        n += count
    n_tiles = n

    ctx = ExitStack()
    with ctx:
        def sem(name):
            return ctx.enter_context(nc.semaphore(name))

        def sb(name, shape, dt=F32, stack=ctx):
            return stack.enter_context(nc.sbuf_tensor(name, shape, dt))

        def dram(name, shape):
            return nc.dram_tensor(name, shape, F32, kind="Internal").ap()

        gate_d = dram("gate_d", (3 * KT, P, S))
        z_d = dram("z_d", (KT, P, S))
        y_d = dram("y_d", (3, KT, P, S))

        x_d = dram("x_d", (KT, P, S))
        xk_d = dram("xk_d", (P, KT, N_MEM))
        xv_d = dram("xv_d", (P, MT, D))

        AH, AL = sb("AH", [P, KT, S], F32R), sb("AL", [P, KT, S], F32R)
        WH, WL = sb("WH", [P, 2, KT, P], F32R), sb("WL", [P, 2, KT, P], F32R)
        wraw = sb("wraw", [P, 4, KT, P])
        ident, ones, bones = sb("ident", [P, P]), sb("ones", [P, P]), sb("bones", [P, P])
        tri, cmask = sb("tri", [P, P]), sb("cmask", [P, P])
        pcol = sb("pcol", [P, P])
        nsink, dskip = sb("nsink", [P, HEADS]), sb("dskip", [P, HEADS])
        dtb, alog = sb("dtb", [P, HEADS]), sb("alog", [P, HEADS])
        sqb, tmp, rst = sb("sqb", [P, 2, S]), sb("tmp", [P, 2, S]), sb("rst", [P, S])
        small = sb("small", [P, 64])

        g = ExitStack()
        xT0 = sb("xT0", [P, KT, S], F32, g)
        prow = sb("prow", [P, P], F32, g)
        memT = sb("memT", [P, KT, N_MEM], F32, g)
        MH, ML = sb("MH", [P, KT, N_MEM], F32R, g), sb("ML", [P, KT, N_MEM], F32R, g)
        xk0, xv0 = sb("xk0", [P, KT, N_MEM], F32, g), sb("xv0", [P, MT, D], F32, g)
        msq, mtmp, mrst = sb("msq", [P, 2, N_MEM], F32, g), sb("mtmp", [P, 2, N_MEM], F32, g), sb("mrst", [P, N_MEM], F32, g)
        g.close()
        g = ExitStack()
        sc_off = [P * qb * (qb + 1) // 2 for qb in range(NT)]
        scores = sb("scores", [P, P * NT * (NT + 1) // 2], F32, g)
        kh, kl = sb("kh", [P, 3, S], F32R, g), sb("kl", [P, 3, S], F32R, g)
        kvt, svt = sb("kvt", [P, NT, 2 * HD], F32, g), sb("svt", [P, NT, P], F32, g)
        qT = sb("qT", [P, PAIRS, S], F32, g)
        qst = sb("qst", [P, 2, 2, P], F32R, g)
        otok, oT = sb("otok", [P, 2, P], F32, g), sb("oT", [P, 2, P], F32, g)
        swm = sb("swm", [P, 2 * P], F32, g)
        wukv = oT
        m8, ixw = sb("m8", [P, 2, 8], F32, g), sb("ixw", [P, NT, IDX_HEADS], F32, g)
        stat = sb("stat", [P, 2, 8], F32, g)
        g.close()
        iqT, ckvT, ikd = qT[:, 0:4, :], qT[:, 5:7, :], qT[:, 7, :]
        ikh, ikl = kh[:, 1, :], kl[:, 1, :]
        g = ExitStack()
        xcT = sb("xcT", [P, XC, S], F32, g)
        zt, xtok, ztok = sb("zt", [P, KT, P], F32, g), sb("xtok", [P, 2, D], F32, g), sb("ztok", [P, D], F32, g)
        xdt, xw, btok = sb("xdt", [P, D], F32, g), sb("xw", [P, D], F32, g), sb("btok", [P, 2 * STATE], F32, g)
        st = sb("st", [P, D], F32, g)
        yt, yoff = sb("yt", [P, D], F32, g), sb("yoff", [P, D], F32, g)
        dts = sb("dts", [P, 6, NT, HEADS], F32, g)
        g.close()
        g = ExitStack()
        xT = sb("xT", [P, KT, S], F32, g)
        g2 = ExitStack()
        merged = sb("merged", [P, KT, S], F32, g2)
        yst = sb("yst", [P, KT - 2, S], F32, g2)
        g2.close()
        g2 = ExitStack()
        xqT = sb("xqT", [P, KT, S], F32, g2)
        xkT, xv = sb("xkT", [P, KT, N_MEM], F32, g2), sb("xv", [P, MT, D], F32, g2)
        g2.close()
        g2 = ExitStack()
        HH, HL = sb("HH", [P, FC, S], F32R, g2), sb("HL", [P, FC, S], F32R, g2)
        g2.close()
        g.close()

        psG = ctx.enter_context(nc.psum_tensor("psG", [P, 2, S], F32))
        psA = ctx.enter_context(nc.psum_tensor("psA", [P, S], F32))
        psB = ctx.enter_context(nc.psum_tensor("psB", [P, 512], F32))
        psC = ctx.enter_context(nc.psum_tensor("psC", [P, 512], F32))


        s_par, s_const, s_pcol, s_alog = sem("s_par"), sem("s_const"), sem("s_pcol"), sem("s_alog")
        x_in = [sem("x_in0"), sem("x_in1")]
        x_tr, x_cp = sem("x_tr"), sem("x_cp")
        n_sq, n_acc, n_sum, n_rstd, n_out, n_hi, n_lo = (sem(f"n_{x}") for x in ("sq", "acc", "sum", "rstd", "out", "hi", "lo"))
        w_in = [sem(f"w_in{i}") for i in range(4)]
        w_hi, w_lo = sem("w_hi"), sem("w_lo")
        mm = sem("mm")
        free = [sem("free0"), sem("free1")]
        ik_step, kv_sq, kv_pe, kv_ln, kv_done, kp_step = (sem(x) for x in ("ik_step", "kv_sq", "kv_pe", "kv_ln", "kv_done", "kp_step"))
        ix_q, ix_pe, ix_relu, ix_acc, tk_max, tk_rep, masked = (sem(x) for x in ("ix_q", "ix_pe", "ix_relu", "ix_acc", "tk_max", "tk_rep", "masked"))
        g_st = [sem("g_st0"), sem("g_st1")]
        q_sq, q_sum, q_ln, q_rstd, q_done = (sem(f"q_{x}") for x in ("sq", "sum", "ln", "rstd", "done"))
        sv_cp = sem("sv_cp")
        a_q, a_s, a_mx0, a_mx, a_exp, a_snk, a_pv, a_den, a_ri, a_o, a_ot, a_oc = (
            sem(f"a_{x}") for x in ("q", "s", "mx0", "mx", "exp", "snk", "pv", "den", "ri", "o", "ot", "oc"))
        a_t, a_cp = [sem("a_t0"), sem("a_t1")], [sem("a_cp0"), sem("a_cp1")]
        y_st = [sem("y_st0"), sem("y_st1")]
        dt_step, acv, cv_acc, cv_out = sem("dt_step"), sem("acv"), sem("cv_acc"), sem("cv_out")
        s_zin, s_xt, s_xdt, s_xtok, s_xw, s_zt, s_ztok, s_bt, s_btok, s_g = (
            sem(f"s_{x}") for x in ("zin", "xt", "xdt", "xtok", "xw", "zt", "ztok", "bt", "btok", "g"))
        s_bc, s_df, s_dm, s_e, s_m, s_yd, s_yo, s_upd, s_dec, s_stt, s_y, s_skip, s_ysum, s_yg, s_ss, s_rs, s_yn, s_ytr, s_ycp, s_yst = (
            sem(f"s_{x}") for x in ("bc", "df", "dm", "e", "m", "yd", "yo", "upd", "dec", "stt", "y", "skip", "ysum", "yg", "ss", "rs", "yn",
                                    "ytr", "ycp", "yst"))
        g_in = [sem("g_in0"), sem("g_in1")]
        b_in = [sem(f"b_in{k}") for k in range(KT)]
        b_hi, b_lo, m_add = sem("b_hi"), sem("b_lo"), sem("m_add")
        xk_sq, xk_sum, xk_ln, xk_rstd, xk_done = (sem(f"xk_{x}") for x in ("sq", "sum", "ln", "rstd", "done"))
        c_s, c_mx0, c_mx, c_exp, c_t, c_cp, c_pv, c_ri, c_o, c_ot, c_hi, c_lo = (
            sem(f"c_{x}") for x in ("s", "mx0", "mx", "exp", "t", "cp", "pv", "ri", "o", "ot", "hi", "lo"))
        f_hi, f_lo = sem("f_hi"), sem("f_lo")
        o_tr, o_cp, o_st = sem("o_tr"), [sem("o_cp0"), sem("o_cp1")], [sem("o_st0"), sem("o_st1")]
        t_raw, t_tr, t_out = sem("t_raw"), sem("t_tr"), sem("t_out")
        s_off, m_st, x_back, xkv_back = sem("s_off"), sem("m_st"), sem("x_back"), sem("xkv_back")
        pool_go, dve_go = sem("pool_go"), sem("dve_go")
        block = ctx.enter_context(nc.Block())
        MIX, XA, FFN, MEM, CW, CB, KVN, SSN, XQN, XKN, DQ, DK, SQ, SK, IW, IB = (
            0, 8, 16, 24, 32, 80, 92, 94, 102, 104, 106, 107, 108, 109, 110, 111)

        ix_units = [(t, h) for t in range(TOPK // P, NT) for h in range(IDX_HEADS)]

        def col(i):
            return pcol[:, i:i + 1]

        def heads3(x, n=NT):
            return x.rearrange("p (t c) -> p t c", t=n)

        def read_out(eng, tile):
            eng.wait_ge(free[tile % 2], tile // 2 + 1)

        def all_read_out(eng, tile):
            read_out(eng, tile - 1)
            read_out(eng, tile - 2)

        def nk(kind, t):
            return P * (t + 1 if kind == "dsa" else min(t + 1, 2))

        def long(kind, t):
            return kind == "dsa" and (t + 1) * P > 512

        def turns_of(kind, q, h, t, nb):
            pairs, short = NT * PAIRS, 512 // P * PAIRS
            if long(kind, t):
                n = short + 2 * (q - short) + h
                return [(0, 0, 4, n), (1, 4, nb, n)]
            return [(h, 0, nb, q if kind == "dsa" else 2 * pairs - short + q - pairs)]

        def up_tile(n):
            return first[f"gu{n // FC * FC}"] + 2 * (n % FC) + 1

        def wide(x, shape):
            return x.unsqueeze(len(shape) - 1).to_broadcast(shape)

        w_dram = {k: ap[k][0].rearrange("(k p) n -> p k n", p=P)
                  for k in ("w_in", "w_br_dsa", "w_br_swa", "w_br_ssm", "w_out", "xa_wkv", "xa_wq", "xa_wo",
                            "ffn_w_gate_up", "ffn_w_down")}
        x_rows = ap["x"][0].rearrange("(t p) d -> t p d", p=P)
        mem_rows = ap["mem"][0].rearrange("(t p) d -> t p d", p=P)
        out_rows = out[0].rearrange("(t p) d -> t p d", p=P)
        def mixed(k):
            return tmp[:, k, :] if k < 2 else yst[:, k - 2, :]

        turns = [(mem_rows, MT, memT), (x_rows, NT, xT0)]
        turn_first = [0, MT]
        norms = [(memT, MEM, N_MEM, msq, mrst, mtmp, MH, ML)] + [
            (src, gain, S, sqb, rst, tmp, AH, AL) for src, gain in ((xT0, MIX), (xT, XA), (xT, FFN))]

        @block.sync
        def _(sp):
            def turn(i):
                src, tiles, _ = turns[i]
                for t in range(tiles):
                    q = turn_first[i] + t
                    if q >= 2:
                        sp.wait_ge(x_tr, q - 1)
                    sp.dma_start(tmp[:, q % 2, :], src[t]).then_inc(x_in[q % 2], 16)

            def weight_tiles(name, lo, hi):
                _, w, k0, kn, c0, width, count = next(x for x in plan if x[0] == name)
                t0 = first[name]

                def one(u, j):
                    slot = (t0 + u) % 4
                    if t0 + u >= 4:
                        sp.wait_ge(w_lo, t0 + u - 3 + 4 * j)
                    if isinstance(c0, tuple):
                        c = c0[u % 2] + P * (u // 2) + 2 * P * j
                    else:
                        c = c0 + P * u + 4 * P * j
                    sp.dma_start(wraw[:, slot, 0:kn, 0:width], w_dram[w][:, k0:k0 + kn, bass.ds(c, width)])\
                        .then_inc(w_in[slot], 16)

                if hi is not None:
                    for u in range(lo, hi):
                        one(u, 0)
                elif count % 4 == 0 and count > 4:
                    for u in range(4):
                        one(u, 0)
                    with sp.Fori(0, count // 4 - 1) as j:
                        for u in range(4, 8):
                            one(u, j)
                else:
                    for u in range(count):
                        one(u, 0)

            def weights(name):
                weight_tiles(name, 0, None)

            sp.wait_ge(s_const, 1)
            for key, at in (("norm_mix", MIX), ("norm_xa", XA), ("norm_ffn", FFN), ("norm_mem", MEM),
                            ("ssm_conv_b", CB), ("dsa_kv_norm", KVN), ("ssm_norm", SSN), ("xa_q_norm", XQN),
                            ("xa_k_norm", XKN)):
                rows = ap[key][0].rearrange("(r c) -> r c", c=P)
                sp.dma_start(prow[at:at + rows.shape[0], :], rows).then_inc(s_par, 16)
            sp.dma_start(prow[CW:CW + CONV * XC, :], ap["ssm_conv_w"][0].rearrange("j (r c) -> (j r) c", c=P))\
                .then_inc(s_par, 16)
            for key, at in (("dsa_q_norm", DQ), ("dsa_k_norm", DK), ("swa_q_norm", SQ), ("swa_k_norm", SK),
                            ("idx_k_ln_w", IW), ("idx_k_ln_b", IB)):
                for half in range(2):
                    sp.dma_start(prow[at:at + 1, half * HD:(half + 1) * HD], ap[key]).then_inc(s_par, 16)
            for key, dst in (("swa_sinks", nsink), ("ssm_d", dskip), ("ssm_dt_bias", dtb), ("ssm_a_log", alog)):
                sp.dma_start(dst[:, :], ap[key][0].partition_broadcast(P)).then_inc(s_par, 16)
            sp.dma_start(wukv[:, :, :], ap["dsa_w_ukv"][0].rearrange("(k p) n -> p k n", p=P)).then_inc(s_par, 16)
            turn(0)
            weight_tiles("xk", 0, 4)
            turn(1)
            weight_tiles("xk", 4, 8)
            sp.wait_ge(x_cp, MT + NT)
            sp.dma_start(x_d.rearrange("k p s -> p k s"), xT0[:, :, :]).then_inc(m_st, 16)
            weights("xv")
            weights("ikw")
            weights("ckv")
            weights("iq")
            weights("gate")
            weights("z")
            weights("q")
            weights("sk")
            weights("sv")
            weights("sq")
            weights("dt")
            weights("xbc")
            for c in range(NT):
                if c == 0:
                    for i in range(2):
                        sp.wait_ge(g_st[i], 16 * 16)
                else:
                    sp.wait_ge(s_zt, c)
                sp.dma_start(zt[:, :, :], z_d[:, :, c * P:(c + 1) * P].rearrange("k p s -> p k s"))\
                    .then_inc(s_zin, 16)
            weight_tiles("br0", 0, 4)
            for i in range(2):
                sp.wait_ge(y_st[i], 16 * 64)
            sp.wait_ge(s_yst, 16 * NT)

            def mixer_in(b, k):
                if b:
                    sp.wait_ge(b_lo, KT * (b - 1) + k + 1)
                sp.dma_start(mixed(k), y_d[b, k]).then_inc(b_in[k], 16)

            for k in range(KT):
                mixer_in(0, k)
            for b in range(3):
                for k in range(KT):
                    n = KT * b + k
                    if n >= 2:
                        read_out(sp, first[f"br{b}"] + k - 2)
                    sp.dma_start(sqb[:, n % 2, :], gate_d[n]).then_inc(g_in[n % 2], 16)
                    if k < 4:
                        weight_tiles(f"br{b}", k + 4, k + 5)
                    elif b < 2:
                        weight_tiles(f"br{b + 1}", k - 4, k - 3)
                    if b < 2:
                        mixer_in(b + 1, k)
                if b == 0:
                    sp.dma_start(xT[:, :, :], x_d.rearrange("k p s -> p k s")).then_inc(x_back, 16)
            weight_tiles("out", 0, 4)
            sp.wait_ge(b_lo, 3 * KT)
            sp.dma_start(xkT[:, :, :], xk_d).then_inc(xkv_back, 16)
            sp.dma_start(xv[:, :, :], xv_d).then_inc(xkv_back, 16)
            weight_tiles("out", 4, 8)
            weights("xq")
            weights("xo")
            for c in range(0, FT, FC):
                weights(f"gu{c}")
                weights(f"dn{c}")
            for t in range(NT):
                sp.wait_ge(o_cp[t % 2], t // 2 + 1)
                sp.dma_start(out_rows[t], sqb[:, t % 2, :]).then_inc(o_st[t % 2], 16)
            for i in range(2):
                sp.wait_ge(o_st[i], 16 * NT // 2)

        @block.gpsimd
        def _(pool):
            pool.memset(prow[:, :], 0.0).then_inc(s_const, 1)
            pool.memset(ident[:, :], 0.0).then_inc(s_const, 1)
            pool.memset(ones[:, :], 1.0).then_inc(s_const, 1)
            pool.memset(bones[:, :], 0.0).then_inc(s_const, 1)
            pool.memset(cmask[:, :], 0.0).then_inc(s_const, 1)
            pool.wait_ge(s_const, 5)
            pool.affine_select(out=ident[:, :], in_=ident[:, :], compare_op=ALU.not_equal, fill=1.0, base=0,
                               pattern=[[-1, P]], channel_multiplier=1).then_inc(s_const, 1)
            pool.affine_select(out=tri[:, :], in_=ones[:, :], compare_op=ALU.is_ge, fill=0.0, base=0,
                               pattern=[[1, P]], channel_multiplier=-1).then_inc(s_const, 1)
            pool.affine_select(out=cmask[:, :], in_=cmask[:, :], compare_op=ALU.is_ge, fill=NEG, base=0,
                               pattern=[[1, P]], channel_multiplier=-1).then_inc(s_const, 1)
            for i in range(2):
                pool.wait_ge(s_const, 8 + i)
                pool.memset(bones[i * HD:(i + 1) * HD, i * HD:(i + 1) * HD], 1.0).then_inc(s_const, 1)

            def split(name):
                _, w, k0, kn, c0, width, count = next(x for x in plan if x[0] == name)
                t0 = first[name]

                def one(u, j):
                    raw, two = (t0 + u) % 4, (t0 + u) % 2
                    src = wraw[:, raw, 0:kn, 0:width]
                    hi, lo = WH[:, two, 0:kn, 0:width], WL[:, two, 0:kn, 0:width]
                    if t0 + u >= 2:
                        pool.wait_ge(mm, t0 + u - 1 + 4 * j)
                    pool.wait_ge(w_in[raw], 16 * ((t0 + u) // 4 + 1 + j))
                    pool.sem_inc(pool_go, 1)
                    pool.tensor_copy(hi, src).then_inc(w_hi, 1)
                    pool.wait_ge(w_hi, t0 + u + 1 + 4 * j)
                    pool.tensor_tensor(lo, src, hi.bitcast(F32), ALU.subtract).then_inc(w_lo, 1)

                if count % 4 == 0 and count > 4:
                    for u in range(4):
                        one(u, 0)
                    with pool.Fori(0, count // 4 - 1) as j:
                        for u in range(4, 8):
                            one(u, j)
                else:
                    for u in range(count):
                        one(u, 0)

            def stage(n, src, staged):
                pool.tensor_copy(qst[:, n % 2, :, :], src.unsqueeze(1).to_broadcast([P, 2, P])).then_inc(staged, 1)
                for h in range(2):
                    a, b = slice(h * HD, (h + 1) * HD), slice((1 - h) * HD, (2 - h) * HD)
                    pool.wait_ge(staged, 3 * n + 1 + h)
                    pool.tensor_tensor(qst[b, n % 2, h, :], src[a], qst[a, n % 2, h, :].bitcast(F32), ALU.subtract)\
                        .then_inc(staged, 1)
                pool.wait_ge(staged, 3 * n + 3)

            def stage_indexer():
                for m in range((NT - TOPK // P) * IDX_HEADS // 2):
                    if m == 0:
                        all_read_out(pool, first["gate"])
                    if m >= 2:
                        pool.wait_ge(ix_pe, 2 * m - 2)
                    t, p = TOPK // P + m // (IDX_HEADS // 2), m % (IDX_HEADS // 2)
                    stage(m, iqT[:, p, t * P:(t + 1) * P], ix_q)

            def stage_queries(q0):
                for q in range(q0, q0 + NT * PAIRS):
                    if q == q0:
                        pool.wait_ge(q_done, KT * (q0 // 64 + 1))
                    if q >= 2:
                        pool.wait_ge(a_s, 2 * q - 2)
                    t, p = (q - q0) // PAIRS, q % PAIRS
                    stage(q, qT[:, p, t * P:(t + 1) * P], a_q)

            pool.wait_ge(s_const, 10)
            for name in ("xk", "xv", "ikw", "ckv", "iq"):
                split(name)
            stage_indexer()
            for name in ("gate", "z", "q", "sk", "sv"):
                split(name)
            stage_queries(0)
            split("sq")
            stage_queries(64)
            for name in ("dt", "xbc"):
                split(name)
            def add_mask(n):
                pool.wait_ge(s_df, n + 1)
                pool.tensor_tensor(tmp[:, n % 2, 512:1024].rearrange("p (h l) -> p h l", h=4),
                                   tmp[:, n % 2, 0:512].rearrange("p (h l) -> p h l", h=4),
                                   cmask[:, :].unsqueeze(1).to_broadcast([P, 4, P]), ALU.add).then_inc(s_dm, 1)

            def gate(c):
                pool.wait_ge(s_ysum, c + 1)
                pool.wait_ge(s_ztok, c + 1)
                pool.tensor_tensor(yt[:, :], yt[:, :], ztok[:, :], ALU.mult).then_inc(s_yg, 1)

            for c in range(NT):
                add_mask(4 * c)
                add_mask(4 * c + 1)
                if c:
                    gate(c - 1)
                add_mask(4 * c + 2)
                add_mask(4 * c + 3)
                pool.wait_ge(s_xw, c + 1)
                pool.tensor_tensor(heads3(xtok[:, c % 2, :], HEADS), heads3(xtok[:, c % 2, :], HEADS),
                                   wide(dskip[:, :], [P, HEADS, HD]), ALU.mult).then_inc(s_skip, 1)
            gate(NT - 1)
            for name in ("br0", "br1", "br2", "out", "xq", "xo"):
                split(name)
            for c in range(0, FT, FC):
                split(f"gu{c}")
                split(f"dn{c}")

        @block.tensor
        def _(pe):
            def turn(i):
                _, tiles, _ = turns[i]
                for t in range(tiles):
                    q = turn_first[i] + t
                    pe.wait_ge(x_in[q % 2], 16 * (q // 2 + 1))
                    if q:
                        pe.wait_ge(x_cp, q)
                    for k in range(KT):
                        last = nc.tensor.transpose(psA[:, k * P:(k + 1) * P], tmp[:, q % 2, k * P:(k + 1) * P], ident[:, :])
                    last.then_inc(x_tr, 1)

            def halves(n):
                return [(h, min(h + 512, n)) for h in range(0, n, 512)]

            def norm(i):
                n, acc = norms[i][2], norms[i][4]
                pe.wait_ge(n_acc, (KT - 1) * (i + 1))
                for a, b in halves(n):
                    last = nc.tensor.matmul(psA[:, a:b], ones[:, :], acc[:, a:b], start=True, stop=True)
                last.then_inc(n_sum, 1)

            def channel_tile(i, j, hi=AH, lo=AL, kn=KT, n=S, ready=None):
                w = i % 2
                pe.wait_ge(w_lo, i + 1 + 2 * j)
                if i >= 2:
                    pe.wait_ge(free[w], i // 2 + j)
                if ready is None:
                    order = [(k, a, b) for a, b in halves(n) for k in range(kn)]
                else:
                    order = [(k, a, b) for k in range(kn) for a, b in halves(n)]
                for k, a, b in order:
                    if ready is not None and a == 0:
                        pe.wait_ge(ready[0], ready[1] + k + 1)
                    for x, (l, r) in enumerate(((WH, hi), (WH, lo), (WL, hi))):
                        last = nc.tensor.matmul(psG[:, w, a:b], l[:, w, k, :], r[:, k, a:b],
                                                start=(k == 0 and x == 0), stop=(k == kn - 1 and x == 2))
                last.then_inc(mm, 1)

            def token_tiles(i, width, tiles, hi, lo):
                w = i % 2
                pe.wait_ge(w_lo, i + 1)
                if i >= 2:
                    pe.wait_ge(free[w], i // 2)
                for t in range(tiles):
                    for k in range(KT):
                        for x, (l, r) in enumerate(((hi, WH), (lo, WH), (hi, WL))):
                            last = nc.tensor.matmul(psG[:, w, t * P:t * P + width], l[:, k, t * P:(t + 1) * P], r[:, w, k, 0:width],
                                                    start=(k == 0 and x == 0), stop=(k == KT - 1 and x == 2))
                last.then_inc(mm, 1)

            def token_turn(i, raw):
                pe.wait_ge(t_raw, i + 1)
                if i:
                    pe.wait_ge(t_out, i)
                for t in range(NT):
                    last = nc.tensor.transpose(psA[:, t * P:(t + 1) * P], raw[:, t * P:(t + 1) * P], ident[:, :])
                last.then_inc(t_tr, 1)

            def gemm(name, ready=None, **kw):
                count = next(x for x in plan if x[0] == name)[-1]
                t0 = first[name]
                channel_tile(t0, 0, ready=ready, **kw)
                channel_tile(t0 + 1, 0, **kw)
                if count > 2:
                    with pe.Fori(0, count // 2 - 1) as j:
                        for u in (2, 3):
                            channel_tile(t0 + u, j, **kw)

            def key_prep(i):
                pe.wait_ge(kp_step, 10 * i + 6)
                for t in range(NT):
                    last = nc.tensor.transpose(psA[:, t * P:(t + 1) * P], rst[:, t * P:(t + 1) * P], ident[:, :])
                last.then_inc(kp_step, 1)

            def normed(name, i0, n, over, sq, ssum, ln, tiles_each, squares=sqb, ready=None, **kw):
                t0 = first[name]

                def sums(u, j):
                    pe.wait_ge(sq, i0 + u + 1 + 2 * j)
                    if u % tiles_each == 0 and i0 + u >= tiles_each:
                        pe.wait_ge(ln, (i0 + u) // tiles_each + j * (2 // tiles_each))
                    for a, b in halves(n):
                        last = nc.tensor.matmul(psA[:, a:b], over[:, :], squares[:, u % 2, a:b], start=(u % tiles_each == 0),
                                                stop=(u % tiles_each == tiles_each - 1))
                    last.then_inc(ssum, 1)

                def step(u, j):
                    channel_tile(t0 + u, j, n=n, **kw)
                    sums(u - 1, j)

                channel_tile(t0, 0, n=n, ready=ready, **kw)
                step(1, 0)
                step(2, 0)
                with pe.Fori(0, KT // 2 - 2) as j:
                    step(3, j)
                    step(4, j)
                channel_tile(t0 + KT - 1, 0, n=n, **kw)
                sums(KT - 2, 0)
                sums(KT - 1, 0)

            def keys(q, kind, t):
                return (0, t + 1) if kind == "dsa" else (max(0, t - 1), min(t + 1, 2))

            def products(dst, slot, h, hi, lo):
                r = slice(h * HD, (h + 1) * HD)
                for a, b in halves(hi.shape[1]):
                    nc.tensor.matmul(dst[:, a:b], qst[:, slot, h, :], hi[:, a:b], start=True, stop=False)
                    last = nc.tensor.matmul(dst[:, a:b], qst[r, slot, h, :], lo[r, a:b], start=False, stop=True)
                return last

            def att_scores(q, h, pp, kind, t, p, first_static):
                k0, nb = keys(q, kind, t)
                pe.wait_ge(a_q, 3 * (q + 1) + 3 * pp)
                if first_static >= 2:
                    pe.wait_ge(a_mx0, 2 * q + h - 1 + 2 * pp)
                i = 0 if kind == "dsa" else 1 + p // (PAIRS // 2)
                products(psG[:, h, 0:nb * P], q % 2, h, kh[:, i, k0 * P:(k0 + nb) * P], kl[:, i, k0 * P:(k0 + nb) * P]).then_inc(a_s, 1)

            def att_turn(q, h, pp, kind, t):
                pe.wait_ge(a_exp, 2 * q + h + 1 + 2 * pp)
                for bank, b0, b1, n in turns_of(kind, q, h, t, keys(q, kind, t)[1]):
                    if n:
                        pe.wait_ge(a_cp[bank], n + (2 if long(kind, t) else 1) * pp)
                    for b in range(b0, b1):
                        last = nc.tensor.transpose(psA[:, bank * 512 + (b - b0) * P:bank * 512 + (b - b0 + 1) * P],
                                                   tmp[:, h, b * P:(b + 1) * P], ident[:, :])
                    last.then_inc(a_t[bank], 1)

            def att_values(q, h, pp, kind, t, p):
                k0, nb = keys(q, kind, t)
                if 2 * q + h >= 4:
                    pe.wait_ge(a_oc, q - 1 + pp)
                o = (psB, psC)[q % 2][:, h * HD:(h + 1) * HD]
                for bank, b0, b1, n in turns_of(kind, q, h, t, nb):
                    pe.wait_ge(a_cp[bank], n + 1 + (2 if long(kind, t) else 1) * pp)
                    for b in range(b0, b1):
                        if kind == "dsa":
                            v = kvt[:, b, HD:2 * HD]
                        else:
                            v = svt[:, k0 + b, (p // 4) * HD:(p // 4 + 1) * HD]
                        last = nc.tensor.matmul(o, sqb[:, h, b * P:(b + 1) * P], v, start=(b == 0), stop=(b == nb - 1))
                last.then_inc(a_pv, 1)

            def att_out(q, pp):
                pe.wait_ge(a_o, q + 1 + pp)
                nc.tensor.transpose((psB, psC)[q % 2][:, P:2 * P], otok[:, q % 2, :], ident[:, :]).then_inc(a_ot, 1)

            def attention(kind, q0):
                def pair(q, pp, t, p, before, after):
                    att_scores(q, 1, pp, kind, t, p, 2 * q + 1)
                    att_turn(q, 0, pp, kind, t)
                    if before is not None:
                        att_values(q - 1, 1, pp, kind, *before)
                    if after is not None:
                        att_scores(q + 1, 0, pp, kind, *after, 2 * q + 2)
                    att_values(q, 0, pp, kind, t, p)
                    att_turn(q, 1, pp, kind, t)
                    if before is not None:
                        att_out(q - 1, pp)

                att_scores(q0, 0, 0, kind, 0, 0, 2 * q0)
                for t in range(NT):
                    q = q0 + PAIRS * t
                    pair(q, 0, t, 0, (t - 1, PAIRS - 1) if t else None, (t, 1))
                    if kind == "dsa" and t:
                        with pe.Fori(0, PAIRS // 2 - 1) as j:
                            for u in (1, 2):
                                pair(q + u, 2 * j, t, u, (t, u - 1), (t, u + 1))
                    else:
                        for p in range(1, PAIRS - 1):
                            pair(q + p, 0, t, p, (t, p - 1), (t, p + 1))
                    pair(q + PAIRS - 1, 0, t, PAIRS - 1, (t, PAIRS - 2), (t + 1, 0) if t < NT - 1 else None)
                q = q0 + NT * PAIRS - 1
                att_values(q, 1, 0, kind, NT - 1, PAIRS - 1)
                att_out(q, 0)

            pe.wait_ge(s_const, 10)
            pe.wait_ge(s_par, 16 * PARAMS)
            nc.tensor.transpose(psB[:, 0:P], prow[:, :], ident[:, :]).then_inc(s_pcol, 1)
            turn(0)
            pe.wait_ge(x_cp, MT)
            norm(0)
            pe.wait_ge(n_rstd, 1)
            turn(1)
            pe.wait_ge(x_cp, MT + NT)
            normed("xk", 0, N_MEM, ones, xk_sq, xk_sum, xk_ln, 2, squares=msq, ready=(n_lo, 0), hi=MH, lo=ML)
            pe.wait_ge(xk_ln, XH)
            norm(1)
            for i in range(KT):
                token_tiles(first["xv"] + i, P, MT, MH, ML)
            channel_tile(first["ikw"], 0, ready=(n_lo, KT))
            gemm("ckv")
            token_turn(0, tmp[:, 1, :])
            all_read_out(pe, first["iq"])
            for t in range(NT):
                for k in range(2):
                    nc.tensor.matmul(psB[:, t:t + 1], sqb[:, k, t * P:(t + 1) * P], ones[:, 0:1], start=(k == 0), stop=(k == 1))
            pe.wait_ge(t_out, 1)
            for t in range(NT):
                for k in range(2):
                    last = nc.tensor.matmul(psA[:, t * P:(t + 1) * P], ckvT[:, k, t * P:(t + 1) * P], wukv[:, k, :],
                                            start=(k == 0), stop=(k == 1))
            last.then_inc(kv_pe, 1)
            channel_tile(first["iq"], 0)
            channel_tile(first["iq"] + 1, 0)
            pe.wait_ge(ik_step, 10)
            pe.wait_ge(kv_done, 1)
            for t in range(NT):
                last = nc.tensor.transpose(psA[:, t * P:(t + 1) * P], ikd[:, t * P:(t + 1) * P], ident[:, :])
            last.then_inc(ik_step, 1)
            channel_tile(first["iq"] + 2, 0)
            key_prep(0)
            channel_tile(first["iq"] + 3, 0)
            pe.wait_ge(ik_step, 14)
            all_read_out(pe, first["gate"])
            for v, (t, h) in enumerate(ix_units):
                if v >= 2:
                    pe.wait_ge(ix_relu, v - 1)
                pe.wait_ge(ix_q, 3 * (v // 2 + 1))
                n = (t + 1) * P
                products(psG[:, v % 2, 0:n], v // 2 % 2, h % 2, ikh[:, 0:n], ikl[:, 0:n]).then_inc(ix_pe, 1)
            pe.wait_ge(ix_relu, len(ix_units))
            gemm("gate")
            gemm("z")
            normed("q", 0, S, bones, q_sq, q_sum, q_ln, 1)
            channel_tile(first["sk"], 0)
            channel_tile(first["sv"], 0)
            pe.wait_ge(q_ln, KT)
            token_turn(1, tmp[:, 0, :])
            token_turn(2, sqb[:, 0, :])
            pe.wait_ge(t_out, 3)
            key_prep(1)
            key_prep(2)
            all_read_out(pe, first["sq"])
            pe.wait_ge(kp_step, 30)
            attention("dsa", 0)
            pe.wait_ge(a_mx0, 128)
            normed("sq", KT, S, bones, q_sq, q_sum, q_ln, 1)
            all_read_out(pe, first["dt"])
            pe.wait_ge(q_ln, 2 * KT)
            attention("swa", 64)
            pe.wait_ge(a_mx0, 256)
            channel_tile(first["dt"], 0)
            token_turn(3, tmp[:, 0, :])
            gemm("xbc")
            pe.wait_ge(dt_step, 6)
            pe.wait_ge(a_o, 128)
            a_all = dts[:, 1, :, :].rearrange("p t h -> p (t h)")
            nc.tensor.matmul(psB[:, 0:P], tri[:, :], a_all, start=True, stop=True)
            nc.tensor.matmul(psB[:, P:2 * P], ones[:, :], a_all, start=True, stop=True).then_inc(dt_step, 1)
            pe.wait_ge(cv_out, XC)
            pe.wait_ge(dt_step, 13)
            pe.wait_ge(a_oc, 128)
            all_read_out(pe, first["br0"])
            def decays(n):
                c, q = n // 4, n % 4
                if n >= 2:
                    pe.wait_ge(s_df, n - 1)
                for i in range(4):
                    h = 4 * q + i
                    last = nc.tensor.matmul((psB, psC)[n % 2][:, i * P:(i + 1) * P], dts[:, 1, c, h:h + 1].to_broadcast([P, P]),
                                            tri[:, :], start=True, stop=True)
                last.then_inc(s_bc, 1)

            def within(n):
                c, q = n // 4, n % 4
                pe.wait_ge(s_m, n + 1)
                if q == 0:
                    pe.wait_ge(s_xdt, c + 1)
                for i in range(4):
                    h = 4 * q + i
                    last = nc.tensor.matmul(psG[:, 0, h * HD:(h + 1) * HD], sqb[:, n % 2, 512 + i * P:512 + (i + 1) * P],
                                            xdt[:, h * HD:(h + 1) * HD], start=True, stop=True)
                last.then_inc(s_yd, 1)

            def added(c, g):
                nc.tensor.matmul(psA[:, g * 512:(g + 1) * 512], btok[:, g * P:(g + 1) * P], xw[:, g * 512:(g + 1) * 512],
                                 start=True, stop=True).then_inc(s_upd, 1)

            def y_turn(c):
                pe.wait_ge(s_yn, 2 * c + 2)
                for k in range(KT):
                    last = nc.tensor.transpose(psG[:, 1, k * P:(k + 1) * P], yt[:, k * P:(k + 1) * P], ident[:, :])
                last.then_inc(s_ytr, 1)

            for c in range(NT):
                cc = slice(c * P, (c + 1) * P)
                decays(4 * c)
                decays(4 * c + 1)
                if c:
                    pe.wait_ge(s_y, c)
                for k in range(KT):
                    last = nc.tensor.transpose(psG[:, 0, k * P:(k + 1) * P], xcT[:, k, cc], ident[:, :])
                last.then_inc(s_xt, 1)
                if c:
                    pe.wait_ge(s_stt, 2 * c - 1)
                for g in range(GROUPS):
                    last = nc.tensor.transpose(psA[:, g * P:(g + 1) * P], xcT[:, KT + g, cc], ident[:, :])
                last.then_inc(s_bt, 1)
                if c:
                    pe.wait_ge(s_stt, 2 * c)
                for g in range(GROUPS):
                    last = nc.tensor.matmul(psA[:, 512 + g * P:512 + (g + 1) * P], xcT[:, KT + g, cc],
                                            xcT[:, KT + GROUPS + g, cc], start=True, stop=True)
                last.then_inc(s_g, 1)
                within(4 * c)
                decays(4 * c + 2)
                within(4 * c + 1)
                decays(4 * c + 3)
                if c:
                    y_turn(c - 1)
                    pe.wait_ge(s_ycp, c)
                pe.wait_ge(s_zin, 16 * (c + 1))
                for k in range(KT):
                    last = nc.tensor.transpose(psG[:, 1, k * P:(k + 1) * P], zt[:, k, :], ident[:, :])
                last.then_inc(s_zt, 1)
                within(4 * c + 2)
                if c < NT - 1:
                    pe.wait_ge(s_btok, c + 1)
                    pe.wait_ge(s_xw, c + 1)
                    added(c, 0)
                if c:
                    pe.wait_ge(s_ztok, c + 1)
                    for g in range(GROUPS):
                        last = nc.tensor.matmul(psG[:, 1, g * 512:(g + 1) * 512], xcT[:, KT + GROUPS + g, cc],
                                                st[:, g * 512:(g + 1) * 512], start=True, stop=True)
                    last.then_inc(s_yo, 1)
                within(4 * c + 3)
                if c < NT - 1:
                    added(c, 1)
            y_turn(NT - 1)
            pe.wait_ge(s_ycp, NT)
            for b in range(3):
                gemm(f"br{b}", ready=(b_lo, KT * b))
            gemm("out", ready=(b_lo, 3 * KT))
            norm(2)
            normed("xq", KT, S, ones, xk_sq, xk_sum, xk_ln, 2, ready=(n_lo, 2 * KT))
            units = NT * XH
            pe.wait_ge(xk_done, 4 * XH)
            pe.wait_ge(xkv_back, 32)
            all_read_out(pe, first["xo"])

            def cross(w):
                return slice((w // XH) * P, (w // XH + 1) * P), w % XH, w % 2

            for w in range(units + 3):
                if w < units:
                    tt, h, z = cross(w)
                    if w >= 2:
                        pe.wait_ge(c_exp, w - 1)
                    for i in range(2):
                        last = nc.tensor.matmul(psG[:, z, 0:N_MEM], xqT[:, 2 * h + i, tt], xkT[:, 2 * h + i, :],
                                                start=(i == 0), stop=(i == 1))
                    last.then_inc(c_s, 1)
                if 1 <= w <= units:
                    tt, h, z = cross(w - 1)
                    pe.wait_ge(c_exp, w)
                    if w >= 3:
                        pe.wait_ge(c_cp, w - 2)
                    for i in range(MT):
                        last = nc.tensor.transpose(psA[:, z * 512 + i * P:z * 512 + (i + 1) * P],
                                                   sqb[:, z, i * P:(i + 1) * P], ident[:, :])
                    last.then_inc(c_t, 1)
                if 2 <= w <= units + 1:
                    tt, h, z = cross(w - 2)
                    pe.wait_ge(c_cp, w - 1)
                    if w >= 4:
                        pe.wait_ge(c_o, w - 3)
                    for i in range(MT):
                        last = nc.tensor.matmul((psB, psC)[z][:, 0:XD], tmp[:, z, i * P:(i + 1) * P],
                                                xv[:, i, h * XD:(h + 1) * XD], start=(i == 0), stop=(i == MT - 1))
                    last.then_inc(c_pv, 1)
                if 3 <= w:
                    tt, h, z = cross(w - 3)
                    pe.wait_ge(c_o, w - 2)
                    if w >= 5:
                        pe.wait_ge(c_lo, w - 4)
                    for i in range(2):
                        last = nc.tensor.transpose(psG[:, z, 512 + i * P:512 + (i + 1) * P],
                                                   tmp[:, z, 512 + i * P:512 + (i + 1) * P], ident[:, :])
                    last.then_inc(c_ot, 1)
            pe.wait_ge(c_lo, units)
            gemm("xo")
            norm(3)
            for c in range(0, FT, FC):
                gemm(f"gu{c}", ready=None if c else (n_lo, 3 * KT))
                gemm(f"dn{c}", ready=(f_lo, c), hi=HH, lo=HL, kn=min(FC, FT - c))
            all_read_out(pe, n_tiles)
            for t in range(NT):
                if t >= 2:
                    pe.wait_ge(o_cp[t % 2], t // 2)
                for k in range(KT):
                    last = nc.tensor.transpose(psG[:, t % 2, k * P:(k + 1) * P], xT[:, k, t * P:(t + 1) * P], ident[:, :])
                last.then_inc(o_tr, 1)


        @block.scalar
        def _(act):
            def norm_squares(i):
                src, _, n, sq, acc = norms[i][:5]
                if i < 2:
                    act.wait_ge(x_cp, turn_first[i] + turns[i][1])
                for k in range(KT):
                    if i >= 2:
                        read_out(act, first["out" if i == 2 else "xo"] + k)
                    if k >= 3:
                        act.wait_ge(n_acc, (KT - 1) * i + k - 2)
                    act.activation(sq[:, k % 2, 0:n] if k else acc[:, 0:n], src[:, k, 0:n], ACT.Square).then_inc(n_sq, 1)

            def norm_root(i):
                n, acc = norms[i][2], norms[i][4]
                act.wait_ge(n_sum, i + 1)
                act.activation(acc[:, 0:n], psA[:, 0:n], ACT.Ln, scale=1.0 / D, bias=EPS).then_inc(n_rstd, 1)
                act.wait_ge(n_rstd, 2 * i + 1)
                act.activation(acc[:, 0:n], acc[:, 0:n], ACT.Exp, scale=-0.5).then_inc(n_rstd, 1)
                if i >= 2:
                    act.wait_ge(mm, first["xq" if i == 2 else "gu0"])

            def norm_round(i, k):
                n, scaled, hi = norms[i][2], norms[i][5], norms[i][6]
                act.wait_ge(n_out, KT * i + k + 1)
                act.activation(hi[:, k, 0:n], scaled[:, k % 2, 0:n], ACT.Copy).then_inc(n_hi, 1)

            def norm(i):
                norm_squares(i)
                norm_root(i)
                for k in range(KT):
                    norm_round(i, k)

            def stored(name, func, dst, m0):
                t0 = first[name]
                count = next(x for x in plan if x[0] == name)[-1]

                def pair(us, j):
                    for u in us:
                        w, z = (t0 + u) % 2, (m0 + u) % 2
                        act.wait_ge(mm, t0 + u + 1 + 2 * j)
                        if m0 + u >= 2:
                            act.wait_ge(g_st[z], 16 * ((m0 + u) // 2 + j))
                        act.activation(sqb[:, z, :], psG[:, w, :], func).then_inc(free[w], 1)
                        act.wait_ge(free[w], (t0 + u) // 2 + 1 + j)
                        act.dma_start(dst[bass.ds(u + 2 * j, 1)].rearrange("a p s -> (a p) s"), sqb[:, z, :]).then_inc(g_st[z], 16)

                pair((0, 1), 0)
                with act.Fori(0, count // 2 - 1) as j:
                    pair((2, 3), j)

            def head_norms(name, i0, n, sq, ssum, ln, rstd, done, each, scale, squares=sqb, root_of=rst):
                t0 = first[name]

                def square(u, j):
                    act.wait_ge(mm, t0 + u + 1 + 2 * j)
                    if i0 + u >= 2:
                        act.wait_ge(ssum, i0 + u - 1 + 2 * j)
                    act.activation(squares[:, u % 2, 0:n], psG[:, (t0 + u) % 2, 0:n], ACT.Square).then_inc(sq, 1)

                def root(u, j):
                    if u % each != each - 1:
                        return
                    g = (i0 + u) // each
                    gj = j * (2 // each)
                    act.wait_ge(ssum, i0 + u + 1 + 2 * j)
                    if g >= 1:
                        act.wait_ge(done, g * each + gj * each)
                    act.activation(root_of[:, 0:n], psA[:, 0:n], ACT.Ln, scale=scale, bias=EPS).then_inc(ln, 1)
                    act.wait_ge(ln, g + 1 + gj)
                    act.activation(root_of[:, 0:n], root_of[:, 0:n], ACT.Exp, scale=-0.5).then_inc(rstd, 1)

                square(0, 0)
                for u in (1, 2):
                    square(u, 0)
                    root(u - 1, 0)
                with act.Fori(0, KT // 2 - 2) as j:
                    for u in (3, 4):
                        square(u, j)
                        root(u - 1, j)
                square(KT - 1, 0)
                root(KT - 2, 0)
                root(KT - 1, 0)

            def key_root(i):
                act.wait_ge(kp_step, 10 * i + 2)
                act.activation(small[:, 8:16], small[:, 0:8], ACT.Ln, scale=1.0 / HD, bias=EPS).then_inc(kp_step, 1)
                act.wait_ge(kp_step, 10 * i + 3)
                act.activation(small[:, 8:16], small[:, 8:16], ACT.Exp, scale=-0.5).then_inc(kp_step, 1)
                act.wait_ge(kp_step, 10 * i + 8)
                act.activation(kh[:, i, :], rst[:, :], ACT.Copy).then_inc(kp_step, 1)

            def token_raw(i, name, raw):
                act.wait_ge(mm, first[name] + 1)
                act.activation(raw, psG[:, first[name] % 2, :], ACT.Copy).then_inc(t_raw, 1)
                act.wait_ge(t_raw, i + 1)
                act.sem_inc(free[first[name] % 2], 1)

            def token_out(i, dst, width):
                act.wait_ge(t_tr, i + 1)
                act.activation(dst, heads3(psA[:, :])[:, :, 0:width], ACT.Copy).then_inc(t_out, 1)

            nc.scalar.preload_act_table_set("natural_log_exp_and_others")
            act.wait_ge(s_par, 16 * PARAMS)
            act.activation(alog[:, :], alog[:, :], ACT.Exp).then_inc(s_alog, 1)
            norm(0)
            norm_squares(1)
            head_norms("xk", 0, N_MEM, xk_sq, xk_sum, xk_ln, xk_rstd, xk_done, 2, 1.0 / XD, msq, mrst)
            norm_root(1)
            for k in range(KT):
                norm_round(1, k)
                i = first["xv"] + k
                act.wait_ge(mm, i + 1)
                act.activation(xv0[:, :, k * P:(k + 1) * P], heads3(psG[:, i % 2, 0:MT * P], MT), ACT.Copy).then_inc(free[i % 2], 1)
            act.wait_ge(xk_done, KT)
            act.dma_start(xk_d, xk0[:, :, :]).then_inc(m_st, 16)
            all_read_out(act, first["ikw"])
            act.dma_start(xv_d, xv0[:, :, :]).then_inc(m_st, 16)
            act.wait_ge(n_lo, 2 * KT)
            token_raw(0, "ikw", tmp[:, 1, :])
            act.wait_ge(m_st, 48)
            for k in range(2):
                act.wait_ge(mm, first["ckv"] + k + 1)
                act.activation(sqb[:, k, :], psG[:, (first["ckv"] + k) % 2, :], ACT.Square).then_inc(kv_sq, 1)
            token_out(0, heads3(tmp[:, 0, :])[:, :, 0:IKW], IKW)

            def iq_out(k):
                i = first["iq"] + k
                act.wait_ge(mm, i + 1)
                act.activation(iqT[:, k, :], psG[:, i % 2, :], ACT.Copy).then_inc(free[i % 2], 1)

            act.wait_ge(kv_pe, 1)
            act.activation(small[:, 0:8], psB[:, 0:NT], ACT.Ln, scale=1.0 / KV_RANK, bias=EPS).then_inc(kv_ln, 1)
            act.wait_ge(kv_ln, 1)
            act.activation(small[:, 0:8], small[:, 0:8], ACT.Exp, scale=-0.5).then_inc(kv_ln, 1)
            act.wait_ge(ik_step, 5)
            act.activation(small[:, 24:32], small[:, 16:24], ACT.Ln, scale=1.0 / HD, bias=EPS).then_inc(ik_step, 1)
            act.wait_ge(ik_step, 6)
            act.activation(small[:, 24:32], small[:, 24:32], ACT.Exp, scale=-0.5).then_inc(ik_step, 1)
            iq_out(0)
            iq_out(1)
            act.wait_ge(ik_step, 12)
            act.activation(ikh, ikd, ACT.Copy).then_inc(ik_step, 1)
            key_root(0)
            iq_out(2)
            iq_out(3)
            for v, (t, h) in enumerate(ix_units):
                n = (t + 1) * P
                act.wait_ge(ix_pe, v + 1)
                if v >= 2:
                    act.wait_ge(ix_acc, v - 1)
                else:
                    act.wait_ge(kp_step, 6)
                act.activation(tmp[:, v % 2, 0:n], psG[:, v % 2, 0:n], ACT.Relu).then_inc(ix_relu, 1)
            stored("gate", ACT.Sigmoid, gate_d, 0)
            stored("z", ACT.Silu, z_d, 24)
            nc.scalar.preload_act_table_set("natural_log_exp_and_others")
            for i in range(2):
                act.wait_ge(g_st[i], 16 * 16)
            head_norms("q", 0, S, q_sq, q_sum, q_ln, q_rstd, q_done, 1, 1.0 / HD)
            act.wait_ge(q_done, KT)
            token_raw(1, "sk", tmp[:, 0, :])
            token_raw(2, "sv", sqb[:, 0, :])
            token_out(1, heads3(tmp[:, 1, :]), P)
            token_out(2, svt[:, :, :], P)
            key_root(1)
            key_root(2)

            def att_exp(q, h, pp, n, swa):
                act.wait_ge(a_mx, 2 * q + h + 1 + 2 * pp)
                act.activation(tmp[:, h, 0:n], tmp[:, h, 0:n], ACT.Exp, bias=stat[:, h, 0:1], scale=AT_SCALE,
                               accum_out=stat[:, q % 2, 4 + h:5 + h]).then_inc(a_exp, 1)
                if swa is not None:
                    act.activation(stat[:, q % 2, 6 + h:7 + h], nsink[:, swa + h:swa + h + 1], ACT.Exp,
                                   bias=stat[:, h, 0:1], scale=-1.0).then_inc(a_snk, 1)

            def att_copy(q, h, pp, kind, t):
                for bank, b0, b1, n in turns_of(kind, q, h, t, nk(kind, t) // P):
                    if bank == 0:
                        act.wait_ge(a_t[0], n + 1 + (2 if long(kind, t) else 1) * pp)
                        if q > 0:
                            act.wait_ge(a_pv, 2 * q + h - 1 + 2 * pp)
                        act.activation(sqb[:, h, b0 * P:b1 * P], psA[:, 0:(b1 - b0) * P], ACT.Copy).then_inc(a_cp[0], 1)

            def att_store(q, pp, b, t, p):
                z = q % 2
                act.wait_ge(a_ot, q + 1 + pp)
                if q >= 2:
                    act.wait_ge(y_st[z], 16 * (q // 2) + 8 * pp)
                act.activation(oT[:, z, :], (psB, psC)[z][:, P:2 * P], ACT.Copy).then_inc(a_oc, 1)
                act.wait_ge(a_oc, q + 1 + pp)
                act.dma_start(y_d[b, bass.ds(p + pp, 1), :, t * P:(t + 1) * P].rearrange("a p s -> (a p) s"), oT[:, z, :])\
                    .then_inc(y_st[z], 16)

            def attention(kind, q0, b):
                def sink(p):
                    return 2 * p if kind == "swa" else None

                def pair(q, pp, t, p, before, after):
                    att_copy(q, 0, pp, kind, t)
                    att_exp(q, 1, pp, nk(kind, t), sink(p))
                    if after is not None:
                        att_exp(q + 1, 0, pp, nk(kind, after[0]), sink(after[1]))
                    att_copy(q, 1, pp, kind, t)
                    if before is not None:
                        att_store(q - 1, pp, b, *before)

                att_exp(q0, 0, 0, nk(kind, 0), sink(0))
                for t in range(NT):
                    q = q0 + PAIRS * t
                    pair(q, 0, t, 0, (t - 1, PAIRS - 1) if t else None, (t, 1))
                    if kind == "dsa" and t:
                        with act.Fori(0, PAIRS // 2 - 1) as j:
                            for u in (1, 2):
                                pair(q + u, 2 * j, t, u, (t, u - 1), (t, u + 1))
                    else:
                        for p in range(1, PAIRS - 1):
                            pair(q + p, 0, t, p, (t, p - 1), (t, p + 1))
                    pair(q + PAIRS - 1, 0, t, PAIRS - 1, (t, PAIRS - 2), (t + 1, 0) if t < NT - 1 else None)
                att_store(q0 + NT * PAIRS - 1, 0, b, NT - 1, PAIRS - 1)

            act.wait_ge(masked, NT)
            attention("dsa", 0, 0)
            head_norms("sq", KT, S, q_sq, q_sum, q_ln, q_rstd, q_done, 1, 1.0 / HD)
            attention("swa", 64, 1)
            for i in range(2):
                act.wait_ge(y_st[i], 16 * 64)
            token_raw(3, "dt", tmp[:, 0, :])
            token_out(3, dts[:, 0, :, :], HEADS)
            act.wait_ge(dt_step, 2)
            act.activation(dts[:, 5, :, :], dts[:, 5, :, :], ACT.Exp, scale=-1.0).then_inc(dt_step, 1)
            act.wait_ge(dt_step, 3)
            act.activation(dts[:, 5, :, :], dts[:, 5, :, :], ACT.Ln, bias=1.0).then_inc(dt_step, 1)
            with act.Fori(0, XC // 2) as j:
                for u in range(2):
                    i = first["xbc"] + u
                    act.wait_ge(free[i % 2], i // 2 + 1 + j)
                    act.activation(xcT[:, bass.ds(u + 2 * j, 1), :].rearrange("p a s -> p (a s)"), tmp[:, u, :], ACT.Silu)\
                        .then_inc(cv_out, 1)
            nc.scalar.preload_act_table_set("natural_log_exp_and_others")
            act.wait_ge(dt_step, 9)
            ends = psB[:, P:2 * P].rearrange("p (t h) -> p t h", t=NT)
            act.activation(dts[:, 3, :, :], ends, ACT.Exp).then_inc(dt_step, 1)
            act.wait_ge(dt_step, 10)
            act.activation(dts[:, 4, :, :], dts[:, 2, :, :], ACT.Exp).then_inc(dt_step, 1)
            act.wait_ge(dt_step, 11)
            act.activation(dts[:, 5, :, :], dts[:, 5, :, :], ACT.Exp).then_inc(dt_step, 1)
            def decay(n):
                act.wait_ge(s_dm, n + 1)
                if n >= 2:
                    act.wait_ge(s_m, n - 1)
                act.activation(sqb[:, n % 2, 0:512], tmp[:, n % 2, 512:1024], ACT.Exp).then_inc(s_e, 1)

            def y_root(c):
                act.wait_ge(s_yg, c + 1)
                for g in range(GROUPS):
                    half = slice(g * 512, (g + 1) * 512)
                    act.activation(yoff[:, half], yt[:, half], ACT.Square, accum_out=small[:, 32 + g:33 + g]).then_inc(s_ss, 1)
                act.wait_ge(s_ss, 2 * c + 2)
                act.activation(small[:, 34:36], small[:, 32:34], ACT.Ln, scale=1.0 / 512, bias=EPS).then_inc(s_rs, 1)
                act.wait_ge(s_rs, 2 * c + 1)
                act.activation(small[:, 34:36], small[:, 34:36], ACT.Exp, scale=-0.5).then_inc(s_rs, 1)

            def y_norm(c):
                act.wait_ge(s_rs, 2 * c + 2)
                for g in range(GROUPS):
                    yg = yt[:, g * 512:(g + 1) * 512]
                    act.activation(yg, yg, ACT.Copy, scale=small[:, 34 + g:35 + g]).then_inc(s_yn, 1)

            def y_store(c):
                act.wait_ge(s_ycp, c + 1)
                act.dma_start(y_d[2, :, :, c * P:(c + 1) * P].rearrange("k p s -> p k s"), heads3(rst[:, :])).then_inc(s_yst, 16)

            for c in range(NT):
                act.wait_ge(s_xt, c + 1)
                if c >= 2:
                    act.wait_ge(s_y, c - 1)
                act.activation(xtok[:, c % 2, :], psG[:, 0, :], ACT.Copy).then_inc(s_xtok, 1)
                act.wait_ge(s_bt, c + 1)
                if c:
                    act.wait_ge(s_upd, 2 * c)
                act.activation(btok[:, :], psA[:, 0:2 * STATE], ACT.Copy).then_inc(s_btok, 1)
                decay(4 * c)
                decay(4 * c + 1)
                if c:
                    y_root(c - 1)
                decay(4 * c + 2)
                if c:
                    y_norm(c - 1)
                decay(4 * c + 3)
                act.wait_ge(s_zt, c + 1)
                if c:
                    act.wait_ge(s_yg, c)
                act.activation(ztok[:, :], psG[:, 1, :], ACT.Copy).then_inc(s_ztok, 1)
                if c:
                    y_store(c - 1)
            y_root(NT - 1)
            y_norm(NT - 1)
            y_store(NT - 1)
            for b in range(4):
                act.wait_ge(mm, first[("br0", "br1", "br2", "out")[b]])
                for k in range(KT):
                    n = KT * b + k
                    if b < 3:
                        act.wait_ge(b_in[k], 16 * (b + 1))
                    else:
                        act.wait_ge(m_add, KT + k + 1)
                    src = mixed(k) if b < 3 else merged[:, k, :]
                    act.activation(AH[:, k, :], src, ACT.Copy).then_inc(b_hi, 1)
            norm(2)
            head_norms("xq", KT, S, xk_sq, xk_sum, xk_ln, xk_rstd, xk_done, 2, 1.0 / XD)
            units = NT * XH
            for w in range(units + 3):
                if w < units:
                    z = w % 2
                    act.wait_ge(c_mx, w + 1)
                    if w >= 2:
                        act.wait_ge(c_t, w - 1)
                    act.activation(sqb[:, z, 0:N_MEM], psG[:, z, 0:N_MEM], ACT.Exp, bias=small[:, 40 + z:41 + z],
                                   scale=XA_SCALE, accum_out=small[:, 42 + z:43 + z]).then_inc(c_exp, 1)
                if 1 <= w <= units:
                    z = (w - 1) % 2
                    act.wait_ge(c_t, w)
                    if w >= 3:
                        act.wait_ge(c_pv, w - 2)
                    act.activation(tmp[:, z, 0:N_MEM], psA[:, z * 512:z * 512 + N_MEM], ACT.Copy).then_inc(c_cp, 1)
                if w >= 3:
                    t, h, z = (w - 3) // XH, (w - 3) % XH, (w - 3) % 2
                    act.wait_ge(c_ot, w - 2)
                    act.activation(AH[:, 2 * h:2 * h + 2, t * P:(t + 1) * P], heads3(psG[:, z, 512:768], 2), ACT.Copy)\
                        .then_inc(c_hi, 1)
            norm(3)
            for c in range(0, FT, FC):
                t0 = first[f"gu{c}"]
                for k in range(min(FC, FT - c)):
                    n = c + k
                    act.wait_ge(mm, t0 + 2 * k + 1)
                    if n >= 2:
                        read_out(act, up_tile(n - 2))
                    act.activation(sqb[:, n % 2, :], psG[:, (t0 + 2 * k) % 2, :], ACT.Silu).then_inc(free[(t0 + 2 * k) % 2], 1)
                    read_out(act, up_tile(n))
                    act.activation(HH[:, k, :], tmp[:, n % 2, :], ACT.Copy).then_inc(f_hi, 1)
            for t in range(0, NT, 2):
                act.wait_ge(o_tr, t + 1)
                if t:
                    act.wait_ge(o_st[0], 16 * (t // 2))
                act.activation(sqb[:, 0, :], psG[:, 0, :], ACT.Copy).then_inc(o_cp[0], 1)

        @block.vector
        def _(dve):
            def turn(i):
                _, tiles, dst = turns[i]
                for t in range(tiles):
                    q = turn_first[i] + t
                    dve.wait_ge(x_tr, q + 1)
                    dve.tensor_copy(dst[:, :, t * P:(t + 1) * P], heads3(psA[:, :])).then_inc(x_cp, 1)

            def add_squares(i, k):
                n, sq, acc = norms[i][2:5]
                dve.wait_ge(n_sq, KT * i + k + 1)
                if k > 1:
                    dve.wait_ge(n_acc, (KT - 1) * i + k - 1)
                dve.tensor_tensor(acc[:, 0:n], acc[:, 0:n], sq[:, k % 2, 0:n], ALU.add).then_inc(n_acc, 1)

            def norm(i):
                src, gain, n, _, acc, scaled, hi, lo = norms[i]
                dve.wait_ge(n_rstd, 2 * i + 2)

                def scale(k):
                    if k >= 2:
                        dve.wait_ge(n_lo, KT * i + k - 1)
                    dve.scalar_tensor_tensor(out=scaled[:, k % 2, 0:n], in0=src[:, k, 0:n], scalar=col(gain + k), in1=acc[:, 0:n],
                                             op0=ALU.mult, op1=ALU.mult).then_inc(n_out, 1)

                scale(0)
                for k in range(KT):
                    if k < KT - 1:
                        scale(k + 1)
                    dve.wait_ge(n_hi, KT * i + k + 1)
                    dve.tensor_tensor(lo[:, k, 0:n], scaled[:, k % 2, 0:n], hi[:, k, 0:n].bitcast(F32), ALU.subtract).then_inc(n_lo, 1)

            def head_norms(name, i0, n, dst, gain, sq, rstd, done, each, root_of=rst):
                t0 = first[name]

                def at(u, j):
                    return dst[:, bass.ds(u + 2 * j, 1), :].rearrange("p a s -> p (a s)") if not isinstance(j, int) else dst[:, u, :]

                def gained(u, j):
                    dve.wait_ge(sq, i0 + u + 1 + 2 * j)
                    dve.tensor_scalar(at(u, j), psG[:, (t0 + u) % 2, 0:n], col(gain + u % each), None, ALU.mult)\
                        .then_inc(free[(t0 + u) % 2], 1)

                def divided(u, j):
                    if u % each != each - 1:
                        return
                    dve.wait_ge(rstd, (i0 + u) // each + 1 + j * (2 // each))
                    dve.wait_ge(free[(t0 + u) % 2], (t0 + u) // 2 + 1 + j)
                    for v in range(u - each + 1, u + 1):
                        dve.tensor_tensor(at(v, j), at(v, j), root_of[:, 0:n], ALU.mult).then_inc(done, 1)

                gained(0, 0)
                with dve.Fori(0, KT // 2 - 1) as j:
                    for u in (1, 2):
                        gained(u, j)
                        divided(u - 1, j)
                gained(KT - 1, 0)
                divided(KT - 2, 0)
                divided(KT - 1, 0)

            def key_norm(i, kr):
                dve.tensor_tensor(tmp[:, 0, 0:512].rearrange("p (t c) -> p t c", t=NT), kr, kr, ALU.mult).then_inc(kp_step, 1)
                dve.wait_ge(kp_step, 10 * i + 1)
                dve.tensor_reduce(small[:, 0:8], tmp[:, 0, 0:512].rearrange("p (t c) -> p t c", t=NT), AXX, ALU.add)\
                    .then_inc(kp_step, 1)
                dve.wait_ge(kp_step, 10 * i + 4)
                for half in range(2):
                    dve.tensor_tensor(heads3(rst[:, :])[:, :, half * HD:(half + 1) * HD], kr, wide(small[:, 8:16], [P, NT, HD]),
                                      ALU.mult).then_inc(kp_step, 1)

            def key_gain(i, gain):
                dve.wait_ge(kp_step, 10 * i + 7)
                dve.tensor_scalar(rst[:, :], psA[:, :], col(gain), None, ALU.mult).then_inc(kp_step, 1)
                dve.wait_ge(kp_step, 10 * i + 9)
                dve.tensor_tensor(kl[:, i, :], rst[:, :], kh[:, i, :].bitcast(F32), ALU.subtract).then_inc(kp_step, 1)

            dve.wait_ge(s_pcol, 1)
            dve.tensor_copy(pcol[:, :], psB[:, 0:P]).then_inc(s_pcol, 1)
            dve.tensor_scalar(nsink[:, :], nsink[:, :], -1.0, None, ALU.mult).then_inc(s_pcol, 1)
            dve.wait_ge(s_alog, 1)
            dve.tensor_scalar(alog[:, :], alog[:, :], -1.0, None, ALU.mult).then_inc(s_alog, 1)
            dve.memset(swm[:, :], NEG).then_inc(s_pcol, 1)
            dve.wait_ge(s_pcol, 4)
            dve.memset(swm[0:HD, HD:HD + P], 0.0).then_inc(s_pcol, 1)
            dve.memset(swm[HD:P, P:2 * P], 0.0).then_inc(s_pcol, 1)
            dve.wait_ge(s_pcol, 6)
            turn(0)
            for k in range(1, KT):
                add_squares(0, k)
            norm(0)
            turn(1)
            for k in range(1, KT):
                add_squares(1, k)
            head_norms("xk", 0, N_MEM, xk0, XKN, xk_sq, xk_rstd, xk_done, 2, mrst)
            norm(1)
            dve.wait_ge(m_st, 48)
            for k in range(2):
                i = first["ckv"] + k
                dve.wait_ge(kv_sq, k + 1)
                dve.tensor_scalar(ckvT[:, k, :], psG[:, i % 2, :], col(KVN + k), None, ALU.mult).then_inc(free[i % 2], 1)
            ikr, ikc = heads3(tmp[:, 0, :]), heads3(tmp[:, 1, :])[:, :, 0:HD]
            dve.wait_ge(t_out, 1)
            dve.tensor_reduce(small[:, 16:24], ikr[:, :, 0:HD], AXX, ALU.add).then_inc(ik_step, 1)
            dve.wait_ge(ik_step, 1)
            dve.tensor_scalar(small[:, 16:24], small[:, 16:24], 1.0 / HD, None, ALU.mult).then_inc(ik_step, 1)
            dve.wait_ge(ik_step, 2)
            dve.tensor_tensor(ikc, ikr[:, :, 0:HD], wide(small[:, 16:24], [P, NT, HD]), ALU.subtract).then_inc(ik_step, 1)
            dve.wait_ge(ik_step, 3)
            sq3 = rst[:, 0:512].rearrange("p (t c) -> p t c", t=NT)
            dve.tensor_tensor(sq3, ikc, ikc, ALU.mult).then_inc(ik_step, 1)
            dve.wait_ge(ik_step, 4)
            dve.tensor_reduce(small[:, 16:24], sq3, AXX, ALU.add).then_inc(ik_step, 1)
            dve.wait_ge(ik_step, 7)
            for half in range(2):
                dve.tensor_tensor(heads3(ikd)[:, :, half * HD:(half + 1) * HD], ikc, wide(small[:, 24:32], [P, NT, HD]),
                                  ALU.mult).then_inc(ik_step, 1)
            dve.tensor_scalar(ixw[:, :, :], ikr[:, :, HD:IKW], IDX_SCALE, None, ALU.mult).then_inc(ik_step, 1)
            dve.wait_ge(kv_ln, 2)
            dve.tensor_tensor(kvt[:, :, :], heads3(psA[:, :]), wide(small[:, 0:8], [P, NT, P]), ALU.mult).then_inc(kv_done, 1)
            dve.wait_ge(kv_done, 1)
            dve.wait_ge(ik_step, 11)
            dve.tensor_scalar(ikd, psA[:, :], col(IW), col(IB), ALU.mult, ALU.add).then_inc(ik_step, 1)
            dve.wait_ge(ik_step, 13)
            dve.tensor_tensor(ikl, ikd, ikh.bitcast(F32), ALU.subtract).then_inc(ik_step, 1)
            key_norm(0, kvt[:, :, 0:HD])
            key_gain(0, DK)
            for v, (t, h) in enumerate(ix_units):
                n = (t + 1) * P
                sc = scores[:, sc_off[t]:sc_off[t] + n]
                dve.wait_ge(ix_relu, v + 1)
                if h == 0:
                    dve.tensor_scalar(sc, tmp[:, v % 2, 0:n], ixw[:, t, h:h + 1], None, ALU.mult).then_inc(ix_acc, 1)
                else:
                    dve.wait_ge(ix_acc, v)
                    dve.scalar_tensor_tensor(out=sc, in0=tmp[:, v % 2, 0:n], scalar=ixw[:, t, h:h + 1], in1=sc,
                                             op0=ALU.mult, op1=ALU.add).then_inc(ix_acc, 1)
            def late(t):
                end = sc_off[t] + (t + 1) * P
                return scores[0:HD, end - HD:end]

            for t in range(TOPK // P):
                dve.memset(scores[:, sc_off[t]:sc_off[t] + (t + 1) * P], 0.0).then_inc(tk_max, 1)
                dve.wait_ge(tk_max, t + 1)
                dve.memset(late(t), NEG).then_inc(masked, 1)
            dve.wait_ge(ix_acc, len(ix_units))
            for i in range((NT - TOPK // P) // 2):
                two = (TOPK // P + i, NT - 1 - i)
                m0 = TOPK // P + 2 * (TOPK // 8) * i
                r0 = (2 + 2 * (TOPK // 8)) * i
                sc = [scores[:, sc_off[t]:sc_off[t] + (t + 1) * P] for t in two]
                for t in two:
                    dve.memset(late(t), BARRED).then_inc(tk_rep, 1)
                with dve.Fori(0, TOPK // 8) as j:
                    for v in range(2):
                        dve.wait_ge(tk_rep, r0 + v + 1 + 2 * j)
                        dve.sem_inc(dve_go, 1)
                        dve.max(m8[:, v, :], sc[v]).then_inc(tk_max, 1)
                    for v in range(2):
                        dve.wait_ge(tk_max, m0 + v + 1 + 2 * j)
                        dve.sem_inc(dve_go, 1)
                        dve.match_replace(out=sc[v], in_to_replace=m8[:, v, :], in_values=sc[v], imm_value=TAKEN)\
                            .then_inc(tk_rep, 1)
                for v in range(2):
                    dve.wait_ge(tk_rep, r0 + v + 1 + 2 * (TOPK // 8))
                    dve.tensor_scalar(sc[v], sc[v], 0.5 * (TAKEN + BARRED), NEG, ALU.is_gt, ALU.mult).then_inc(masked, 1)
            head_norms("q", 0, S, qT, DQ, q_sq, q_rstd, q_done, 1)
            for i in (1, 2):
                dve.wait_ge(t_out, 3)
                key_norm(i, heads3(tmp[:, 1, :])[:, :, (i - 1) * HD:i * HD])
                key_gain(i, SK)

            def att_max(q, h, pp, kind, t, p):
                u = 2 * q + h
                n = nk(kind, t)
                mask = scores[:, sc_off[t]:sc_off[t] + n] if kind == "dsa" else swm[:, 2 * P - n:2 * P]
                swa = 2 * p if kind == "swa" else None
                dve.wait_ge(a_s, u + 1 + 2 * pp)
                if q % (NT * PAIRS):
                    before = t if p else t - 1
                    bank, _, _, m = turns_of(kind, q - 1, h, before, nk(kind, before) // P)[-1]
                    dve.wait_ge(a_t[bank], m + 1 + (2 if long(kind, before) else 1) * pp)
                if swa is not None and u >= 130:
                    dve.wait_ge(a_snk, u - 129)
                dve.sem_inc(dve_go, 1)
                dve.tensor_tensor_reduce(out=tmp[:, h, 0:n], in0=psG[:, h, 0:n], in1=mask, scale=1.0, scalar=TAKEN,
                                         op0=ALU.add, op1=ALU.max, accum_out=stat[:, h, 1:2]).then_inc(a_mx0, 1)
                dve.wait_ge(a_mx0, u + 1 + 2 * pp)
                if swa is None:
                    dve.tensor_scalar(stat[:, h, 0:1], stat[:, h, 1:2], -AT_SCALE, None, ALU.mult).then_inc(a_mx, 1)
                else:
                    dve.tensor_scalar(stat[:, h, 0:1], stat[:, h, 1:2], -AT_SCALE, nsink[:, swa + h:swa + h + 1],
                                      ALU.mult, ALU.min).then_inc(a_mx, 1)

            def att_copy(q, h, pp, kind, t):
                for bank, b0, b1, n in turns_of(kind, q, h, t, nk(kind, t) // P):
                    if bank == 1:
                        dve.wait_ge(a_t[1], n + 1 + (2 if long(kind, t) else 1) * pp)
                        if q > 0:
                            dve.wait_ge(a_pv, 2 * q + h - 1 + 2 * pp)
                        dve.tensor_copy(sqb[:, h, b0 * P:b1 * P], psA[:, 512:512 + (b1 - b0) * P]).then_inc(a_cp[1], 1)

            def att_div(q, pp, swa):
                z = q % 2
                dve.wait_ge(a_pv, 2 * q + 2 + 2 * pp)
                if q >= 2:
                    dve.wait_ge(a_ot, q - 1 + pp)
                if swa:
                    dve.wait_ge(a_snk, 2 * (q - 64) + 2)
                    dve.tensor_tensor(stat[:, z, 4:6], stat[:, z, 4:6], stat[:, z, 6:8], ALU.add).then_inc(a_den, 1)
                    dve.wait_ge(a_den, q - 64 + 1)
                dve.reciprocal(stat[:, z, 2:4], stat[:, z, 4:6]).then_inc(a_ri, 1)
                dve.wait_ge(a_ri, q + 1 + pp)
                dve.tensor_tensor(otok[:, z, :].rearrange("p (h c) -> p h c", h=2),
                                  (psB, psC)[z][:, 0:P].rearrange("p (h c) -> p h c", h=2),
                                  wide(stat[:, z, 2:4], [P, 2, HD]), ALU.mult).then_inc(a_o, 1)

            def attention(kind, q0):
                def pair(q, pp, t, p, before, after):
                    att_max(q, 1, pp, kind, t, p)
                    att_copy(q, 0, pp, kind, t)
                    if before is not None:
                        att_div(q - 1, pp, kind == "swa")
                    if after is not None:
                        att_max(q + 1, 0, pp, kind, *after)
                    att_copy(q, 1, pp, kind, t)

                att_max(q0, 0, 0, kind, 0, 0)
                for t in range(NT):
                    q = q0 + PAIRS * t
                    pair(q, 0, t, 0, (t - 1, PAIRS - 1) if t else None, (t, 1))
                    if kind == "dsa" and t:
                        with dve.Fori(0, PAIRS // 2 - 1) as j:
                            for u in (1, 2):
                                pair(q + u, 2 * j, t, u, (t, u - 1), (t, u + 1))
                    else:
                        for p in range(1, PAIRS - 1):
                            pair(q + p, 0, t, p, (t, p - 1), (t, p + 1))
                    pair(q + PAIRS - 1, 0, t, PAIRS - 1, (t, PAIRS - 2), (t + 1, 0) if t < NT - 1 else None)
                att_div(q0 + NT * PAIRS - 1, 0, kind == "swa")

            attention("dsa", 0)
            head_norms("sq", KT, S, qT, SQ, q_sq, q_rstd, q_done, 1)
            attention("swa", 64)
            dve.wait_ge(t_out, 4)
            dve.tensor_tensor(dts[:, 4, :, :], dts[:, 0, :, :], dtb[:, :].unsqueeze(1).to_broadcast([P, NT, HEADS]), ALU.add)\
                .then_inc(dt_step, 1)
            dve.wait_ge(dt_step, 1)
            dve.scalar_tensor_tensor(out=dts[:, 5, :, :], in0=dts[:, 4, :, :], scalar=-1.0, in1=dts[:, 4, :, :],
                                     op0=ALU.mult, op1=ALU.max).then_inc(dt_step, 1)
            dve.wait_ge(dt_step, 4)
            dve.scalar_tensor_tensor(out=dts[:, 0, :, :], in0=dts[:, 4, :, :], scalar=0.0, in1=dts[:, 5, :, :],
                                     op0=ALU.max, op1=ALU.add).then_inc(dt_step, 1)
            dve.wait_ge(dt_step, 5)
            dve.wait_ge(s_alog, 2)
            dve.tensor_tensor(dts[:, 1, :, :], dts[:, 0, :, :], alog[:, :].unsqueeze(1).to_broadcast([P, NT, HEADS]), ALU.mult)\
                .then_inc(dt_step, 1)
            def convolve(j):
                for u in range(2):
                    i = first["xbc"] + u
                    k = u + 2 * j
                    ps, acc = psG[:, i % 2, :], tmp[:, u, :]
                    dve.wait_ge(mm, i + 1 + 2 * j)
                    if not isinstance(j, int):
                        dve.wait_ge(cv_out, u - 1 + 2 * j)
                    dve.tensor_scalar(acc, ps, pcol[:, bass.ds(CW + (CONV - 1) * XC + k, 1)], pcol[:, bass.ds(CB + k, 1)],
                                      ALU.mult, ALU.add).then_inc(cv_acc, 1)
                    for tap in range(CONV - 2, -1, -1):
                        back = CONV - 1 - tap
                        dve.wait_ge(cv_acc, 3 * u + back + 6 * j)
                        ins = dve.scalar_tensor_tensor(out=acc[:, back:], in0=ps[:, 0:S - back],
                                                       scalar=pcol[:, bass.ds(CW + tap * XC + k, 1)], in1=acc[:, back:],
                                                       op0=ALU.mult, op1=ALU.add)
                        ins.then_inc(cv_acc if tap else free[i % 2], 1)

            convolve(0)
            with dve.Fori(1, XC // 2) as j:
                convolve(j)
            dve.wait_ge(dt_step, 7)
            dve.tensor_copy(dts[:, 2, :, :], psB[:, 0:P].rearrange("p (t h) -> p t h", t=NT)).then_inc(dt_step, 1)
            dve.wait_ge(dt_step, 8)
            dve.tensor_tensor(dts[:, 5, :, :], psB[:, P:2 * P].rearrange("p (t h) -> p t h", t=NT), dts[:, 2, :, :], ALU.subtract)\
                .then_inc(dt_step, 1)
            dve.wait_ge(dt_step, 12)
            dve.tensor_tensor(dts[:, 5, :, :], dts[:, 5, :, :], dts[:, 0, :, :], ALU.mult).then_inc(dt_step, 1)
            dve.wait_ge(cv_out, XC)
            dve.wait_ge(dt_step, 13)
            def differences(n):
                dve.wait_ge(s_bc, n + 1)
                if n >= 2:
                    dve.wait_ge(s_e, n - 1)
                c, q = n // 4, n % 4
                dve.tensor_tensor(tmp[:, n % 2, 0:512].rearrange("p (h l) -> p h l", h=4),
                                  (psB, psC)[n % 2][:, :].rearrange("p (h l) -> p h l", h=4),
                                  wide(dts[:, 2, c, 4 * q:4 * q + 4], [P, 4, P]), ALU.subtract).then_inc(s_df, 1)

            def weigh(n):
                dve.wait_ge(s_e, n + 1)
                if n >= 2:
                    dve.wait_ge(s_yd, n - 1)
                if n % 4 == 0:
                    dve.wait_ge(s_g, n // 4 + 1)
                g = 512 + (n % 4 // 2) * P
                dve.tensor_tensor(sqb[:, n % 2, 512:1024].rearrange("p (h l) -> p h l", h=4),
                                  sqb[:, n % 2, 0:512].rearrange("p (h l) -> p h l", h=4),
                                  psA[:, g:g + P].unsqueeze(1).to_broadcast([P, 4, P]), ALU.mult).then_inc(s_m, 1)

            def y_gain(c):
                dve.wait_ge(s_ytr, c + 1)
                if c:
                    dve.wait_ge(s_yst, 16 * c)
                dve.tensor_tensor(heads3(rst[:, :]), heads3(psG[:, 1, :]), wide(pcol[:, SSN:SSN + KT], [P, KT, P]), ALU.mult)\
                    .then_inc(s_ycp, 1)

            for c in range(NT):
                def by_head(i, h0=0, h1=HEADS):
                    return wide(dts[:, i, c, h0:h1], [P, h1 - h0, HD])

                differences(4 * c)
                differences(4 * c + 1)
                dve.wait_ge(s_xtok, c + 1)
                dve.tensor_tensor(heads3(xdt[:, :], HEADS), heads3(xtok[:, c % 2, :], HEADS), by_head(0), ALU.mult).then_inc(s_xdt, 1)
                weigh(4 * c)
                if c:
                    dve.wait_ge(s_upd, 2 * c)
                dve.tensor_tensor(heads3(xw[:, :], HEADS), heads3(xtok[:, c % 2, :], HEADS), by_head(5), ALU.mult).then_inc(s_xw, 1)
                differences(4 * c + 2)
                weigh(4 * c + 1)
                differences(4 * c + 3)
                if c:
                    y_gain(c - 1)
                weigh(4 * c + 2)
                weigh(4 * c + 3)
                if c:
                    dve.wait_ge(s_yo, c)
                    dve.wait_ge(s_rs, 2 * c)
                    dve.tensor_tensor(heads3(yoff[:, :], HEADS), heads3(psG[:, 1, :], HEADS), by_head(4), ALU.mult).then_inc(s_off, 1)
                dve.wait_ge(s_yd, 4 * c + 4)
                dve.wait_ge(s_skip, c + 1)
                dve.tensor_tensor(yt[:, :], xtok[:, c % 2, :], psG[:, 0, :], ALU.add).then_inc(s_y, 1)
                if c:
                    dve.wait_ge(s_off, c)
                    dve.wait_ge(s_y, c + 1)
                    dve.tensor_tensor(yt[:, :], yt[:, :], yoff[:, :], ALU.add).then_inc(s_ysum, 1)
                else:
                    dve.wait_ge(s_y, 1)
                    dve.sem_inc(s_ysum, 1)
                if c < NT - 1:
                    for g in range(GROUPS):
                        sg = st[:, g * 512:(g + 1) * 512]
                        if c:
                            dve.tensor_tensor(heads3(sg, 8), heads3(sg, 8), by_head(3, 8 * g, 8 * g + 8), ALU.mult).then_inc(s_dec, 1)
                            dve.wait_ge(s_dec, 2 * c - 1 + g)
                        dve.wait_ge(s_upd, 2 * c + g + 1)
                        if c:
                            dve.tensor_tensor(sg, sg, psA[:, g * 512:(g + 1) * 512], ALU.add).then_inc(s_stt, 1)
                        else:
                            dve.tensor_copy(sg, psA[:, g * 512:(g + 1) * 512]).then_inc(s_stt, 1)
            y_gain(NT - 1)

            def split_mixer(b):
                for k in range(KT):
                    n = KT * b + k
                    dve.wait_ge(b_hi, n + 1)
                    src = mixed(k) if b < 3 else merged[:, k, :]
                    dve.tensor_tensor(AL[:, k, :], src, AH[:, k, :].bitcast(F32), ALU.subtract).then_inc(b_lo, 1)

            for b in range(3):
                split_mixer(b)
                for k in range(KT):
                    n = KT * b + k
                    i = first[f"br{b}"] + k
                    dve.wait_ge(g_in[n % 2], 16 * (n // 2 + 1))
                    dve.wait_ge(mm, i + 1)
                    if b == 0:
                        dve.tensor_tensor(merged[:, k, :], psG[:, i % 2, :], sqb[:, n % 2, :], ALU.mult).then_inc(free[i % 2], 1)
                    else:
                        if n > KT:
                            dve.wait_ge(m_add, n - KT)
                        dve.tensor_tensor(rst[:, :], psG[:, i % 2, :], sqb[:, n % 2, :], ALU.mult).then_inc(free[i % 2], 1)
                        dve.wait_ge(free[i % 2], i // 2 + 1)
                        dve.tensor_tensor(merged[:, k, :], merged[:, k, :], rst[:, :], ALU.add).then_inc(m_add, 1)
            dve.wait_ge(m_add, 2 * KT)
            split_mixer(3)

            def residual(name):
                norm_after = {"out": 2, "xo": 3}.get(name)
                for k in range(KT):
                    i = first[name] + k
                    dve.wait_ge(mm, i + 1)
                    dve.tensor_tensor(xT[:, k, :], psG[:, i % 2, :], xT[:, k, :], ALU.add).then_inc(free[i % 2], 1)
                    if norm_after and k >= 2:
                        add_squares(norm_after, k - 1)
                if norm_after:
                    add_squares(norm_after, KT - 1)

            dve.wait_ge(x_back, 16)
            residual("out")
            norm(2)
            head_norms("xq", KT, S, xqT, XQN, xk_sq, xk_rstd, xk_done, 2)
            units = NT * XH
            for w in range(units + 3):
                if 2 <= w <= units + 1:
                    z = w % 2
                    dve.wait_ge(c_exp, w - 1)
                    dve.reciprocal(small[:, 46 + z:47 + z], small[:, 42 + z:43 + z]).then_inc(c_ri, 1)
                if w < units:
                    z = w % 2
                    dve.wait_ge(c_s, w + 1)
                    if w >= 2:
                        dve.wait_ge(c_exp, w - 1)
                    dve.tensor_reduce(small[:, 44 + z:45 + z], psG[:, z, 0:N_MEM], AXX, ALU.max).then_inc(c_mx0, 1)
                    dve.wait_ge(c_mx0, w + 1)
                    dve.tensor_scalar(small[:, 40 + z:41 + z], small[:, 44 + z:45 + z], -XA_SCALE, None, ALU.mult).then_inc(c_mx, 1)
                if 2 <= w <= units + 1:
                    z = w % 2
                    dve.wait_ge(c_ri, w - 1)
                    dve.wait_ge(c_pv, w - 1)
                    if w >= 4:
                        dve.wait_ge(c_ot, w - 3)
                    dve.tensor_scalar(tmp[:, z, 512:768], (psB, psC)[z][:, 0:XD], small[:, 46 + z:47 + z], None, ALU.mult)\
                        .then_inc(c_o, 1)
                if w >= 3:
                    t, h, z = (w - 3) // XH, (w - 3) % XH, (w - 3) % 2
                    a = (slice(None), slice(2 * h, 2 * h + 2), slice(t * P, (t + 1) * P))
                    dve.wait_ge(c_hi, w - 2)
                    dve.tensor_tensor(AL[a], heads3(psG[:, z, 512:768], 2), AH[a].bitcast(F32), ALU.subtract).then_inc(c_lo, 1)
            residual("xo")
            norm(3)
            for c in range(0, FT, FC):
                for k in range(min(FC, FT - c)):
                    n = c + k
                    i = up_tile(n)
                    dve.wait_ge(mm, i + 1)
                    read_out(dve, i - 1)
                    if n >= 2:
                        dve.wait_ge(f_lo, n - 1)
                    dve.tensor_tensor(tmp[:, n % 2, :], psG[:, i % 2, :], sqb[:, n % 2, :], ALU.mult).then_inc(free[i % 2], 1)
                    dve.wait_ge(f_hi, n + 1)
                    dve.tensor_tensor(HL[:, k, :], tmp[:, n % 2, :], HH[:, k, :].bitcast(F32), ALU.subtract).then_inc(f_lo, 1)
                residual(f"dn{c}")
            for t in range(1, NT, 2):
                dve.wait_ge(o_tr, t + 1)
                if t > 1:
                    dve.wait_ge(o_st[1], 16 * (t // 2))
                dve.tensor_copy(sqb[:, 1, :], psG[:, 1, :]).then_inc(o_cp[1], 1)


NAMES = ["x", "mem", "norm_mix", "w_in", "dsa_kv_norm", "dsa_w_ukv", "dsa_q_norm", "dsa_k_norm", "idx_k_ln_w", "idx_k_ln_b",
         "swa_q_norm", "swa_k_norm", "swa_sinks", "ssm_conv_w", "ssm_conv_b", "ssm_dt_bias", "ssm_a_log", "ssm_d",
         "ssm_norm", "w_br_dsa", "w_br_swa", "w_br_ssm", "w_out", "norm_xa", "norm_mem", "xa_wq", "xa_wkv", "xa_q_norm",
         "xa_k_norm", "xa_wo", "norm_ffn", "ffn_w_gate_up", "ffn_w_down"]


def kernel(**inputs):
    import numpy as np
    import concourse.bacc as bacc
    from concourse.bass_utils import run_bass_kernel_spmd

    nc = bacc.Bacc("TRN2", target_bir_lowering=False, num_devices=1)
    arrays, ap = {}, {}
    for name in NAMES:
        a = np.ascontiguousarray(inputs[name])
        arrays[f"in_{name}"] = a
        ap[name] = nc.dram_tensor(f"in_{name}", a.shape, mybir.dt.from_np(a.dtype), kind="ExternalInput").ap()
    out = nc.dram_tensor("out_x", (1, S, D), F32, kind="ExternalOutput").ap()
    build(nc, ap, out)
    r = run_bass_kernel_spmd(nc, [arrays], core_ids=[0])
    return r.results[0]["out_x"]
```
